# Optimizing a Trainium2 kernel written in Bass

```python
import math
import jax, jax.numpy as jnp
from jax import lax
import numpy as np

D_MODEL = 1024
BATCH = 1
SEQ = 1024
DEPTH = 1
DEC_BATCH = 8
DEC_SEQ = 8
PAST_LEN = 4096
PAGE_SIZE = 128

FOX_HEADS = 8
FOX_HEAD_DIM = 64
FOX_WIDTH = FOX_HEADS * FOX_HEAD_DIM
FOX_SCALE = FOX_HEAD_DIM ** -0.5
Q_BLOCK = 128
GLA_HEADS = 4
GLA_DK = D_MODEL // 2 // GLA_HEADS
GLA_DV = D_MODEL // GLA_HEADS
GLA_KW = GLA_HEADS * GLA_DK
GLA_VW = GLA_HEADS * GLA_DV
GLA_RANK = 16
GLA_TAU = 16.0
GLA_CHUNK = 64
EPS = 1e-6

SPLIT_SIZES = (FOX_WIDTH, FOX_WIDTH, FOX_WIDTH, FOX_HEADS, FOX_WIDTH,
               GLA_KW, GLA_KW, GLA_VW, GLA_RANK, GLA_VW,
               D_MODEL, D_MODEL)
SPLIT_POINTS = tuple(int(v) for v in np.cumsum(SPLIT_SIZES)[:-1])
D_IN = int(sum(SPLIT_SIZES))

kernel_name = "fox_gla_parallel_gated_decoder_step"

def _rmsnorm(x, g):
    xf = x.astype(jnp.float32)
    y = xf * lax.rsqrt(jnp.mean(xf * xf, axis=-1, keepdims=True) + EPS)
    return (y * g.astype(jnp.float32)).astype(x.dtype)

def _project(x, ln_g, w_in, fox_b_f, q_norm_g, k_norm_g, gla_w_a2, gla_b_a):
    B, L, _ = x.shape
    h = _rmsnorm(x, ln_g)
    z = h @ w_in
    fq, fk, fv, ff, fg, gq, gk, gv, glr, gg, ma, mb = jnp.split(z, SPLIT_POINTS, axis=-1)
    fq = _rmsnorm(fq.reshape(B, L, FOX_HEADS, FOX_HEAD_DIM), q_norm_g)
    fk = _rmsnorm(fk.reshape(B, L, FOX_HEADS, FOX_HEAD_DIM), k_norm_g)
    fv = fv.reshape(B, L, FOX_HEADS, FOX_HEAD_DIM)
    logf = jax.nn.log_sigmoid((ff + fox_b_f).astype(jnp.float32))
    gq = gq.reshape(B, L, GLA_HEADS, GLA_DK) * (GLA_DK ** -0.5)
    gk = gk.reshape(B, L, GLA_HEADS, GLA_DK)
    gv = gv.reshape(B, L, GLA_HEADS, GLA_DV)
    log_a = jax.nn.log_sigmoid((glr @ gla_w_a2 + gla_b_a).astype(jnp.float32)) / GLA_TAU
    log_a = log_a.reshape(B, L, GLA_HEADS, GLA_DK)
    return fq, fk, fv, logf, fg, gq, gk, gv, log_a, gg, ma, mb

def _fox_prompt(q, k, v, logf):
    B, L, H, hd = q.shape
    nb = L // Q_BLOCK
    c = jnp.cumsum(logf, axis=1).transpose(0, 2, 1)
    q_blocks = q.reshape(B, nb, Q_BLOCK, H, hd).transpose(1, 0, 2, 3, 4)
    key_pos = jnp.arange(L)

    def block(args):
        i, q_i = args
        q_pos = i * Q_BLOCK + jnp.arange(Q_BLOCK)
        c_q = lax.dynamic_slice_in_dim(c, i * Q_BLOCK, Q_BLOCK, axis=2)
        s = jnp.einsum('bqhd,bkhd->bhqk', q_i, k).astype(jnp.float32) * FOX_SCALE
        s = s + c_q[..., None] - c[:, :, None, :]
        s = jnp.where(key_pos[None, :] <= q_pos[:, None], s, -jnp.inf)
        p = jax.nn.softmax(s, axis=-1)
        return jnp.einsum('bhqk,bkhd->bqhd', p.astype(v.dtype), v)

    o = lax.map(block, (jnp.arange(nb), q_blocks))
    return o.transpose(1, 0, 2, 3, 4).reshape(B, L, H, hd)

def _fox_sample(q, k_new, v_new, logf_new, cache_k, cache_v, cache_logf, page_table):
    Bd, T, H, hd = q.shape
    n_pages = page_table.shape[1]
    P = n_pages * PAGE_SIZE
    k_past = cache_k[page_table].reshape(Bd, P, H, hd)
    v_past = cache_v[page_table].reshape(Bd, P, H, hd)
    lf_past = cache_logf[page_table].reshape(Bd, P, H).astype(jnp.float32)
    c_past = jnp.cumsum(lf_past, axis=1)
    c_new = c_past[:, -1:, :] + jnp.cumsum(logf_new.astype(jnp.float32), axis=1)
    c_q = c_new.transpose(0, 2, 1)[..., None]
    s_past = jnp.einsum('bqhd,bkhd->bhqk', q, k_past).astype(jnp.float32) * FOX_SCALE
    s_past = s_past + c_q - c_past.transpose(0, 2, 1)[:, :, None, :]
    s_new = jnp.einsum('bqhd,bkhd->bhqk', q, k_new).astype(jnp.float32) * FOX_SCALE
    s_new = s_new + c_q - c_new.transpose(0, 2, 1)[:, :, None, :]
    s_new = jnp.where(jnp.tril(jnp.ones((T, T), dtype=bool)), s_new, -jnp.inf)
    p = jax.nn.softmax(jnp.concatenate([s_past, s_new], axis=-1), axis=-1)
    o = (jnp.einsum('bhqk,bkhd->bqhd', p[..., :P].astype(v_past.dtype), v_past)
         + jnp.einsum('bhqk,bkhd->bqhd', p[..., P:].astype(v_new.dtype), v_new))
    return o

def _gla(q, k, v, log_a, s0):
    B, L, Hh, dk = q.shape
    dv = v.shape[-1]
    C = math.gcd(L, GLA_CHUNK)
    n = L // C

    def chunks(t):
        return t.astype(jnp.float32).reshape(B, n, C, Hh, t.shape[-1]).transpose(1, 0, 3, 2, 4)

    causal = jnp.tril(jnp.ones((C, C), dtype=bool))

    def step(S, inp):
        qc, kc, vc, gc = inp
        b = jnp.cumsum(gc, axis=2)
        b_last = b[:, :, -1:, :]
        q_in = qc * jnp.exp(b)
        k_in = kc * jnp.exp(-b)
        att = jnp.where(causal, jnp.einsum('bhtd,bhsd->bhts', q_in, k_in), 0.0)
        o = jnp.einsum('bhts,bhsv->bhtv', att, vc) + jnp.einsum('bhtd,bhdv->bhtv', q_in, S)
        S = (jnp.exp(b_last[:, :, 0, :])[..., None] * S
             + jnp.einsum('bhsd,bhsv->bhdv', kc * jnp.exp(b_last - b), vc))
        return S, o

    S, o = lax.scan(step, s0.astype(jnp.float32), (chunks(q), chunks(k), chunks(v), chunks(log_a)))
    o = o.transpose(1, 0, 3, 2, 4).reshape(B, L, Hh, dv)
    return o.astype(v.dtype), S

def _merge(x, o_fox, fg, o_gla, gg, ma, mb, gla_norm_g, w_up_a, w_up_b, w_out):
    B, L, _ = x.shape
    a = (o_fox.reshape(B, L, FOX_WIDTH) * jax.nn.silu(fg)) @ w_up_a
    o_gla = _rmsnorm(o_gla, gla_norm_g).reshape(B, L, GLA_VW)
    b = (o_gla * jax.nn.silu(gg)) @ w_up_b
    m = jax.nn.sigmoid(ma) * a + jax.nn.sigmoid(mb) * b
    return x + m @ w_out

def setup_inputs(seed: int = 0) -> dict:
    key = jax.random.key(seed)
    ks = jax.random.split(key, 20)
    n_pages = PAST_LEN // PAGE_SIZE
    n_used = DEC_BATCH * n_pages
    n_phys = n_used + n_used // 4
    f32 = jnp.float32
    nrm = jax.random.normal
    x_prompt = nrm(ks[0], (BATCH, SEQ, D_MODEL), f32)
    x_sample = nrm(ks[1], (DEC_BATCH, DEC_SEQ, D_MODEL), f32)
    cache_k = nrm(ks[2], (DEPTH, n_phys, PAGE_SIZE, FOX_HEADS, FOX_HEAD_DIM), f32)
    cache_v = nrm(ks[3], (DEPTH, n_phys, PAGE_SIZE, FOX_HEADS, FOX_HEAD_DIM), f32)
    cache_logf = jax.nn.log_sigmoid(5.0 + 1.5 * nrm(ks[4], (DEPTH, n_phys, PAGE_SIZE, FOX_HEADS), f32))
    state_gla = 0.5 * nrm(ks[5], (DEPTH, DEC_BATCH, GLA_HEADS, GLA_DK, GLA_DV), f32)
    page_table = jax.random.permutation(ks[6], n_phys)[:n_used].reshape(DEC_BATCH, n_pages).astype(jnp.int32)
    ln_g = 1.0 + 0.05 * nrm(ks[7], (DEPTH, D_MODEL), f32)
    w_in = nrm(ks[8], (DEPTH, D_MODEL, D_IN), f32) * D_MODEL ** -0.5
    fox_b_f = 3.0 + 3.0 * jax.random.uniform(ks[9], (DEPTH, FOX_HEADS), f32)
    q_norm_g = 1.0 + 0.05 * nrm(ks[10], (DEPTH, FOX_HEAD_DIM), f32)
    k_norm_g = 1.0 + 0.05 * nrm(ks[11], (DEPTH, FOX_HEAD_DIM), f32)
    gla_w_a2 = nrm(ks[12], (DEPTH, GLA_RANK, GLA_KW), f32) * GLA_RANK ** -0.5
    gla_b_a = 0.1 * nrm(ks[13], (DEPTH, GLA_KW), f32)
    gla_norm_g = 1.0 + 0.05 * nrm(ks[14], (DEPTH, GLA_DV), f32)
    w_up_a = nrm(ks[15], (DEPTH, FOX_WIDTH, D_MODEL), f32) * FOX_WIDTH ** -0.5
    w_up_b = nrm(ks[16], (DEPTH, GLA_VW, D_MODEL), f32) * GLA_VW ** -0.5
    w_out = nrm(ks[17], (DEPTH, D_MODEL, D_MODEL), f32) * D_MODEL ** -0.5
    return {"x_prompt": x_prompt, "x_sample": x_sample, "cache_k": cache_k, "cache_v": cache_v,
            "cache_logf": cache_logf, "state_gla": state_gla, "page_table": page_table,
            "ln_g": ln_g, "w_in": w_in, "fox_b_f": fox_b_f, "q_norm_g": q_norm_g, "k_norm_g": k_norm_g,
            "gla_w_a2": gla_w_a2, "gla_b_a": gla_b_a, "gla_norm_g": gla_norm_g,
            "w_up_a": w_up_a, "w_up_b": w_up_b, "w_out": w_out}

def reference(x_prompt, x_sample, cache_k, cache_v, cache_logf, state_gla, page_table,
              ln_g, w_in, fox_b_f, q_norm_g, k_norm_g, gla_w_a2, gla_b_a, gla_norm_g,
              w_up_a, w_up_b, w_out):
    yp, ys = x_prompt, x_sample
    kp, vp, lfp, sp = [], [], [], []
    kq, vq, lfq, sq = [], [], [], []
    for l in range(DEPTH):
        proj = (ln_g[l], w_in[l], fox_b_f[l], q_norm_g[l], k_norm_g[l], gla_w_a2[l], gla_b_a[l])
        outp = (gla_norm_g[l], w_up_a[l], w_up_b[l], w_out[l])
        fq, fk, fv, logf, fg, gq, gk, gv, la, gg, ma, mb = _project(yp, *proj)
        o_f = _fox_prompt(fq, fk, fv, logf)
        s0 = jnp.zeros((yp.shape[0], GLA_HEADS, GLA_DK, GLA_DV), jnp.float32)
        o_g, s_end = _gla(gq, gk, gv, la, s0)
        kp.append(fk); vp.append(fv); lfp.append(logf); sp.append(s_end)
        yp = _merge(yp, o_f, fg, o_g, gg, ma, mb, *outp)
        fq, fk, fv, logf, fg, gq, gk, gv, la, gg, ma, mb = _project(ys, *proj)
        o_f = _fox_sample(fq, fk, fv, logf, cache_k[l], cache_v[l], cache_logf[l], page_table)
        o_g, s_end = _gla(gq, gk, gv, la, state_gla[l])
        kq.append(fk); vq.append(fv); lfq.append(logf); sq.append(s_end)
        ys = _merge(ys, o_f, fg, o_g, gg, ma, mb, *outp)
    k_prompt = jnp.stack(kp)
    v_prompt = jnp.stack(vp)
    logf_prompt = jnp.stack(lfp)
    gla_prompt = jnp.stack(sp)
    k_sample = jnp.stack(kq)
    v_sample = jnp.stack(vq)
    logf_sample = jnp.stack(lfq)
    gla_sample = jnp.stack(sq)
    return (yp, ys, k_prompt, v_prompt, logf_prompt, gla_prompt, k_sample, v_sample, logf_sample, gla_sample)


_drawn_inputs = setup_inputs


def setup_inputs(seed=0):
    import zlib

    import numpy as np

    out = dict(_drawn_inputs(seed))
    spreads = {}
    factors = {'cache_logf': 6.767, 'q_norm_g': 8.0, 'gla_norm_g': 3.796}
    for name, (base, spread) in spreads.items():
        noise = np.random.default_rng([zlib.crc32(name.encode()), seed]).standard_normal(out[name].shape)
        drawn = base * np.exp(spread * noise) if base else spread * noise
        out[name] = __import__('jax').numpy.asarray(drawn.astype(out[name].dtype))
    for name, factor in factors.items():
        out[name] = (out[name] * factor).astype(out[name].dtype)
    return out
```

```python
from contextlib import ExitStack

import numpy as np

import concourse.bass as bass
from concourse import mybir

F32 = mybir.dt.float32
F32R = mybir.dt.float32r
I32 = mybir.dt.int32
ALU = mybir.AluOpType
ACT = mybir.ActivationFunctionType
AX_X = mybir.AxisListType.X
ds = bass.ds

P = 128
D = 1024
SEQ = 1024
NB, TS = 8, 8
NSAMP = NB * TS
NT = SEQ + NSAMP
KT_ = D // P
H, HD = 8, 64
FW = H * HD
NHP = H // 2
GH, DK, DV = 4, 128, 256
CH = 64
RANK = 16
PAGE = 128
NPG = 32
PAST = NPG * PAGE
HALF = PAST // 2
NPHYS = NB * NPG + NB * NPG // 4
EPS = 1e-6
TAU = 16.0
BIG = 3.0e38
CHUNKS = [(0, 512), (512, 512), (SEQ, NSAMP)]
TT = SEQ // P

CONST_W = {}
_w = 0
for _n, _c in [("ident", 128), ("causal", 128), ("glamax", 128), ("glamin", 128), ("smpmax", 64),
               ("smpmin", 64), ("scan", 512), ("scan_s", 64), ("bdones", 128), ("rowmask", 8), ("newmask", 8)]:
    CONST_W[_n] = (_w, _c)
    _w += _c
NCONST = _w
VEC_W = {}
_w = 0
for _n, _c in [("ln_g", KT_), ("gq", 1), ("gk", 1), ("gla_g", 2), ("b_f", 1), ("b_a", GH)]:
    VEC_W[_n] = (_w, _c)
    _w += _c
NVEC = _w


def constants():
    c = np.zeros((P, NCONST), np.float32)

    def put(name, a):
        o, w = CONST_W[name]
        c[:a.shape[0], o:o + w] = a
    r = np.arange(P)
    put("ident", np.eye(P))
    put("causal", np.where(r[None, :] <= r[:, None], 0, -BIG))
    ok = (r[:, None] <= r[None, :]) & (r[:, None] // CH == r[None, :] // CH)
    put("glamax", np.where(ok, BIG, 0))
    put("glamin", np.where(ok, -BIG, 0))
    s = np.arange(NSAMP)
    ok = (s[:, None] <= s[None, :]) & (s[:, None] // TS == s[None, :] // TS)
    put("smpmax", np.where(ok, BIG, 0))
    put("smpmin", np.where(ok, -BIG, 0))
    put("scan", np.tile((np.arange(512) % CH != 0).astype(np.float32), (P, 1)))
    put("scan_s", np.tile((s % TS != 0).astype(np.float32), (P, 1)))
    put("bdones", (r[:, None] // HD == r[None, :] // HD).astype(np.float32))
    put("rowmask", (s[:, None] // TS == np.arange(NB)[None, :]).astype(np.float32))
    put("newmask", np.where(np.arange(TS)[None, :] <= (s % TS)[:, None], 0, -BIG))
    return c


def upto(i, per, k, base=0):
    return i * per + (base + max(k, 0) + 1)


def opened(eng, *sems):
    for s in sems:
        eng.sem_inc(s, 1)


def fox_gla_step(nc, ins, outs, scratch):
    top = ExitStack()
    with top:
        def sem(name):
            return nc.alloc_semaphore(name=name)

        def sb(ctx, name, shape, dt=F32):
            return ctx.enter_context(nc.sbuf_tensor(name, shape, dt))

        psum = top.enter_context(nc.psum_tensor("psum", [P, 8 * 512], F32))
        bank = [psum[:, n * 512:(n + 1) * 512] for n in range(8)]

        con = sb(top, "con", [P, NCONST])
        vec = sb(top, "vec", [P, NVEC])

        def cc(name, rows=P):
            o, w = CONST_W[name]
            return con[0:rows, o:o + w]

        def vv(name, rows=P, col=0, n=1):
            o, _ = VEC_W[name]
            return vec[0:rows, o + col:o + col + n]

        epsb = sb(top, "epsb", [P, 1])
        gq8 = sb(top, "gq8", [P, 1])
        h_hi = sb(top, "h_hi", [P, KT_, NT], F32R)
        h_lo = sb(top, "h_lo", [P, KT_, NT], F32R)
        w_raw = [sb(top, f"w_raw{s}", [P, KT_, P]) for s in range(2)]
        w_hi = sb(top, "w_hi", [P, 2, KT_, P], F32R)
        w_lo = sb(top, "w_lo", [P, 2, KT_, P], F32R)
        os_fm = sb(top, "os_fm", [P, NHP, NSAMP])
        decode_ctx = top.enter_context(ExitStack())
        q_s = sb(decode_ctx, "q_s", [P, NHP, NSAMP])
        k_s_hi = sb(decode_ctx, "k_s_hi", [P, NHP, NSAMP], F32R)
        k_s_lo = sb(decode_ctx, "k_s_lo", [P, NHP, NSAMP], F32R)
        glr = sb(decode_ctx, "glr", [RANK, NT])
        newb = sb(decode_ctx, "newb", [NSAMP, NSAMP])

        stream = WeightStream(sem, ins["w_tiles"], w_raw, w_hi, w_lo, h_hi, h_lo, bank)
        with nc.cleanup_on_exit():
            build_inputs(nc, ins, outs, scratch, sem, sb, bank, con, vec, cc, vv, epsb, gq8, h_hi, h_lo, glr, stream)
        with nc.cleanup_on_exit():
            build_fox(nc, ins, outs, scratch, sem, sb, psum, bank, cc, vv, epsb, gq8, stream, os_fm, q_s, k_s_hi,
                      k_s_lo, newb)
        with nc.cleanup_on_exit():
            build_gla(nc, ins, outs, scratch, sem, sb, psum, bank, cc, vv, epsb, stream, os_fm, q_s, k_s_hi, k_s_lo,
                      newb, glr)
        decode_ctx.close()
        with nc.cleanup_on_exit():
            build_merge(nc, ins, outs, scratch, sem, sb, bank, stream, os_fm)


class WeightStream:

    def __init__(self, sem, dram, raw, hi, lo, h_hi, h_lo, bank):
        self.dram, self.raw, self.hi, self.lo = dram, raw, hi, lo
        self.h_hi, self.h_lo, self.bank = h_hi, h_lo, bank
        self.loaded = [sem(f"w_loaded{s}") for s in range(2)]
        self.const_in = sem("const_in")
        self.passed = sem("passed")
        self.hi_set, self.lo_set = sem("w_hi_set"), sem("w_lo_set")
        self.projected = sem("w_projected")
        self.z_read = sem("z_read")

    def phase(self, base, per, ring):
        self.base, self.per, self.ring = base, per, ring

    def pass_waits(self, eng):
        eng.sem_inc(self.passed, 1)

    def open_act(self, act):
        opened(act, self.hi_set)

    def open_dve(self, dve):
        opened(dve, self.lo_set, self.z_read)

    def open_pe(self, pe):
        opened(pe, self.projected)

    def load_first(self, sp, g):
        sp.dma_start(self.raw[g][:], self.dram[g]).then_inc(self.loaded[g], 16)

    def split_hi_first(self, act):
        act.wait_ge(self.loaded[0], 16)
        act.activation(self.hi[:, 0], self.raw[0][:], ACT.Copy).then_inc(self.hi_set, 1)

    def split_lo_first(self, dve):
        dve.wait_ge(self.hi_set, 2)
        dve.tensor_tensor(self.lo[:, 0], self.raw[0][:], self.hi[:, 0].bitcast(F32),
                          ALU.subtract).then_inc(self.lo_set, 1)

    def load(self, sp, i, n):
        sp.wait_ge(self.lo_set, upto(i, self.per, n + 1, self.base))
        sp.dma_start(self.raw[n % 2][:], self.dram[ds(i * self.per + (self.base + n + 2), 1)]
                     .rearrange("o p k c -> (o p) k c")).then_inc(self.loaded[n % 2], 16)

    def split_hi(self, act, i, n):
        s = (n + 1) % 2
        act.wait_ge(self.loaded[s], i * (self.per * 8) + 16 * ((self.base + n + 1) // 2 + 1))
        act.wait_ge(self.projected, i * (3 * self.per) + 3 * (self.base + n) + 1)
        act.activation(self.hi[:, s], self.raw[s][:], ACT.Copy).then_inc(self.hi_set, 1)

    def split_lo(self, dve, i, n):
        s = (n + 1) % 2
        dve.wait_ge(self.hi_set, upto(i, self.per, n + 2, self.base))
        dve.tensor_tensor(self.lo[:, s], self.raw[s][:], self.hi[:, s].bitcast(F32),
                          ALU.subtract).then_inc(self.lo_set, 1)

    def chunk(self, i, n, c):
        return upto(i, 3 * self.per, 3 * n + c + 1, 3 * self.base)

    def bank_of(self, n, c):
        return self.bank[self.ring[(3 * n + c) % len(self.ring)]][:, 0:CHUNKS[c][1]]

    def project(self, pe, i, n, c, ks=range(KT_)):
        t0, w = CHUNKS[c]
        s = n % 2
        if ks[0] == 0:
            pe.wait_ge(self.lo_set, upto(i, self.per, n + 1, self.base))
            pe.wait_ge(self.z_read, i * (3 * self.per) + 3 * self.base + max(3 * n + c + 1 - len(self.ring), 0) + 1)
        out = self.bank_of(n, c)
        for k in ks:
            for a, (wt, h) in enumerate(((self.hi, self.h_hi), (self.hi, self.h_lo), (self.lo, self.h_hi))):
                m = pe.matmul(out, wt[:, s, k, :], h[:, k, t0:t0 + w], start=(k == 0 and a == 0),
                              stop=(k == KT_ - 1 and a == 2))
        if ks[-1] == KT_ - 1:
            m.then_inc(self.projected, 1)


def build_inputs(nc, ins, outs, scratch, sem, sb, bank, con, vec, cc, vv, epsb, gq8, h_hi, h_lo, glr, stream):
    with ExitStack() as ctx:
        x_in = [sb(ctx, f"x_in{s}", [P, D]) for s in range(2)]
        hn = [sb(ctx, f"hn{s}", [P, D]) for s in range(2)]
        junk = sb(ctx, "x_junk", [P, D])
        hg = [sb(ctx, f"hg{s}", [P, 4, P]) for s in range(2)]
        stat = sb(ctx, "x_stat", [P, 2, 4])
        w_gate = sb(ctx, "w_gate", [P, KT_, 48])
        w_gate_hi = sb(ctx, "w_gate_hi", [P, KT_, 48], F32R)
        w_gate_lo = sb(ctx, "w_gate_lo", [P, KT_, 48], F32R)
        ffx = sb(ctx, "ffx", [H, NT])
        ffa = sb(ctx, "ffa", [H, NT])
        logf = sb(ctx, "logf", [H, NT])
        ones = sb(ctx, "ones_row", [H, SEQ])
        cum = sb(ctx, "cum", [H, NT])
        ncum = sb(ctx, "ncum", [H, SEQ])
        lft = sb(ctx, "logf_tok", [P, TT + 1, H])

        x_loaded = [sem(f"x_loaded{s}") for s in range(2)]
        const_in = stream.const_in
        eps_set, sq_sum, ms_ln, rms_inv = sem("eps_set"), sem("sq_sum"), sem("ms_ln"), sem("rms_inv")
        x_scaled, x_turned, x_gained, h_hi_set, h_lo_set = (sem(n) for n in
            ("x_scaled", "x_turned", "x_gained", "h_hi_set", "h_lo_set"))
        wg_zero, wg_in, wg_hi, wg_lo = sem("wg_zero"), sem("wg_in"), sem("wg_hi"), sem("wg_lo")
        gate_mm, ff_x, ff_ab, ff_exp, ff_ln, glr_set = (sem(n) for n in
            ("gate_mm", "ff_x", "ff_ab", "ff_exp", "ff_ln", "glr_set"))
        logf_set, cum_set, lf_turned, lf_tok, a_stored = (sem(n) for n in
            ("logf_set", "cum_set", "lf_turned", "lf_tok", "a_stored"))

        xp = ins["x_prompt"].rearrange("a l d -> (a l) d")
        xs = ins["x_sample"].rearrange("b l d -> (b l) d")
        def tiles(eng):
            with eng.Fori(0, TT // 2) as i:
                for s in range(2):
                    yield i * 2 + s, i, s, P, i * (2 * P) + s * P
            yield TT, TT // 2, 0, NSAMP, SEQ

        with nc.Block() as block:
            @block.sync
            def _(sp):
                sp.dma_start(con[:], ins["const"]).then_inc(const_in, 16)
                sp.dma_start(vec[:], ins["vecs"]).then_inc(const_in, 16)
                sp.wait_ge(wg_zero, 1)
                sp.dma_start(w_gate[:, :, 0:H], ins["w_ff"]).then_inc(wg_in, 16)
                sp.dma_start(w_gate[:, :, 32:32 + RANK], ins["w_lr"]).then_inc(wg_in, 16)
                for t, i, s, n, t0 in tiles(sp):
                    sp.wait_ge(x_scaled, upto(i, 2, s - 1))
                    src = xp[ds(t0, P), :] if n == P else xs
                    sp.dma_start(x_in[s][0:n, :], src).then_inc(x_loaded[s], 16)
                for g in range(2):
                    stream.load_first(sp, g)
                sp.wait_ge(lf_tok, 2)
                sp.dma_start(outs["logf_p"].rearrange("(t p) h -> p t h", p=P), lft[:, 0:TT, :]).then_inc(a_stored, 16)
                sp.dma_start(outs["logf_s"], lft[0:NSAMP, TT, :]).then_inc(a_stored, 16)
                sp.wait_ge(cum_set, 3)
                sp.dma_start(scratch["cum"], cum[:, 0:SEQ]).then_inc(a_stored, 16)
                sp.dma_start(scratch["ncum"], ncum[:]).then_inc(a_stored, 16)
                sp.dma_start(scratch["cum_s"], cum[:, SEQ:NT]).then_inc(a_stored, 16)
                sp.dma_start(scratch["ones"], ones[0:1, :]).then_inc(a_stored, 16)
                sp.wait_ge(a_stored, 6 * 16)

            @block.gpsimd
            def _(pool):
                pool.memset(epsb[:], EPS).then_inc(eps_set, 1)
                pool.memset(w_gate[:], 0.0).then_inc(wg_zero, 1)
                pool.memset(ones[:], 1.0).then_inc(eps_set, 1)

            @block.scalar
            def _(act):
                act.preload_act_table_set("natural_log_exp_and_others")
                opened(act, sq_sum, ms_ln, rms_inv, h_hi_set)
                act.wait_ge(eps_set, 2)
                for t, i, s, n, t0 in tiles(act):
                    act.wait_ge(x_loaded[s], i * 16 + 16)
                    act.activation(junk[0:n, :], x_in[s][0:n, :], ACT.Square,
                                   accum_out=stat[0:n, s, 0:1]).then_inc(sq_sum, 1)
                    act.wait_ge(sq_sum, upto(t, 1, 1))
                    act.activation(stat[0:n, s, 1:2], stat[0:n, s, 0:1], ACT.Ln, bias=epsb[0:n, :],
                                   scale=1.0 / D).then_inc(ms_ln, 1)
                    act.wait_ge(ms_ln, upto(t, 1, 1))
                    act.activation(stat[0:n, s, 2:3], stat[0:n, s, 1:2], ACT.Exp, scale=-0.5).then_inc(rms_inv, 1)
                    for g in range(2):
                        act.wait_ge(x_gained, upto(t, 2, g + 1))
                        act.activation(h_hi[:, 4 * g:4 * g + 4, ds(t0, n)], hg[g][:, :, 0:n], ACT.Copy).then_inc(h_hi_set, 1)
                stream.open_act(act)
                stream.split_hi_first(act)
                act.wait_ge(wg_in, 32)
                act.activation(w_gate_hi[:], w_gate[:], ACT.Copy).then_inc(wg_hi, 1)
                act.wait_ge(ff_ab, 1)
                act.activation(ffa[:], ffa[:], ACT.Exp, scale=-1.0).then_inc(ff_exp, 1)
                act.wait_ge(ff_exp, 1)
                act.activation(ffa[:], ffa[:], ACT.Ln, bias=1.0).then_inc(ff_ln, 1)

            @block.vector
            def _(dve):
                opened(dve, x_scaled, x_gained, h_lo_set)
                dve.wait_ge(const_in, 32)
                dve.tensor_scalar(gq8[:], vv("gq"), HD ** -0.5, None, ALU.mult)
                for t, i, s, n, t0 in tiles(dve):
                    dve.wait_ge(rms_inv, upto(t, 1, 1))
                    dve.wait_ge(x_turned, upto(i, 4, 2 * (s - 1)))
                    dve.tensor_scalar(hn[s][0:n, :], x_in[s][0:n, :], stat[0:n, s, 2:3], None, ALU.mult).then_inc(x_scaled, 1)
                    for g in range(2):
                        dve.wait_ge(x_turned, upto(t, 2, g + 1))
                        dve.wait_ge(h_lo_set, upto(t, 2, 0))
                        gain = vv("ln_g", P, 4 * g, 4).unsqueeze(2).to_broadcast([P, 4, n])
                        dve.tensor_tensor(hg[g][:, :, 0:n], bank[g].rearrange("p (k t) -> p k t", k=4)[:, :, 0:n],
                                          gain, ALU.mult).then_inc(x_gained, 1)
                    for g in range(2):
                        dve.wait_ge(h_hi_set, upto(t, 2, g + 1))
                        dve.tensor_tensor(h_lo[:, 4 * g:4 * g + 4, ds(t0, n)], hg[g][:, :, 0:n],
                                          h_hi[:, 4 * g:4 * g + 4, ds(t0, n)].bitcast(F32), ALU.subtract).then_inc(h_lo_set, 1)
                stream.open_dve(dve)
                stream.split_lo_first(dve)
                dve.wait_ge(wg_hi, 1)
                dve.tensor_tensor(w_gate_lo[:], w_gate[:], w_gate_hi[:].bitcast(F32), ALU.subtract).then_inc(wg_lo, 1)
                for c, (t0, n) in enumerate(CHUNKS):
                    dve.wait_ge(gate_mm, c + 1)
                    dve.tensor_scalar(ffx[:, t0:t0 + n], bank[2 + c][0:H, 0:n], vv("b_f", H), None, ALU.add).then_inc(ff_x, 1)
                    dve.tensor_copy(glr[:, t0:t0 + n], bank[2 + c][32:32 + RANK, 0:n]).then_inc(glr_set, 1)
                dve.wait_ge(ff_x, 3)
                dve.scalar_tensor_tensor(out=ffa[:], in0=ffx[:], scalar=-1.0, in1=ffx[:], op0=ALU.mult, op1=ALU.max).then_inc(ff_ab, 1)
                dve.wait_ge(ff_ln, 1)
                dve.scalar_tensor_tensor(out=logf[:], in0=ffx[:], scalar=0.0, in1=ffa[:], op0=ALU.min,
                                         op1=ALU.subtract).then_inc(logf_set, 1)
                dve.wait_ge(logf_set, 1)
                dve.wait_ge(eps_set, 2)
                dve.tensor_tensor_scan(cum[:, 0:SEQ], ones[:], logf[:, 0:SEQ], 0.0, ALU.mult, ALU.add).then_inc(cum_set, 1)
                dve.tensor_tensor_scan(cum[:, SEQ:NT], cc("scan_s", H), logf[:, SEQ:NT], 0.0, ALU.mult, ALU.add).then_inc(cum_set, 1)
                dve.wait_ge(cum_set, 2)
                dve.tensor_scalar(ncum[:], cum[:, 0:SEQ], -1.0, None, ALU.mult).then_inc(cum_set, 1)
                dve.wait_ge(lf_turned, 1)
                dve.tensor_copy(lft[:, 0:TT, :], bank[5][:, 0:TT * H].rearrange("p (t h) -> p t h", h=H)).then_inc(lf_tok, 1)
                dve.tensor_copy(lft[0:NSAMP, TT, :], bank[5][0:NSAMP, TT * H:(TT + 1) * H]).then_inc(lf_tok, 1)

            @block.tensor
            def _(pe):
                opened(pe, x_turned)
                stream.open_pe(pe)
                pe.wait_ge(const_in, 32)
                for t, i, s, n, t0 in tiles(pe):
                    pe.wait_ge(x_scaled, upto(t, 1, 1))
                    for g in range(2):
                        pe.wait_ge(x_gained, upto(t, 2, 0))
                        for k in range(4):
                            kk = 4 * g + k
                            m = pe.transpose(bank[g][:, k * P:k * P + n], hn[s][0:n, kk * P:(kk + 1) * P], cc("ident", n)[:, 0:n])
                        m.then_inc(x_turned, 1)
                pe.wait_ge(h_lo_set, upto(TT + 1, 2, 0))
                pe.wait_ge(wg_lo, 1)
                for c, (t0, n) in enumerate(CHUNKS):
                    for k in range(KT_):
                        for a, (w, h) in enumerate(((w_gate_hi, h_hi), (w_gate_hi, h_lo), (w_gate_lo, h_hi))):
                            m = pe.matmul(bank[2 + c][0:48, 0:n], w[:, k, :], h[:, k, t0:t0 + n],
                                          start=(k == 0 and a == 0), stop=(k == KT_ - 1 and a == 2))
                    m.then_inc(gate_mm, 1)
                pe.wait_ge(logf_set, 1)
                for t in range(TT + 1):
                    n = P if t < TT else NSAMP
                    m = pe.transpose(bank[5][0:n, t * H:(t + 1) * H], logf[:, t * P:t * P + n], cc("ident", H)[:, 0:H])
                m.then_inc(lf_turned, 1)


def build_fox(nc, ins, outs, scratch, sem, sb, psum, bank, cc, vv, epsb, gq8, stream, os_fm, q_s, k_s_hi, k_s_lo, newb):
    V, K, Q, G = range(4)
    U = 2 * TT
    PG = NPG // NHP
    with ExitStack() as ctx:
        ofox = sb(ctx, "ofox", [P, SEQ])
        v_fm = sb(ctx, "v_fm", [P, NT])
        v_tok = sb(ctx, "v_tok", [P, TT + 1, P])
        k_tok = sb(ctx, "k_tok", [P, TT + 1, P])
        ks_fm = sb(ctx, "ks_fm", [P, NSAMP])
        q_aug = sb(ctx, "q_aug", [HD + 2, 2, SEQ])
        k_aug = sb(ctx, "k_aug", [HD + 2, 2, SEQ])
        sq = sb(ctx, "sq", [P, 2, 512])
        inv = sb(ctx, "inv", [P, 2, 512])
        eg = sb(ctx, "eg", [P, 512])
        prob = [sb(ctx, f"prob{s}", [P, SEQ]) for s in range(2)]
        prob_t = [sb(ctx, f"prob_t{s}", [P, TT, P]) for s in range(2)]
        nmax = sb(ctx, "nmax", [P, 2])
        den = sb(ctx, "den", [P, 2])
        rden = sb(ctx, "rden", [P, 2])
        o_tok = sb(ctx, "o_tok", [P, 2, P])
        lfk = sb(ctx, "lfk", [P, PG, NB * H])
        lfc = sb(ctx, "lfc", [NB * H, PAST])
        total = sb(ctx, "total", [NB * H, 1])
        one = sb(ctx, "one", [P, 1])
        pages = sb(ctx, "pages", [1, NB * NPG], I32)

        names = ("v_turned v_tok_set k_turned k_tok_set squared norm_mm norm_ln norm_inv k_aug_set q_aug_set ks_set "
                 "ks_hi ks_lo g_exp g_one g_rec s_mm s_masked max_set exp_set p_turned pt_a pt_b pv_mm rden_set "
                 "o_set o_turned o_gated lf_turned2 lf_copied").split()
        S = {n: sem(n) for n in names}
        aug_in, aug_one, kv_stored, pg_in, lf_in = (sem(n) for n in ("aug_in", "aug_one", "kv_stored", "pg_in", "lf_in"))
        one_set, past_cum, past_bias, fin_in, newb_set, b_stored, of_stored = (sem(n) for n in
            ("one_set", "past_cum", "past_bias", "fin_in", "newb_set", "b_stored", "of_stored"))
        stream.phase(0, 4, (0, 1, 6))
        kp = outs["k_p"].rearrange("a b (t p) h d -> p (a b t) (h d)", p=P)
        vp = outs["v_p"].rearrange("a b (t p) h d -> p (a b t) (h d)", p=P)
        ks = outs["k_s"].rearrange("a b t h d -> (a b t) (h d)")
        vs = outs["v_s"].rearrange("a b t h d -> (a b t) (h d)")

        def W(eng, name, i, per, k):
            eng.wait_ge(S[name], upto(i, per, k))

        with nc.Block() as block:
            @block.sync
            def _(sp):
                for hh in range(2):
                    sp.dma_start(q_aug[HD:HD + 1, hh, :], scratch["ones"]).then_inc(aug_one, 16)
                    sp.dma_start(k_aug[HD + 1:HD + 2, hh, :], scratch["ones"]).then_inc(aug_one, 16)
                for t in range(TS):
                    sp.dma_start(newb[t:t + TS * (H - 1) + 1:TS, :], scratch["cum_s"]).then_inc(fin_in, 16)
                sp.sem_inc(kv_stored, 16)
                sp.sem_inc(of_stored, 16)
                with sp.Fori(0, NHP) as i:
                    W(sp, "s_mm", i, U, 0)
                    for hh in range(2):
                        sp.dma_start(q_aug[HD + 1:HD + 2, hh, :], scratch["cum"][ds(i * 2 + hh, 1), :]).then_inc(aug_in, 16)
                        sp.dma_start(k_aug[HD:HD + 1, hh, :], scratch["ncum"][ds(i * 2 + hh, 1), :]).then_inc(aug_in, 16)
                    for n in range(4):
                        stream.load(sp, i, n)
                        if n == Q:
                            W(sp, "v_tok_set", i, 3, 3)
                            sp.dma_start(vp[:, :, ds(i * P, P)], v_tok[:, 0:TT, :]).then_inc(kv_stored, 16)
                            sp.dma_start(vs[:, ds(i * P, P)], v_tok[0:NSAMP, TT, :]).then_inc(kv_stored, 16)
                    W(sp, "k_tok_set", i, 3, 3)
                    sp.dma_start(kp[:, :, ds(i * P, P)], k_tok[:, 0:TT, :]).then_inc(kv_stored, 16)
                    sp.dma_start(ks[:, ds(i * P, P)], k_tok[0:NSAMP, TT, :]).then_inc(kv_stored, 16)
                    W(sp, "o_gated", i, TT, TT)
                    sp.dma_start(scratch["ofox"][ds(i, 1)].rearrange("o p t -> (o p) t"), ofox[:]).then_inc(of_stored, 16)
                sp.wait_ge(of_stored, NHP * 16 + 16)
                sp.wait_ge(kv_stored, NHP * 64 + 16)
                sp.wait_ge(past_bias, 1)
                sp.dma_start(scratch["bias"], lfc[:]).then_inc(b_stored, 16)
                sp.wait_ge(b_stored, 16)

            @block.gpsimd
            def _(pool):
                pool.memset(one[:], 1.0).then_inc(one_set, 1)
                pool.dma_start(pages[:], ins["page_table"]).then_inc(pg_in, 16)
                pool.wait_ge(pg_in, 16)
                with pool.Fori(0, NHP) as i:
                    W(pool, "lf_turned2", i, 2, 0)
                    for g in range(PG):
                        for b in range(NB):
                            page = pool.value_load(pages[0:1, ds(i * PG + (b * NPG + g), 1)], min_val=0, max_val=NPHYS - 1)
                            pool.dma_start(lfk[:, g, b * H:(b + 1) * H], ins["cache_logf"][ds(page, 1)]
                                           .rearrange("o p h -> (o p) h")).then_inc(lf_in, 16)

            @block.scalar
            def _(act):
                opened(act, *(S[n] for n in ("v_tok_set", "k_tok_set", "squared", "norm_ln", "norm_inv", "ks_hi",
                                             "g_exp", "exp_set", "pt_b", "lf_copied")))

                def copy_out(i, tok, src, name, turned, b0):
                    for p in range(3):
                        if p == 0:
                            act.wait_ge(kv_stored, i * 64 + 16)
                        W(act, turned, i, 3, p + 1)
                        if p < 2:
                            act.activation(tok[:, 4 * p:4 * p + 4, :], src[b0 + p].rearrange("p (t c) -> p t c", t=4),
                                           ACT.Copy).then_inc(S[name], 1)
                        else:
                            act.activation(tok[0:NSAMP, TT, :], src[b0][0:NSAMP, 0:P], ACT.Copy).then_inc(S[name], 1)

                def exp(i, u):
                    n = (u // 2 + 1) * P
                    W(act, "max_set", i, U, u + 1)
                    W(act, "p_turned", i, U, u - 1)
                    W(act, "rden_set", i, U, u - 1)
                    act.activation(prob[u % 2][:, 0:n], psum[:, (2 + 2 * (u % 2)) * 512:][:, 0:n], ACT.Exp,
                                   bias=nmax[:, u % 2:u % 2 + 1], accum_out=den[:, u % 2:u % 2 + 1]).then_inc(S["exp_set"], 1)

                with act.Fori(0, NHP) as i:
                    for n in range(4):
                        stream.split_hi(act, i, n)
                        if n == K:
                            copy_out(i, v_tok, bank, "v_tok_set", "v_turned", 2)
                        for c, (t0, w) in enumerate(CHUNKS):
                            z = stream.bank_of(n, c)
                            if n == Q and c == 1:
                                copy_out(i, k_tok, bank, "k_tok_set", "k_turned", 4)
                            if n in (K, Q):
                                e = 3 * (n - K) + c
                                act.wait_ge(stream.projected, stream.chunk(i, n, c))
                                W(act, "norm_mm", i, 6, e - 1)
                                act.activation(sq[:, e % 2, 0:w], z, ACT.Square).then_inc(S["squared"], 1)
                                W(act, "norm_mm", i, 6, e + 1)
                                act.wait_ge(stream.z_read, i * 12 + 3 * n + c)
                                act.activation(inv[:, e % 2, 0:w], bank[7][:, 0:w], ACT.Ln, bias=epsb[:], scale=1.0 / HD)\
                                   .then_inc(S["norm_ln"], 1)
                                W(act, "norm_ln", i, 6, e + 1)
                                act.activation(inv[:, e % 2, 0:w], inv[:, e % 2, 0:w], ACT.Exp, scale=-0.5)\
                                   .then_inc(S["norm_inv"], 1)
                            if n == G:
                                act.wait_ge(stream.projected, stream.chunk(i, n, c))
                                act.wait_ge(stream.z_read, i * 12 + 3 * n + c + 1)
                                act.activation(eg[:, 0:w], z, ACT.Exp, scale=-1.0).then_inc(S["g_exp"], 1)
                        if n == K:
                            W(act, "ks_set", i, 1, 1)
                            act.activation(k_s_hi[:, ds(i, 1), :], ks_fm[:].unsqueeze(1), ACT.Copy).then_inc(S["ks_hi"], 1)
                    for p in range(2):
                        W(act, "lf_turned2", i, 2, p + 1)
                        act.activation(lfc[:, ds(i * (PG * P) + p * 512, 512)], bank[6 + p][0:NB * H, :], ACT.Copy)\
                           .then_inc(S["lf_copied"], 1)
                    exp(i, 0)
                    for u in range(U):
                        if u + 1 < U:
                            exp(i, u + 1)
                        if u // 2 >= 4:
                            b = u - 8
                            W(act, "p_turned", i, U, u + 1)
                            W(act, "pv_mm", i, U, u - 1)
                            act.activation(prob_t[u % 2][:, 4:u // 2 + 1, :], bank[7][:, 0:(u // 2 - 3) * P]
                                           .rearrange("p (k q) -> p k q", q=P), ACT.Copy).then_inc(S["pt_b"], 1)

            @block.vector
            def _(dve):
                opened(dve, *(S[n] for n in ("k_aug_set", "q_aug_set", "ks_set", "ks_lo", "g_one", "g_rec", "s_masked",
                                             "max_set", "pt_a", "rden_set", "o_set", "o_gated")))

                def head_rows(out, z, r, t0, w, gain, name):
                    for hh in range(2):
                        rows = slice(hh * HD, (hh + 1) * HD)
                        m = dve.scalar_tensor_tensor(out=out[0:HD, hh, t0:t0 + w], in0=z[rows], scalar=gain[rows],
                                                     in1=r[rows], op0=ALU.mult, op1=ALU.mult)
                        if hh == 0:
                            m.then_inc(S[name], 1)
                    m.then_inc(stream.z_read, 1)

                def smax(i, u):
                    qb, base = u // 2, (2 + 2 * (u % 2)) * 512
                    n = (qb + 1) * P
                    W(dve, "s_mm", i, U, u + 1)
                    diag = psum[:, base + qb * P:base + n]
                    dve.tensor_tensor(diag, diag, cc("causal"), ALU.add).then_inc(S["s_masked"], 1)
                    W(dve, "s_masked", i, U, u + 1)
                    W(dve, "exp_set", i, U, u - 1)
                    dve.tensor_reduce(nmax[:, u % 2:u % 2 + 1], psum[:, base:base + n], AX_X, ALU.max,
                                      negate=True).then_inc(S["max_set"], 1)

                def finish(i, u):
                    hh = u % 2
                    W(dve, "exp_set", i, U, u + 1)
                    dve.reciprocal(rden[:, hh:hh + 1], den[:, hh:hh + 1]).then_inc(S["rden_set"], 1)
                    W(dve, "rden_set", i, U, u + 1)
                    W(dve, "pv_mm", i, U, u + 1)
                    W(dve, "o_turned", i, TT, u // 2 - 1)
                    dve.tensor_scalar(o_tok[:, u // 2 % 2, hh * HD:(hh + 1) * HD], bank[hh][:, 0:HD],
                                      rden[:, hh:hh + 1], None, ALU.mult).then_inc(S["o_set"], 1)

                with dve.Fori(0, NHP) as i:
                    for n in range(4):
                        stream.split_lo(dve, i, n)
                        for c, (t0, w) in enumerate(CHUNKS):
                            z = stream.bank_of(n, c)
                            if n == V:
                                dve.wait_ge(stream.projected, stream.chunk(i, n, c))
                                W(dve, "v_turned", i, 3, 0)
                                dve.tensor_copy(v_fm[:, t0:t0 + w], z).then_inc(stream.z_read, 1)
                            if n in (K, Q):
                                e = 3 * (n - K) + c
                                r = inv[:, e % 2, 0:w]
                                W(dve, "norm_inv", i, 6, e + 1)
                                if c == 0:
                                    W(dve, "s_mm", i, U, 0)
                                if c < 2 and n == K:
                                    head_rows(k_aug, z, r, t0, w, vv("gk"), "k_aug_set")
                                elif c < 2:
                                    head_rows(q_aug, z, r, t0, w, gq8, "q_aug_set")
                                elif n == K:
                                    W(dve, "k_turned", i, 3, 0)
                                    dve.scalar_tensor_tensor(out=ks_fm[:], in0=z, scalar=vv("gk"), in1=r, op0=ALU.mult,
                                                             op1=ALU.mult).then_inc(S["ks_set"], 1)
                                    W(dve, "ks_set", i, 1, 1)
                                    W(dve, "ks_hi", i, 1, 1)
                                    dve.tensor_tensor(k_s_lo[:, ds(i, 1), :], ks_fm[:].unsqueeze(1),
                                                      k_s_hi[:, ds(i, 1), :].bitcast(F32), ALU.subtract)\
                                       .then_inc(stream.z_read, 1)
                                else:
                                    dve.scalar_tensor_tensor(out=q_s[:, ds(i, 1), :], in0=z.unsqueeze(1), scalar=gq8[:],
                                                             in1=r.unsqueeze(1), op0=ALU.mult, op1=ALU.mult)\
                                       .then_inc(stream.z_read, 1)
                            if n == G:
                                W(dve, "g_exp", i, 3, c + 1)
                                dve.tensor_scalar(eg[:, 0:w], eg[:, 0:w], 1.0, None, ALU.add).then_inc(S["g_one"], 1)
                                W(dve, "g_one", i, 3, c + 1)
                                dve.reciprocal(eg[:, 0:w], eg[:, 0:w]).then_inc(S["g_rec"], 1)
                                W(dve, "g_rec", i, 3, c + 1)
                                if c == 0:
                                    dve.wait_ge(of_stored, i * 16 + 16)
                                o = ofox[:, t0:t0 + w].unsqueeze(1) if c < 2 else os_fm[:, ds(i, 1), :]
                                dve.tensor_tensor(o, z.unsqueeze(1), eg[:, 0:w].unsqueeze(1), ALU.mult)\
                                   .then_inc(stream.z_read, 1)
                    smax(i, 0)
                    for u in range(U + 2):
                        if u + 1 < U:
                            smax(i, u + 1)
                        if u < U:
                            k = min(u // 2 + 1, 4)
                            W(dve, "p_turned", i, U, u + 1)
                            W(dve, "pv_mm", i, U, u - 1)
                            dve.tensor_copy(prob_t[u % 2][:, 0:k, :], bank[6][:, 0:k * P].rearrange("p (k q) -> p k q", q=P))\
                               .then_inc(S["pt_a"], 1)
                        if 1 <= u <= U:
                            finish(i, u - 1)
                        if u >= 2 and u % 2 == 1:
                            qb = (u - 2) // 2
                            W(dve, "o_turned", i, TT, qb + 1)
                            o = ofox[:, qb * P:(qb + 1) * P]
                            dve.tensor_tensor(o, bank[1][:, P:2 * P], o, ALU.mult).then_inc(S["o_gated"], 1)
                dve.wait_ge(one_set, 1)
                dve.wait_ge(S["lf_copied"], upto(NHP, 2, 0))
                dve.tensor_tensor_scan(lfc[:], one[0:NB * H, :].to_broadcast([NB * H, PAST]), lfc[:], 0.0, ALU.mult,
                                       ALU.add).then_inc(past_cum, 1)
                dve.wait_ge(past_cum, 1)
                dve.tensor_copy(total[:], lfc[:, PAST - 1:PAST]).then_inc(past_cum, 1)
                dve.wait_ge(past_cum, 2)
                dve.tensor_scalar(lfc[:], lfc[:], -1.0, total[:], ALU.mult, ALU.add).then_inc(past_bias, 1)
                dve.wait_ge(fin_in, 16 * TS)
                nb = newb[:].rearrange("r (b k) -> r b k", b=NB)
                dve.tensor_tensor(nb, cc("newmask", NSAMP).unsqueeze(1).to_broadcast([NSAMP, NB, TS]), nb,
                                  ALU.subtract).then_inc(newb_set, 1)

            @block.tensor
            def _(pe):
                opened(pe, *(S[n] for n in ("v_turned", "k_turned", "norm_mm", "s_mm", "p_turned", "pv_mm", "o_turned",
                                            "lf_turned2")))

                def turn_kv(i, src, name, done, b0):
                    for p in range(3):
                        W(pe, done, i, 3, p - 1 if p == 2 else 0)
                        stream.pass_waits(pe)
                        for t in (range(4 * p, 4 * p + 4) if p < 2 else [TT]):
                            out = bank[b0 + p % 2]
                            for o, a, ident in src(t):
                                n = P if t < TT else NSAMP
                                m = pe.transpose(out[0:n, (t % 4) * P + o:(t % 4) * P + o + ident.shape[1]], a, ident)
                        m.then_inc(S[name], 1)

                def scores(i, u):
                    qb, hh = u // 2, u % 2
                    W(pe, "exp_set", i, U, u - 1)
                    for c in range(0, qb + 1, 4):
                        n = min(4, qb + 1 - c) * P
                        b = 2 + 2 * hh + c // 4
                        m = pe.matmul(bank[b][:, 0:n], q_aug[:, hh, qb * P:(qb + 1) * P], k_aug[:, hh, c * P:c * P + n],
                                      start=True, stop=True)
                    m.then_inc(S["s_mm"], 1)

                def norm_sum(i, e):
                    w = CHUNKS[e % 3][1]
                    if e == 0:
                        W(pe, "pt_b", i, U - 8, 0)
                    W(pe, "squared", i, 6, e + 1)
                    W(pe, "norm_ln", i, 6, e)
                    pe.matmul(bank[7][:, 0:w], cc("bdones"), sq[:, e % 2, 0:w], start=True, stop=True).then_inc(S["norm_mm"], 1)

                with pe.Fori(0, NHP) as i:
                    for n in range(4):
                        for c in range(3):
                            stream.project(pe, i, n, c)
                            if n == G and c == 0:
                                norm_sum(i, 5)
                            e = 3 * (n - K) + c - 1
                            if n in (K, Q) and e >= 0:
                                norm_sum(i, e)
                            if n == K and c == 0:
                                pe.wait_ge(stream.z_read, stream.chunk(i, V, 2))
                                W(pe, "exp_set", i, U, 0)
                                turn_kv(i, lambda t: [(0, v_fm[:, t * P:min((t + 1) * P, NT)], cc("ident"))],
                                        "v_turned", "v_tok_set", 2)
                            if n == Q and c == 1:
                                pe.wait_ge(stream.z_read, stream.chunk(i, K, 2))
                                turn_kv(i, lambda t: [(hh * HD, k_aug[0:HD, hh, t * P:(t + 1) * P], cc("ident", HD)[:, 0:HD])
                                                      for hh in range(2)] if t < TT else [(0, ks_fm[:], cc("ident"))],
                                        "k_turned", "k_tok_set", 4)
                    for p in range(2):
                        pe.wait_ge(lf_in, i * (PG * NB * 16) + PG * NB * 16)
                        pe.wait_ge(stream.z_read, stream.chunk(i, G, 2))
                        W(pe, "pt_a", i, U, 0)
                        W(pe, "pt_b", i, U - 8, 0)
                        W(pe, "norm_ln", i, 6, 6)
                        stream.pass_waits(pe)
                        for g in range(4):
                            m = pe.transpose(bank[6 + p][0:NB * H, g * P:(g + 1) * P], lfk[:, 4 * p + g, :], cc("ident"))
                        m.then_inc(S["lf_turned2"], 1)
                    pe.wait_ge(stream.z_read, stream.chunk(i, Q, 2))
                    pe.wait_ge(aug_one, 64)
                    pe.wait_ge(aug_in, i * 64 + 64)
                    W(pe, "v_tok_set", i, 3, 3)
                    W(pe, "k_tok_set", i, 3, 3)
                    scores(i, 0)
                    for u in range(U + 2):
                        if u + 1 < U:
                            scores(i, u + 1)
                        if u < U:
                            W(pe, "exp_set", i, U, u + 1)
                            if u == 0:
                                W(pe, "lf_copied", i, 2, 2)
                            W(pe, "pt_a", i, U, u)
                            for k in range(u // 2 + 1):
                                if k == 4:
                                    W(pe, "pt_b", i, U - 8, u - 8)
                                m = pe.transpose(bank[6 + k // 4][:, (k % 4) * P:(k % 4 + 1) * P],
                                                 prob[u % 2][:, k * P:(k + 1) * P], cc("ident"))
                            m.then_inc(S["p_turned"], 1)
                        if 1 <= u <= U:
                            v = u - 1
                            W(pe, "pt_a", i, U, v + 1)
                            if v // 2 >= 4:
                                W(pe, "pt_b", i, U - 8, v - 7)
                            W(pe, "o_set", i, U, v - 1)
                            if v == 0:
                                pe.wait_ge(stream.z_read, stream.chunk(i, G, 2))
                            if v % 2:
                                W(pe, "o_gated", i, TT, v // 2)
                            for k in range(v // 2 + 1):
                                m = pe.matmul(bank[v % 2][:, 0:HD], prob_t[v % 2][:, k, :],
                                              v_tok[:, k, (v % 2) * HD:(v % 2 + 1) * HD], start=(k == 0), stop=(k == v // 2))
                            m.then_inc(S["pv_mm"], 1)
                        if u >= 2 and u % 2 == 1:
                            qb = (u - 2) // 2
                            W(pe, "o_set", i, U, 2 * qb + 2)
                            pe.transpose(bank[1][:, P:2 * P], o_tok[:, qb % 2, :], cc("ident")).then_inc(S["o_turned"], 1)
                    W(pe, "o_gated", i, TT, TT)


def schedule():
    V0, V1, Q, K, G0, G1 = range(6)

    def tile(n, after):
        out = []
        for c in range(3):
            out += [("z", n, c, 0), ("z", n, c, 1)] if c < 2 else [("z", n, c, 2)]
            out += [("evac", n, c)] + after.get(c, [])
        return out

    def gla(t):
        return [("att", t), ("o", t), ("og", t)]
    other = [("start",), ("decay", 0), ("decay", 1), ("decay", 2)]
    other += tile(V0, {})
    other += [("vturn", 0, p) for p in range(3)] + tile(V1, {})
    other += [("vturn", 1, p) for p in range(3)] + [("decayed",)]
    other += tile(Q, {}) + tile(K, {})
    other += [("kturn", p) for p in range(3)]
    g = [x for t in range(TT) for x in gla(t)] + [("satt",)] + [("sstate", r) for r in range(NB // 2)] + [("so",), ("sog",)]
    z = tile(G0, {}) + tile(G1, {})
    pre, post = z[:len(z) // 2], z[len(z) // 2:]
    other += pre + post[:4]
    rest = post[4:]
    while g:
        other.append(g.pop(0))
        if rest:
            other.append(rest.pop(0))
    assert not rest
    other += [("end",)]
    decode = []
    for q in range(2):
        decode += [("prep", q)] + [("k", q, p) for p in range(NPG + 1)] + [("soft", q)]
        decode += [("v", q, v) for v in range(NPG // 2 + 1)] + [("out", q), ("gate", q)]
    cost = {"k": 1, "v": 1.3, "soft": 0, "prep": 0, "out": 0.2, "gate": 0.2}
    total = sum(cost[d[0]] for d in decode)
    out, done, used = [], 0.0, 0
    for d in decode:
        out.append(d)
        done += cost[d[0]]
        want = int(len(other) * done / total + 0.5)
        while used < min(want, len(other)):
            out.append(other[used])
            used += 1
    out += other[used:]
    return out


def build_gla(nc, ins, outs, scratch, sem, sb, psum, bank, cc, vv, epsb, stream, os_fm, q_s, k_s_hi, k_s_lo, newb, glr):
    V0, V1, Q, K, G0, G1 = range(6)
    GTS = TT + 1
    with ExitStack() as ctx:
        wa = sb(ctx, "wa", [RANK, DK])
        ba = sb(ctx, "ba", [P, 1])
        t1 = sb(ctx, "t1", [P, 512])
        kdec = sb(ctx, "kdec", [P, NT])
        q_in = sb(ctx, "q_in", [P, NT])
        k_in = sb(ctx, "k_in", [P, NT])
        v_fm = k_in
        b_last = sb(ctx, "b_last", [P, SEQ // CH + NB])
        e_last = sb(ctx, "e_last", [P, SEQ // CH + NB])
        v_tok = sb(ctx, "gv_tok", [P, GTS, DV])
        k_tok = sb(ctx, "gk_tok", [P, GTS, DK])
        gate = sb(ctx, "gate", [P, 2, NT])
        state = sb(ctx, "state", [P, 3, DV])
        att = sb(ctx, "att", [P, P])
        o_n = sb(ctx, "o_n", [P, DV])
        ost = sb(ctx, "ost", [P, 3])
        s0 = sb(ctx, "s0", [P, 2, DV])
        s1 = sb(ctx, "s1", [P, 2, DV])
        q_diag = sb(ctx, "q_diag", [P, NB, NSAMP])
        k_row = sb(ctx, "k_row", [NSAMP, 2, DK])
        k_page = [sb(ctx, f"k_page{r}", [P, FW]) for r in range(4)]
        v_page = [sb(ctx, f"v_page{r}", [P, FW]) for r in range(4)]
        kt_hi = sb(ctx, "kt_hi", [P, 2, FW], F32R)
        kt_lo = sb(ctx, "kt_lo", [P, 2, FW], F32R)
        v_hi = sb(ctx, "v_hi", [P, 2, FW], F32R)
        v_lo = sb(ctx, "v_lo", [P, 2, FW], F32R)
        vn_hi = sb(ctx, "vn_hi", [TS, FW], F32R)
        vn_lo = sb(ctx, "vn_lo", [TS, FW], F32R)
        q_bd = sb(ctx, "q_bd", [P, NHP, 2, NSAMP], F32R)
        sc = sb(ctx, "sc", [P, HALF + TS])
        p_t = sb(ctx, "p_t", [P, 2, 2, 2, NSAMP], F32R)
        pn_t = sb(ctx, "pn_t", [TS, 2, NSAMP], F32R)
        smst = sb(ctx, "smst", [P, 8])
        u_lo = sb(ctx, "u_lo", [NSAMP, FW])
        vn_raw = u_lo[0:TS, :]
        pages = sb(ctx, "pages2", [1, NB * NPG], I32)

        per = {}
        for names, n in (("dc_mm dc_abs dc_exp dc_ln dc_min dc_y dc_cum", 3), ("v_turned vt_set", 6), ("kd_turned kd_set", 3),
                         ("bl_set", 2), ("eb_set en_set el_set dd_set ed_set ba_set st_zero", 1), ("kin_set", 3),
                         ("g_exp2 g_one2 g_rec2", 6), ("att_mm att_min att_set o_mm", GTS), ("u_mm u_half", TT), ("st_set", 2 * TT),
                         ("ss_set sl_set sr_set on_set ot_mm g1_set gated", GTS), ("qd_set", 1), ("kr_set", NB),
                         ("su_mm", NB // 2), ("s1_set", NB), ("kt_mm kt_hi_set kt_lo_set sc_mm s_add1 s_add", 2 * NPG),
                         ("new_mm n_add1 n_add", 2), ("qb_hi", 4), ("qb_lo", 4), ("qb_hi_a", 2), ("pad_set", 2),
                         ("mx1 mx2 mx3 mx4 exp2 dn1 dn2 dn3", 2), ("pt_mm pt_hi pt_lo", NPG), ("pn_mm pn_hi pn_lo", 2),
                         ("v_hi_set v_lo_set pv", 2 * NPG), ("vn_hi_set vn_lo_set pvn u_set od_set od_mm od_g", 2)):
            for n_ in names.split():
                per[n_] = n
        S = {n: sem("c_" + n) for n in per}
        k_in_s = [sem(f"k_landed{r}") for r in range(4)]
        v_in_s = [sem(f"v_landed{r}") for r in range(4)]
        sc_in, vn_in, wa_in, pg_in, s0_in, s1_out, st_out, og_out, zero_set, qbd_zero = (sem(n) for n in
            ("sc_in", "vn_in", "wa_in", "pg_in2", "s0_in", "s1_out", "st_out", "og_out", "zero_set", "qbd_zero"))
        stream.phase(TT * 2, 6, (0, 1))
        steps = schedule()

        def W(eng, name, i, k):
            eng.wait_ge(S[name], upto(i, per[name], k))

        def inc(m, name):
            m.then_inc(S[name], 1)

        def run(eng, handlers, i):
            reg = eng.alloc_register("turn")
            mine = [st for st in steps if st[0] in handlers]
            for n, st in enumerate(mine):
                if n % 6 == 0:
                    eng.reg_mov(reg, i)
                    turn = eng.snap(reg, min_val=0, max_val=GH - 1)
                handlers[st[0]](turn, *st[1:])

        rows = [slice(0, HD), slice(HD, P)]

        with nc.Block() as block:
            @block.sync
            def _(sp):
                sp.dma_start(pages[:], ins["page_table"]).then_inc(pg_in, 16)
                sp.wait_ge(pg_in, 16)
                for s in (st_out, og_out, s1_out):
                    sp.sem_inc(s, 16)

                def page_of(i, q, p):
                    return sp.value_load(pages[0:1, ds(i * (2 * NPG) + (q * NPG + p), 1)], min_val=0, max_val=NPHYS - 1)

                def load_k(i, q, p):
                    n = q * NPG + p
                    W(sp, "kt_mm", i, n - 3)
                    sp.dma_start(k_page[n % 4][:], ins["cache_k"][ds(page_of(i, q, p), 1)].rearrange("o p c -> (o p) c"))\
                      .then_inc(k_in_s[n % 4], 16)

                def load_v(i, q, n):
                    m = q * NPG + n
                    W(sp, "v_lo_set", i, m - 3)
                    page = page_of(i, q, n // 2 + (NPG // 2) * (n % 2))
                    sp.dma_start(v_page[m % 4][:], ins["cache_v"][ds(page, 1)].rearrange("o p c -> (o p) c"))\
                      .then_inc(v_in_s[m % 4], 16)

                def prep(i, q):
                    if q == 0:
                        for p in range(4):
                            load_k(i, q, p)
                    W(sp, "pt_mm", i, NPG // 2 * q)
                    for half in range(2):
                        for h in range(H):
                            src = scratch["bias"][ds(i * (2 * H) + (q * H + h), 1), half * HALF:(half + 1) * HALF]
                            sp.dma_start(sc[half * NSAMP + h * TS:half * NSAMP + (h + 1) * TS, 0:HALF],
                                         src.to_broadcast([TS, HALF])).then_inc(sc_in, 16)
                    W(sp, "od_mm", i, q)
                    sp.dma_start(vn_raw, outs["v_s"].rearrange("a b t h d -> (a b) t (h d)")[ds(i * 2 + q, 1)]
                                 .rearrange("o t c -> (o t) c")).then_inc(vn_in, 16)

                def kstep(i, q, p):
                    if p + 4 < NPG:
                        load_k(i, q, p + 4)
                    elif NPG > p >= NPG - 4:
                        load_v(i, q, p - (NPG - 4))

                def vstep(i, q, g):
                    for n in (2 * g + 2, 2 * g + 3):
                        if g >= 1 and n < NPG:
                            load_v(i, q, n)
                    if q == 0 and g >= NPG // 2 - 3 and g < NPG // 2 + 1:
                        load_k(i, 1, g - (NPG // 2 - 3))

                def start(i):
                    W(sp, "dc_mm", i, 0)
                    sp.dma_start(wa[:], ins["w_a2"][ds(i, 1)].rearrange("o r c -> (o r) c")).then_inc(wa_in, 16)

                def z(i, n, c, part):
                    if c == 0 and part == 0:
                        stream.load(sp, i, n)

                def state_in(i, r):
                    W(sp, "s1_set", i, 2 * r)
                    for j in range(2):
                        src = ins["state"][2 * r + j, ds(i, 1)].rearrange("o k v -> (o k) v")
                        sp.dma_start(s0[:, j, :], src).then_inc(s0_in, 16)

                def state_out(i, r):
                    W(sp, "s1_set", i, 2 * r + 2)
                    for j in range(2):
                        dst = outs["gla_s"][0, 2 * r + j, ds(i, 1)].rearrange("o k v -> (o k) v")
                        sp.dma_start(dst, s1[:, j, :]).then_inc(s1_out, 16)

                def att_step(i, t):
                    if t == TT - 1:
                        state_in(i, 0)

                def satt(i):
                    W(sp, "st_set", i, 2 * TT)
                    dst = outs["gla_p"][0, 0, ds(i, 1)].rearrange("o k v -> (o k) v")
                    sp.dma_start(dst, state[:, 2 * TT % 3, :]).then_inc(st_out, 16)

                def sstate(i, r):
                    if r + 1 < NB // 2:
                        state_in(i, r + 1)
                    state_out(i, r)

                def end(i):
                    W(sp, "gated", i, GTS)
                    sp.dma_start(scratch["ogla"][ds(i, 1)].rearrange("o p a t -> (o p) a t"), gate[:]).then_inc(og_out, 16)

                with sp.Fori(0, GH) as i:
                    run(sp, {"prep": prep, "k": kstep, "v": vstep, "start": start, "z": z, "att": att_step, "satt": satt,
                             "sstate": sstate, "end": end}, i)
                sp.wait_ge(st_out, GH * 16 + 16)
                sp.wait_ge(og_out, GH * 16 + 16)
                sp.wait_ge(s1_out, GH * NB * 16 + 16)

            @block.gpsimd
            def _(pool):
                opened(pool, S["v_lo_set"])
                pool.memset(q_diag[:], 0.0).then_inc(zero_set, 1)

                def low(i, q, n):
                    m = q * NPG + n
                    W(pool, "v_hi_set", i, m + 1)
                    inc(pool.tensor_tensor(v_lo[:, m % 2, :], v_page[m % 4][:], v_hi[:, m % 2, :].bitcast(F32),
                                           ALU.subtract), "v_lo_set")

                def vstep(i, q, g):
                    if g < NPG // 2:
                        low(i, q, 2 * g)
                        low(i, q, 2 * g + 1)

                with pool.Fori(0, GH) as i:
                    run(pool, {"v": vstep}, i)

            @block.scalar
            def _(act):
                opened(act, *(S[n] for n in ("dc_abs dc_exp dc_ln vt_set kd_set eb_set en_set el_set ed_set g_exp2 ss_set "
                                             "sl_set sr_set kt_hi_set qb_hi exp2 pt_hi pn_hi v_hi_set vn_hi_set u_set").split()))
                A = act.activation

                def prep(i, q):
                    W(act, "new_mm", i, q)
                    act.wait_ge(qbd_zero, 1)
                    for half in range(2):
                        dst = q_bd[rows[half]].rearrange("p a b c -> p (a b c)")[:, half * TS:]
                        inc(A(diag(dst, 2 * NSAMP + 2 * TS, NHP), q_s[rows[half], :, ds(i * (2 * TS) + q * TS, TS)], ACT.Copy), "qb_hi")
                    act.wait_ge(vn_in, i * 32 + 16 * (q + 1))
                    W(act, "pvn", i, q)
                    inc(A(vn_hi[:], vn_raw, ACT.Copy), "vn_hi_set")

                def kstep(i, q, p):
                    if p < NPG:
                        n = q * NPG + p
                        W(act, "kt_mm", i, n + 1)
                        W(act, "sc_mm", i, n - 1)
                        inc(A(kt_hi[:, n % 2, :], bank[3 + n % 2], ACT.Copy), "kt_hi_set")

                def soft(i, q):
                    W(act, "mx4", i, q + 1)
                    inc(A(sc[:], sc[:], ACT.Exp, bias=smst[:, 2:3], accum_out=smst[:, 4:5]), "exp2")

                def vstep(i, q, g):
                    if g < NPG // 2:
                        for h in range(2):
                            m = q * NPG + 2 * g + h
                            act.wait_ge(v_in_s[m % 4], i * (16 * 16) + 16 * (m // 4 + 1))
                            W(act, "pv", i, m - 1)
                            inc(A(v_hi[:, m % 2, :], v_page[m % 4][:], ACT.Copy), "v_hi_set")
                            if h == 0:
                                u = q * (NPG // 2) + g
                                W(act, "pt_mm", i, u + 1)
                                W(act, "pv", i, 2 * u - 2)
                                inc(A(p_t[:, u % 2, :, 0, :], bank[3 + u % 2][:, 0:P].rearrange("p (h r) -> p h r", h=2),
                                      ACT.Copy), "pt_hi")
                    else:
                        W(act, "pn_mm", i, q + 1)
                        inc(A(pn_t[:, 0, :], bank[5][0:TS, 0:NSAMP], ACT.Copy), "pn_hi")

                def out(i, q):
                    W(act, "pvn", i, q + 1)
                    W(act, "dn3", i, q + 1)
                    W(act, "od_mm", i, q)
                    W(act, "vn_lo_set", i, q + 1)
                    inc(A(u_lo[:], bank[6][NSAMP:P, :], ACT.Identity, scale=smst[NSAMP:P, 6:7]), "u_set")

                def decay(i, c):
                    w = CHUNKS[c][1]
                    W(act, "dc_mm", i, c + 1)
                    W(act, "ba_set", i, 1)
                    W(act, "dc_y", i, c)
                    act.wait_ge(stream.z_read, upto(i, 18, 0, 3 * 16))
                    inc(A(t1[:, 0:w], bank[2][:, 0:w], ACT.Abs, bias=ba[:]), "dc_abs")
                    W(act, "dc_abs", i, c + 1)
                    inc(A(t1[:, 0:w], t1[:, 0:w], ACT.Exp, scale=-1.0), "dc_exp")
                    W(act, "dc_exp", i, c + 1)
                    inc(A(t1[:, 0:w], t1[:, 0:w], ACT.Ln, bias=1.0), "dc_ln")

                def decayed(i):
                    W(act, "dc_cum", i, 3)
                    W(act, "o_mm", i, 0)
                    inc(A(q_in[:], kdec[:], ACT.Exp, scale=1.0 / TAU), "eb_set")
                    W(act, "v_turned", i, 6)
                    inc(A(k_in[:], kdec[:], ACT.Exp, scale=-1.0 / TAU), "en_set")
                    W(act, "bl_set", i, 2)
                    W(act, "st_set", i, 0)
                    W(act, "s1_set", i, 0)
                    inc(A(e_last[:], b_last[:], ACT.Exp, scale=1.0 / TAU), "el_set")
                    W(act, "dd_set", i, 1)
                    inc(A(kdec[:], kdec[:], ACT.Exp, scale=1.0 / TAU), "ed_set")

                def turned(i, dst, half, p, name, mm, k):
                    W(act, mm, i, k + 1)
                    b = bank[(2, 7, 2)[p]]
                    if p < 2:
                        inc(A(dst[:, 4 * p:4 * p + 4, half * P:(half + 1) * P], b.rearrange("p (t c) -> p t c", t=4), ACT.Copy), name)
                    else:
                        inc(A(dst[0:NSAMP, TT, half * P:(half + 1) * P], b[0:NSAMP, 0:P], ACT.Copy), name)

                def vturn(i, n, p):
                    turned(i, v_tok, n, p, "vt_set", "v_turned", 3 * n + p)

                def kturn(i, p):
                    turned(i, k_tok, 0, p, "kd_set", "kd_turned", p)

                def z(i, n, c, part):
                    if c == 0 and part == 0:
                        stream.split_hi(act, i, n)

                def evac(i, n, c):
                    if n >= G0:
                        w = CHUNKS[c][1]
                        act.wait_ge(stream.projected, stream.chunk(i, n, c))
                        act.wait_ge(stream.z_read, i * 18 + 3 * 16 + 3 * n + c + 1)
                        inc(A(t1[:, 0:w], stream.bank_of(n, c), ACT.Exp, scale=-1.0), "g_exp2")

                def ostat(i, t, w):
                    W(act, "o_mm", i, t + 1)
                    W(act, "ot_mm", i, t)
                    inc(A(o_n[0:w], bank[7][0:w, P:P + DV], ACT.Square, accum_out=ost[0:w, 0:1]), "ss_set")
                    W(act, "ss_set", i, t + 1)
                    inc(A(ost[0:w, 1:2], ost[0:w, 0:1], ACT.Ln, bias=epsb[0:w], scale=1.0 / DV), "sl_set")
                    W(act, "sl_set", i, t + 1)
                    inc(A(ost[0:w, 2:3], ost[0:w, 1:2], ACT.Exp, scale=-0.5), "sr_set")

                with act.Fori(0, GH) as i:
                    run(act, {"prep": prep, "k": kstep, "soft": soft, "v": vstep, "out": out, "decay": decay,
                              "decayed": decayed, "vturn": vturn, "kturn": kturn, "z": z, "evac": evac,
                              "o": lambda i, t: ostat(i, t, P), "so": lambda i: ostat(i, TT, NSAMP)}, i)

            @block.vector
            def _(dve):
                opened(dve, *(S[n] for n in ("dc_min dc_y dc_cum bl_set dd_set ba_set st_zero kin_set g_one2 g_rec2 att_min "
                                             "att_set st_set on_set g1_set gated qd_set kr_set s1_set kt_lo_set s_add1 s_add n_add1 n_add "
                                             "pad_set qb_lo mx1 mx2 mx3 mx4 dn1 dn2 dn3 pt_lo pn_lo vn_lo_set od_set od_g").split()))
                dve.memset(q_bd[:].bitcast(F32), 0.0).then_inc(qbd_zero, 1)
                dve.wait_ge(qbd_zero, 1)
                T = dve.tensor_tensor

                def prep(i, q):
                    W(dve, "exp2", i, q)
                    stream.pass_waits(dve)
                    inc(dve.memset(sc[NSAMP:P, HALF:HALF + TS], -BIG), "pad_set")
                    W(dve, "new_mm", i, q)
                    W(dve, "qb_hi", i, 2 * q + 2)
                    for half in range(2):
                        flat = q_bd[rows[half]].rearrange("p a b c -> p (a b c)")
                        hi = diag(flat[:, half * TS:], 2 * NSAMP + 2 * TS, NHP)
                        lo = diag(flat[:, NSAMP + half * TS:], 2 * NSAMP + 2 * TS, NHP)
                        inc(T(lo, q_s[rows[half], :, ds(i * (2 * TS) + q * TS, TS)], hi.bitcast(F32), ALU.subtract), "qb_lo")
                    W(dve, "vn_hi_set", i, q + 1)
                    inc(T(vn_lo[:], vn_raw, vn_hi[:].bitcast(F32), ALU.subtract), "vn_lo_set")

                def kstep(i, q, p):
                    if p < NPG:
                        n = q * NPG + p
                        W(dve, "kt_hi_set", i, n + 1)
                        inc(T(kt_lo[:, n % 2, :], bank[3 + n % 2], kt_hi[:, n % 2, :].bitcast(F32), ALU.subtract), "kt_lo_set")
                    if p >= 1:
                        n = q * NPG + p - 1
                        half, col = (p - 1) // (NPG // 2), (p - 1) % (NPG // 2) * PAGE
                        dst = sc[rows[half], col:col + PAGE]
                        if p == 1:
                            dve.wait_ge(sc_in, i * 512 + 256 * (q + 1))
                        W(dve, "sc_mm", i, n + 1)
                        inc(T(dst, bank[5 + n % 2][0:NSAMP, 0:PAGE], dst, ALU.add), "s_add1")
                        W(dve, "s_add1", i, n + 1)
                        inc(T(dst, bank[5 + n % 2][NSAMP:P, 0:PAGE], dst, ALU.add), "s_add")

                def soft(i, q):
                    new = sc[0:NSAMP, HALF:HALF + TS]
                    W(dve, "new_mm", i, q + 1)
                    inc(T(new, bank[5][0:NSAMP, 0:TS], newb[:, ds(i * (2 * TS) + q * TS, TS)], ALU.add), "n_add1")
                    W(dve, "n_add1", i, q + 1)
                    inc(T(new, bank[5][NSAMP:P, 0:TS], new, ALU.add), "n_add")
                    W(dve, "n_add", i, q + 1)
                    W(dve, "s_add", i, NPG * (q + 1))
                    W(dve, "pad_set", i, q + 1)
                    inc(dve.tensor_reduce(smst[:, 0:1], sc[:], AX_X, ALU.max), "mx1")
                    W(dve, "mx1", i, q + 1)
                    inc(dve.tensor_copy(smst[0:NSAMP, 1:2], smst[NSAMP:P, 0:1]), "mx2")
                    W(dve, "mx2", i, q + 1)
                    inc(dve.tensor_scalar(smst[0:NSAMP, 2:3], smst[0:NSAMP, 0:1], smst[0:NSAMP, 1:2], -1.0, ALU.max, ALU.mult), "mx3")
                    W(dve, "mx3", i, q + 1)
                    inc(dve.tensor_copy(smst[NSAMP:P, 2:3], smst[0:NSAMP, 2:3]), "mx4")
                    W(dve, "exp2", i, q + 1)
                    inc(dve.tensor_copy(smst[0:NSAMP, 5:6], smst[NSAMP:P, 4:5]), "dn1")
                    W(dve, "dn1", i, q + 1)
                    inc(T(smst[0:NSAMP, 7:8], smst[0:NSAMP, 4:5], smst[0:NSAMP, 5:6], ALU.add), "dn2")
                    W(dve, "dn2", i, q + 1)
                    dve.reciprocal(smst[0:NSAMP, 6:7], smst[0:NSAMP, 7:8])
                    inc(dve.reciprocal(smst[NSAMP:P, 6:7], smst[0:NSAMP, 7:8]), "dn3")

                def vstep(i, q, g):
                    if g < NPG // 2:
                        u = q * (NPG // 2) + g
                        W(dve, "pt_hi", i, u + 1)
                        inc(T(p_t[:, u % 2, :, 1, :], bank[3 + u % 2][:, 0:P].rearrange("p (h r) -> p h r", h=2),
                              p_t[:, u % 2, :, 0, :].bitcast(F32), ALU.subtract), "pt_lo")
                    else:
                        W(dve, "pn_hi", i, q + 1)
                        inc(T(pn_t[:, 1, :], bank[5][0:TS, 0:NSAMP], pn_t[:, 0, :].bitcast(F32), ALU.subtract), "pn_lo")

                def out(i, q):
                    W(dve, "u_set", i, q + 1)
                    inc(dve.scalar_tensor_tensor(out=u_lo[:], in0=bank[6][0:NSAMP, :], scalar=smst[0:NSAMP, 6:7], in1=u_lo[:],
                                                 op0=ALU.mult, op1=ALU.add), "od_set")

                def gate_out(i, q):
                    W(dve, "od_mm", i, q + 1)
                    for half in range(2):
                        src = diag(bank[5][rows[half], half * TS:], NSAMP + 2 * TS, NHP)
                        dst = os_fm[rows[half], :, ds(i * (2 * TS) + q * TS, TS)]
                        m = T(dst, src, dst, ALU.mult)
                    inc(m, "od_g")

                def start(i):
                    W(dve, "dc_ln", i, 0)
                    W(dve, "o_mm", i, 0)
                    o, _ = VEC_W["b_a"]
                    inc(dve.tensor_copy(ba[:], vv("b_a", P, 0, GH)[:, ds(i, 1)]), "ba_set")
                    W(dve, "ba_set", i, 1)
                    inc(dve.memset(state[:, 0, :], 0.0), "st_zero")

                def decay(i, c):
                    t0, w = CHUNKS[c]
                    y = kdec[:, t0:t0 + w]
                    W(dve, "dc_abs", i, c + 1)
                    W(dve, "kd_turned", i, 0)
                    inc(dve.tensor_scalar(y, bank[2][:, 0:w], ba[:], 0.0, ALU.add, ALU.min), "dc_min")
                    W(dve, "dc_min", i, c + 1)
                    W(dve, "dc_ln", i, c + 1)
                    inc(T(y, y, t1[:, 0:w], ALU.subtract), "dc_y")
                    W(dve, "dc_y", i, c + 1)
                    inc(dve.tensor_tensor_scan(y, cc("scan") if c < 2 else cc("scan_s"), y, 0.0, ALU.mult, ALU.add), "dc_cum")

                def decayed(i):
                    W(dve, "dc_cum", i, 3)
                    W(dve, "el_set", i, 0)
                    np_ = SEQ // CH
                    main = kdec[:, 0:SEQ].rearrange("p (c t) -> p c t", t=CH)
                    tail = kdec[:, SEQ:NT].rearrange("p (c t) -> p c t", t=TS)
                    inc(dve.tensor_copy(b_last[:, 0:np_].unsqueeze(2), main[:, :, CH - 1:CH]), "bl_set")
                    inc(dve.tensor_copy(b_last[:, np_:].unsqueeze(2), tail[:, :, TS - 1:TS]), "bl_set")
                    W(dve, "bl_set", i, 2)
                    W(dve, "en_set", i, 1)
                    T(main, b_last[:, 0:np_].unsqueeze(2).to_broadcast([P, np_, CH]), main, ALU.subtract)
                    inc(T(tail, b_last[:, np_:].unsqueeze(2).to_broadcast([P, NB, TS]), tail, ALU.subtract), "dd_set")

                def z(i, n, c, part):
                    if c == 0 and part == 0:
                        stream.split_lo(dve, i, n)

                def evac(i, n, c):
                    t0, w = CHUNKS[c]
                    zb = stream.bank_of(n, c)
                    dve.wait_ge(stream.projected, stream.chunk(i, n, c))
                    if n in (V0, V1):
                        W(dve, "v_turned", i, 3 * n)
                        W(dve, "att_mm", i, 0)
                        dve.tensor_copy(v_fm[:, t0:t0 + w], zb).then_inc(stream.z_read, 1)
                    if n == Q:
                        W(dve, "eb_set", i, 1)
                        dve.scalar_tensor_tensor(out=q_in[:, t0:t0 + w], in0=zb, scalar=DK ** -0.5, in1=q_in[:, t0:t0 + w],
                                                 op0=ALU.mult, op1=ALU.mult).then_inc(stream.z_read, 1)
                    if n == K:
                        W(dve, "ed_set", i, 1)
                        inc(T(k_in[:, t0:t0 + w], zb, k_in[:, t0:t0 + w], ALU.mult), "kin_set")
                        T(kdec[:, t0:t0 + w], zb, kdec[:, t0:t0 + w], ALU.mult).then_inc(stream.z_read, 1)
                    if n >= G0:
                        e = 3 * (n - G0) + c
                        W(dve, "g_exp2", i, e + 1)
                        inc(dve.tensor_scalar(t1[:, 0:w], t1[:, 0:w], 1.0, None, ALU.add), "g_one2")
                        W(dve, "g_one2", i, e + 1)
                        inc(dve.reciprocal(t1[:, 0:w], t1[:, 0:w]), "g_rec2")
                        W(dve, "g_rec2", i, e + 1)
                        dve.wait_ge(og_out, i * 16 + 16)
                        T(gate[:, n - G0, t0:t0 + w], zb, t1[:, 0:w], ALU.mult).then_inc(stream.z_read, 1)

                def att_mask(i, t, w, hi, lo):
                    W(dve, "att_mm", i, t + 1)
                    W(dve, "o_mm", i, t)
                    inc(T(att[0:w, 0:w], bank[7][0:w, 0:w], cc(hi, w), ALU.min), "att_min")
                    W(dve, "att_min", i, t + 1)
                    inc(T(att[0:w, 0:w], att[0:w, 0:w], cc(lo, w), ALU.max), "att_set")

                def att_step(i, t):
                    att_mask(i, t, P, "glamax", "glamin")
                    W(dve, "u_mm", i, t + 1)
                    if t == 0:
                        W(dve, "el_set", i, 1)
                        W(dve, "st_zero", i, 1)
                        dve.wait_ge(st_out, i * 16 + 16)
                    for j in range(2):
                        c = 2 * t + j
                        W(dve, "st_set", i, c)
                        inc(dve.scalar_tensor_tensor(out=state[:, (c + 1) % 3, :], in0=state[:, c % 3, :], scalar=e_last[:, c:c + 1],
                                                     in1=bank[2][:, j * DV:(j + 1) * DV], op0=ALU.mult, op1=ALU.add), "st_set")

                def o_norm(i, t, w):
                    W(dve, "sr_set", i, t + 1)
                    W(dve, "ot_mm", i, t)
                    inc(dve.tensor_scalar(o_n[0:w], bank[7][0:w, P:P + DV], ost[0:w, 2:3], None, ALU.mult), "on_set")

                def og(i, t, w):
                    W(dve, "ot_mm", i, t + 1)
                    for j in range(2):
                        dst = gate[:, j, t * P:t * P + w]
                        m = dve.scalar_tensor_tensor(out=dst, in0=bank[7][:, (0, 3 * P)[j]:(0, 3 * P)[j] + w],
                                                     scalar=vv("gla_g", P, j), in1=dst, op0=ALU.mult, op1=ALU.mult)
                    inc(m, "gated")

                def satt(i):
                    att_mask(i, TT, NSAMP, "smpmax", "smpmin")
                    dve.wait_ge(zero_set, 1)
                    inc(dve.tensor_copy(diag(q_diag[:].rearrange("p b t -> p (b t)"), NSAMP + TS, NB),
                                        q_in[:, SEQ:NT].rearrange("p (b t) -> p b t", b=NB)), "qd_set")

                def sstate(i, r):
                    W(dve, "su_mm", i, r)
                    for j in range(2):
                        b = 2 * r + j
                        inc(dve.tensor_scalar(k_row[:, j, :], k_tok[0:NSAMP, TT, :], cc("rowmask", NSAMP)[:, b:b + 1], None,
                                              ALU.mult), "kr_set")
                    W(dve, "su_mm", i, r + 1)
                    dve.wait_ge(s1_out, i * 128 + 32 * r + 16)
                    for j in range(2):
                        b = 2 * r + j
                        c = SEQ // CH + b
                        inc(dve.scalar_tensor_tensor(out=s1[:, j, :], in0=s0[:, j, :], scalar=e_last[:, c:c + 1],
                                                     in1=bank[2][:, j * DV:(j + 1) * DV], op0=ALU.mult, op1=ALU.add), "s1_set")

                with dve.Fori(0, GH) as i:
                    run(dve, {"prep": prep, "k": kstep, "soft": soft, "v": vstep, "out": out, "gate": gate_out, "start": start,
                              "decay": decay, "decayed": decayed, "z": z, "evac": evac, "att": att_step,
                              "o": lambda i, t: o_norm(i, t, P), "og": lambda i, t: og(i, t, P), "satt": satt,
                              "sstate": sstate, "so": lambda i: o_norm(i, TT, NSAMP), "sog": lambda i: og(i, TT, NSAMP)}, i)

            @block.tensor
            def _(pe):
                opened(pe, *(S[n] for n in ("dc_mm v_turned kd_turned att_mm o_mm u_mm u_half ot_mm su_mm kt_mm sc_mm new_mm pt_mm "
                                            "pn_mm pv pvn od_mm").split()))
                MM = pe.matmul

                def kstep(i, q, p):
                    if p < NPG:
                        n = q * NPG + p
                        pe.wait_ge(k_in_s[n % 4], i * (16 * 16) + 16 * (n // 4 + 1))
                        W(pe, "kt_lo_set", i, n - 1)
                        if p < 2:
                            W(pe, "pt_lo", i, q * (NPG // 2))
                        for hp in range(NHP):
                            m = pe.transpose(bank[3 + n % 2][:, hp * P:(hp + 1) * P], k_page[n % 4][:, hp * P:(hp + 1) * P], cc("ident"))
                        inc(m, "kt_mm")
                    if p >= 1:
                        n = q * NPG + p - 1
                        W(pe, "kt_lo_set", i, n + 1)
                        W(pe, "s_add", i, n - 1)
                        if p == 1:
                            W(pe, "qb_lo", i, 2 * q + 2)
                            W(pe, "od_g", i, q)
                        if p == 2:
                            W(pe, "od_set", i, q)
                        for k, kt in enumerate((kt_hi, kt_lo)):
                            for hp in range(NHP):
                                m = MM(bank[5 + n % 2][:, 0:PAGE], q_bd[:, hp].rearrange("p a c -> p (a c)"),
                                       kt[:, n % 2, hp * P:(hp + 1) * P], start=(k == 0 and hp == 0), stop=(k == 1 and hp == 3))
                        inc(m, "sc_mm")

                def soft(i, q):
                    W(pe, "s_add", i, NPG * (q + 1))
                    b8 = ds(i * (2 * TS) + q * TS, TS)
                    for k, kt in enumerate((k_s_hi, k_s_lo)):
                        for hp in range(NHP):
                            m = MM(bank[5][:, 0:TS], q_bd[:, hp].rearrange("p a c -> p (a c)"), kt[:, hp, b8],
                                   start=(k == 0 and hp == 0), stop=(k == 1 and hp == 3))
                    inc(m, "new_mm")

                def vstep(i, q, g):
                    if g < NPG // 2:
                        u = q * (NPG // 2) + g
                        W(pe, "exp2", i, q + 1)
                        W(pe, "pt_lo", i, u - 1)
                        if g < 2:
                            W(pe, "kt_lo_set", i, NPG * (q + 1))
                        inc(pe.transpose(bank[3 + u % 2][:, 0:P], sc[:, g * P:(g + 1) * P], cc("ident")), "pt_mm")
                    else:
                        W(pe, "n_add", i, q + 1)
                        stream.pass_waits(pe)
                        inc(pe.transpose(bank[5][0:TS, 0:NSAMP], sc[0:NSAMP, HALF:HALF + TS], cc("ident", NSAMP)[:, 0:NSAMP]), "pn_mm")
                    if g >= 1:
                        u = q * (NPG // 2) + g - 1
                        W(pe, "pt_lo", i, u + 1)
                        for h in range(2):
                            m_ = q * NPG + 2 * (g - 1) + h
                            W(pe, "v_lo_set", i, m_ + 1)
                            for k, v in enumerate((v_hi, v_lo)):
                                m = MM(bank[6], p_t[:, u % 2, h].rearrange("p a c -> p (a c)"), v[:, m_ % 2, :],
                                       start=(g == 1 and h == 0 and k == 0), stop=False)
                            inc(m, "pv")

                def out(i, q):
                    W(pe, "pn_lo", i, q + 1)
                    W(pe, "vn_lo_set", i, q + 1)
                    MM(bank[6], pn_t[:].rearrange("p a c -> p (a c)"), vn_hi[:], start=False, stop=False)
                    inc(MM(bank[6], pn_t[:].rearrange("p a c -> p (a c)"), vn_lo[:], start=False, stop=True), "pvn")

                def gate_out(i, q):
                    W(pe, "od_set", i, q + 1)
                    stream.pass_waits(pe)
                    for hp in range(NHP):
                        m = pe.transpose(bank[5][:, hp * NSAMP:(hp + 1) * NSAMP], u_lo[:, hp * P:(hp + 1) * P],
                                         cc("ident", NSAMP)[:, 0:NSAMP])
                    inc(m, "od_mm")

                def decay(i, c):
                    t0, w = CHUNKS[c]
                    pe.wait_ge(wa_in, i * 16 + 16)
                    W(pe, "dc_min", i, c)
                    W(pe, "s1_set", i, 0)
                    stream.pass_waits(pe)
                    inc(MM(bank[2][:, 0:w], wa[:], glr[:, t0:t0 + w], start=True, stop=True), "dc_mm")

                def turn(i, src, p, name, done, k):
                    W(pe, done, i, k - 1)
                    if p == 0:
                        W(pe, "dc_min", i, 3)
                        W(pe, "gated", i, 0)
                    stream.pass_waits(pe)
                    for t in (range(4 * p, 4 * p + 4) if p < 2 else [TT]):
                        n = P if t < TT else NSAMP
                        m = pe.transpose(bank[(2, 7, 2)[p]][0:n, (t % 4) * P:(t % 4) * P + P], src[:, t * P:t * P + n], cc("ident"))
                    inc(m, name)

                def vturn(i, n, p):
                    pe.wait_ge(stream.z_read, stream.chunk(i, n, 2))
                    W(pe, "vt_set", i, 3 * n + p - 1)
                    turn(i, v_fm, p, "v_turned", "vt_set", 3 * n + p)

                def kturn(i, p):
                    pe.wait_ge(stream.z_read, stream.chunk(i, K, 2))
                    W(pe, "vt_set", i, 6)
                    turn(i, kdec, p, "kd_turned", "kd_set", p)

                def z(i, n, c, part):
                    stream.project(pe, i, n, c, (range(0, 4), range(4, 8), range(8))[part])

                def att_step(i, t):
                    if t == 0:
                        W(pe, "vt_set", i, 6)
                        W(pe, "kd_set", i, 3)
                        W(pe, "kin_set", i, 3)
                    W(pe, "gated", i, t)
                    tok = slice(t * P, (t + 1) * P)
                    inc(MM(bank[7][:, 0:P], k_in[:, tok], q_in[:, tok], start=True, stop=True), "att_mm")
                    W(pe, "st_set", i, 2 * t)
                    for j in range(2):
                        if j == 1:
                            W(pe, "u_half", i, t + 1)
                        m = MM(bank[2][:, j * DV:(j + 1) * DV], k_tok[rows[j], t, :], v_tok[rows[j], t, :], start=True, stop=True)
                        inc(m, ("u_half", "u_mm")[j])

                def o_step(i, t):
                    W(pe, "att_set", i, t + 1)
                    MM(bank[7][:, P:P + DV], att[:], v_tok[:, t, :], start=True, stop=False, skip_group_check=True)
                    W(pe, "st_set", i, 2 * t + 1)
                    for j in range(2):
                        c = 2 * t + j
                        m = MM(bank[7][rows[j], P:P + DV], q_in[:, c * CH:(c + 1) * CH], state[:, c % 3, :], start=False,
                               stop=(j == 1), skip_group_check=True)
                    inc(m, "o_mm")

                def og(i, t, w):
                    W(pe, "on_set", i, t + 1)
                    stream.pass_waits(pe)
                    for j in range(2):
                        m = pe.transpose(bank[7][:, (0, 3 * P)[j]:(0, 3 * P)[j] + w], o_n[0:w, j * P:(j + 1) * P],
                                         cc("ident", w)[:, 0:w])
                    inc(m, "ot_mm")

                def satt(i):
                    W(pe, "gated", i, TT)
                    stream.pass_waits(pe)
                    inc(MM(bank[7][0:NSAMP, 0:NSAMP], k_in[:, SEQ:NT], q_in[:, SEQ:NT], start=True, stop=True), "att_mm")

                def sstate(i, r):
                    if r == 0:
                        W(pe, "att_set", i, TT + 1)
                        W(pe, "qd_set", i, 1)
                        W(pe, "st_set", i, 2 * TT)
                        stream.pass_waits(pe)
                        MM(bank[7][0:NSAMP, P:P + DV], att[0:NSAMP, 0:NSAMP], v_tok[0:NSAMP, TT, :], start=True, stop=False,
                           skip_group_check=True)
                    pe.wait_ge(s0_in, i * 128 + 32 * (r + 1))
                    W(pe, "s1_set", i, 2 * r)
                    W(pe, "kr_set", i, 2 * r + 2)
                    stream.pass_waits(pe)
                    for j in range(2):
                        m = MM(bank[7][0:NSAMP, P:P + DV], q_diag[:, 2 * r + j, :], s0[:, j, :], start=False,
                               stop=(r == 3 and j == 1), skip_group_check=True)
                    if r == 3:
                        inc(m, "o_mm")
                    for j in range(2):
                        m = MM(bank[2][:, j * DV:(j + 1) * DV], k_row[:, j, :], v_tok[0:NSAMP, TT, :], start=True, stop=True)
                    inc(m, "su_mm")

                with pe.Fori(0, GH) as i:
                    run(pe, {"k": kstep, "soft": soft, "v": vstep, "out": out, "gate": gate_out, "decay": decay, "vturn": vturn,
                             "kturn": kturn, "z": z, "att": att_step, "o": o_step, "og": lambda i, t: og(i, t, P),
                             "satt": satt, "sstate": sstate, "sog": lambda i: og(i, TT, NSAMP)}, i)


def build_merge(nc, ins, outs, scratch, sem, sb, bank, stream, os_fm):
    NA, NBR, HW = NHP, 2 * GH, D // 2
    YT = TT + 1
    with ExitStack() as ctx:
        fox_o = sb(ctx, "fox_o", [P, NA, NT])
        gla_o = sb(ctx, "gla_o", [P, NBR, NT])
        m_fm = sb(ctx, "m_fm", [P, KT_, NT])
        up_a = sb(ctx, "up_a", [P, NA, P])
        up_b = sb(ctx, "up_b", [P, NBR, P])
        g_a = sb(ctx, "g_a", [P, NT])
        g_b = sb(ctx, "g_b", [P, NT])
        x_ring = fox_o[:, 0:2, :].rearrange("p a t -> p (a t)")
        y_ring = fox_o[:, 2:4, :].rearrange("p a t -> p (a t)")

        per = {"ga_exp": 6, "gb_exp": 6, "a_mm": 6, "b_mm": 6, "g_one": 12, "g_rec": 12, "a_read": 6, "b_read": 6, "m_set": 6,
               "y_mm": YT, "y_set": YT}
        S = {n: sem("d_" + n) for n in per}
        o_in, up_a_in, up_b_in, w_in, os_in = (sem(n) for n in ("o_in", "up_a_in", "up_b_in", "w_out_in", "os_in"))
        x_in = [sem(f"xr_in{t}") for t in range(3)]
        y_out = [sem(f"y_out{t}") for t in range(3)]
        stream.phase(TT * 2 + 6 * GH, 4, (0, 1))
        xp = ins["x_prompt"].rearrange("a l d -> (a l) d")
        xs = ins["x_sample"].rearrange("b l d -> (b l) d")
        yp = outs["y_p"].rearrange("a l d -> (a l) d")
        ys = outs["y_s"].rearrange("b l d -> (b l) d")

        def W(eng, name, i, k):
            eng.wait_ge(S[name], upto(i, per[name], k))

        def inc(m, name):
            m.then_inc(S[name], 1)

        def ring(r, t):
            return r[:, t % 3 * HW:(t % 3 + 1) * HW]

        with nc.Block() as block:
            @block.sync
            def _(sp):
                for k in range(NA):
                    sp.dma_start(fox_o[:, k, 0:SEQ], scratch["ofox"][k]).then_inc(o_in, 16)
                for k in range(GH):
                    sp.dma_start(gla_o[:, 2 * k:2 * k + 2, :], scratch["ogla"][k]).then_inc(o_in, 16)
                with sp.Fori(0, KT_ // 2) as i:
                    for s in range(2):
                        W(sp, "a_mm", i, 3 * s)
                        sp.dma_start(up_a[:], ins["w_up_a"][ds(i * 2 + s, 1)].rearrange("o p k c -> (o p) k c")).then_inc(up_a_in, 16)
                        W(sp, "b_mm", i, 3 * s)
                        sp.dma_start(up_b[:], ins["w_up_b"][ds(i * 2 + s, 1)].rearrange("o p k c -> (o p) k c")).then_inc(up_b_in, 16)
                        for n in range(2):
                            stream.load(sp, i, 2 * s + n)
                W(sp, "b_mm", KT_ // 2, 0)
                W(sp, "a_mm", KT_ // 2, 0)
                for h in range(2):
                    sp.dma_start(gla_o[:, :, h * HW:(h + 1) * HW], ins["w_out"][:, :, h * HW:(h + 1) * HW]).then_inc(w_in, 16)
                    sp.wait_ge(w_in, 16 * (h + 1))
                for t in range(3):
                    sp.sem_inc(y_out[t], 16)

                with sp.Fori(0, 2) as h:
                    W(sp, "y_set", h, 0)

                    def load_x(t):
                        src = xp[t * P:(t + 1) * P, ds(h * HW, HW)] if t < TT else xs[:, ds(h * HW, HW)]
                        sp.dma_start(ring(x_ring, t)[0:P if t < TT else NSAMP], src).then_inc(x_in[t % 3], 16)
                    for t in range(3):
                        load_x(t)
                    for t in range(YT):
                        W(sp, "y_set", h, t + 1)
                        dst = yp[t * P:(t + 1) * P, ds(h * HW, HW)] if t < TT else ys[:, ds(h * HW, HW)]
                        sp.dma_start(dst, ring(y_ring, t)[0:P if t < TT else NSAMP]).then_inc(y_out[t % 3], 16)
                        if t + 3 < YT:
                            load_x(t + 3)
                for t in range(3):
                    sp.wait_ge(y_out[t], 16 + 2 * (YT // 3) * 16)

            @block.scalar
            def _(act):
                opened(act, S["ga_exp"], S["gb_exp"])
                act.activation(fox_o[:, :, SEQ:NT], os_fm[:], ACT.Copy).then_inc(os_in, 1)
                with act.Fori(0, KT_ // 2) as i:
                    for s in range(2):
                        for n, (g, name) in enumerate(((g_a, "ga_exp"), (g_b, "gb_exp"))):
                            stream.split_hi(act, i, 2 * s + n)
                            for c, (t0, w) in enumerate(CHUNKS):
                                act.wait_ge(stream.projected, stream.chunk(i, 2 * s + n, c))
                                W(act, "m_set", i, 3 * (s - 1) + c + 1 if s else 0)
                                m = act.activation(g[:, t0:t0 + w], stream.bank_of(2 * s + n, c), ACT.Exp, scale=-1.0)
                                m.then_inc(S[name], 1)
                                W(act, name, i, 3 * s + c + 1)
                                act.sem_inc(stream.z_read, 1)

            @block.vector
            def _(dve):
                opened(dve, *(S[n] for n in ("g_one", "g_rec", "a_read", "b_read", "m_set", "y_set")))
                with dve.Fori(0, KT_ // 2) as i:
                    for s in range(2):
                        for n, (g, name) in enumerate(((g_a, "ga_exp"), (g_b, "gb_exp"))):
                            stream.split_lo(dve, i, 2 * s + n)
                            for c, (t0, w) in enumerate(CHUNKS):
                                e = 6 * s + 3 * n + c
                                W(dve, name, i, 3 * s + c + 1)
                                inc(dve.tensor_scalar(g[:, t0:t0 + w], g[:, t0:t0 + w], 1.0, None, ALU.add), "g_one")
                                W(dve, "g_one", i, e + 1)
                                inc(dve.reciprocal(g[:, t0:t0 + w], g[:, t0:t0 + w]), "g_rec")
                        for c, (t0, w) in enumerate(CHUNKS):
                            e = 3 * s + c
                            W(dve, "g_rec", i, 6 * s + 3 + c + 1)
                            W(dve, "a_mm", i, e + 1)
                            inc(dve.tensor_tensor(g_a[:, t0:t0 + w], bank[2 + c][:, 0:w], g_a[:, t0:t0 + w], ALU.mult), "a_read")
                            W(dve, "b_mm", i, e + 1)
                            inc(dve.tensor_tensor(g_b[:, t0:t0 + w], bank[5 + c][:, 0:w], g_b[:, t0:t0 + w], ALU.mult), "b_read")
                            W(dve, "a_read", i, e + 1)
                            W(dve, "b_read", i, e + 1)
                            inc(dve.tensor_tensor(m_fm[:, ds(i * 2 + s, 1), t0:t0 + w], g_a[:, t0:t0 + w].unsqueeze(1),
                                                  g_b[:, t0:t0 + w].unsqueeze(1), ALU.add), "m_set")
                with dve.Fori(0, 2) as h:
                    for t in range(YT):
                        n = P if t < TT else NSAMP
                        W(dve, "y_mm", h, t + 1)
                        dve.wait_ge(x_in[t % 3], h * (YT // 3 * 16) + (t // 3 + 1) * 16)
                        dve.wait_ge(y_out[t % 3], h * (YT // 3 * 16) + (t // 3 + 1) * 16)
                        inc(dve.tensor_tensor(ring(y_ring, t)[0:n], bank[2 + t % 3][0:n, 0:HW], ring(x_ring, t)[0:n], ALU.add), "y_set")

            @block.tensor
            def _(pe):
                opened(pe, *(S[n] for n in ("a_mm", "b_mm", "y_mm")))
                pe.wait_ge(os_in, 1)
                pe.wait_ge(o_in, (NA + GH) * 16)
                with pe.Fori(0, KT_ // 2) as i:
                    for s in range(2):
                        for n in range(2):
                            for c in range(3):
                                stream.project(pe, i, 2 * s + n, c)
                        for c, (t0, w) in enumerate(CHUNKS):
                            for name, read, b0, wt, o, nk in (("a_mm", "a_read", 2, up_a, fox_o, NA),
                                                              ("b_mm", "b_read", 5, up_b, gla_o, NBR)):
                                if c == 0:
                                    pe.wait_ge(up_a_in if nk == NA else up_b_in, i * 32 + (s + 1) * 16)
                                W(pe, read, i, 3 * s + c - 2 if s else 0)
                                if s:
                                    W(pe, read, i, c + 1)
                                for k in range(nk):
                                    m = pe.matmul(bank[b0 + c][:, 0:w], wt[:, k, :], o[:, k, t0:t0 + w], start=(k == 0), stop=(k == nk - 1))
                                inc(m, name)
                with pe.Fori(0, 2) as h:
                    W(pe, "m_set", KT_ // 2, 0)
                    pe.wait_ge(w_in, h * 16 + 16)
                    for t in range(YT):
                        n = P if t < TT else NSAMP
                        W(pe, "y_set", h, t - 2)
                        stream.pass_waits(pe)
                        for k in range(KT_):
                            m = pe.matmul(bank[2 + t % 3][0:n, 0:HW], m_fm[:, k, t * P:t * P + n], gla_o[:, k, ds(h * HW, HW)],
                                          start=(k == 0), stop=(k == KT_ - 1))
                        inc(m, "y_mm")


def diag(flat, step, n):
    return bass.AP(flat.tensor, flat.offset, [list(flat.ap[0]), [step, n], [1, TS]])


_OUTS = {"y_p": (1, SEQ, D), "y_s": (NB, TS, D), "k_p": (1, 1, SEQ, H, HD), "v_p": (1, 1, SEQ, H, HD),
         "logf_p": (SEQ, H), "gla_p": (1, 1, GH, DK, DV), "k_s": (1, NB, TS, H, HD), "v_s": (1, NB, TS, H, HD),
         "logf_s": (NSAMP, H), "gla_s": (1, NB, GH, DK, DV)}


def kernel(x_prompt, x_sample, cache_k, cache_v, cache_logf, state_gla, page_table, ln_g, w_in, fox_b_f,
           q_norm_g, k_norm_g, gla_w_a2, gla_b_a, gla_norm_g, w_up_a, w_up_b, w_out):
    import concourse.bacc as bacc
    from concourse.bass_utils import run_bass_kernel_spmd as run

    def f(a):
        return np.ascontiguousarray(a)

    w = np.asarray(w_in)[0].reshape(KT_, P, -1).transpose(1, 0, 2)
    at = dict(zip(("fq", "fk", "fv", "ff", "fg", "gq", "gk", "gv", "glr", "gg", "ma", "mb"),
                  np.concatenate([[0], np.cumsum((FW, FW, FW, H, FW, GH * DK, GH * DK, GH * DV, RANK, GH * DV, D))])))

    def tile(name, j):
        c = at[name] + j * P
        return w[:, :, c:c + P]

    order = [(n, j) for j in range(NHP) for n in ("fv", "fk", "fq", "fg")]
    order += [t for g in range(GH) for t in (("gv", 2 * g), ("gv", 2 * g + 1), ("gq", g), ("gk", g),
                                             ("gg", 2 * g), ("gg", 2 * g + 1))]
    order += [(n, j) for j in range(KT_) for n in ("ma", "mb")]
    order += [("ma", 0), ("mb", 0)]
    vecs = np.zeros((P, NVEC), np.float32)

    def put(name, a):
        o, c = VEC_W[name]
        vecs[:a.shape[0], o:o + c] = a
    put("ln_g", np.asarray(ln_g)[0].reshape(KT_, P).T)
    put("gq", np.tile(np.asarray(q_norm_g)[0], 2)[:, None])
    put("gk", np.tile(np.asarray(k_norm_g)[0], 2)[:, None])
    put("gla_g", np.asarray(gla_norm_g)[0].reshape(2, P).T)
    put("b_f", np.asarray(fox_b_f)[0][:, None])
    put("b_a", np.asarray(gla_b_a)[0].reshape(GH, DK).T)
    arrays = {
        "x_prompt": x_prompt, "x_sample": x_sample, "const": constants(), "vecs": vecs,
        "w_ff": w[:, :, at["ff"]:at["ff"] + H], "w_lr": w[:, :, at["glr"]:at["glr"] + RANK],
        "w_tiles": np.stack([tile(n, j) for n, j in order]),
        "w_up_a": np.asarray(w_up_a)[0].reshape(NHP, P, KT_, P).transpose(2, 1, 0, 3),
        "w_up_b": np.asarray(w_up_b)[0].reshape(KT_, P, KT_, P).transpose(2, 1, 0, 3),
        "w_out": np.asarray(w_out)[0].reshape(KT_, P, D).transpose(1, 0, 2),
        "cache_k": np.asarray(cache_k).reshape(NPHYS, PAGE, FW), "cache_v": np.asarray(cache_v).reshape(NPHYS, PAGE, FW),
        "cache_logf": np.asarray(cache_logf).reshape(NPHYS, PAGE, H),
        "state": np.asarray(state_gla)[0], "page_table": np.asarray(page_table).reshape(1, NB * NPG),
        "w_a2": np.asarray(gla_w_a2)[0].reshape(RANK, GH, DK).transpose(1, 0, 2),
    }
    nc = bacc.Bacc("TRN2", target_bir_lowering=False, num_devices=1)
    feeds, ins, outs = {}, {}, {}
    for name, a in arrays.items():
        a = f(a)
        feeds[f"in_{name}"] = a
        ins[name] = nc.dram_tensor(f"in_{name}", a.shape, mybir.dt.from_np(a.dtype), kind="ExternalInput").ap()
    for name, shape in _OUTS.items():
        outs[name] = nc.dram_tensor(f"out_{name}", shape, F32, kind="ExternalOutput").ap()
    scratch = {name: nc.dram_tensor(f"tmp_{name}", shape, F32, kind="Internal").ap() for name, shape in
               {"cum": (H, SEQ), "ncum": (H, SEQ), "cum_s": (H, NSAMP), "ones": (1, SEQ), "ofox": (NHP, P, SEQ),
                "bias": (NB * H, PAST), "ogla": (GH, P, 2, NT)}.items()}
    fox_gla_step(nc, ins, outs, scratch)
    r = run(nc, [feeds], core_ids=[0]).results[0]
    o = {n: r[f"out_{n}"] for n in _OUTS}
    return (o["y_p"], o["y_s"], o["k_p"], o["v_p"], o["logf_p"].reshape(1, 1, SEQ, H), o["gla_p"],
            o["k_s"], o["v_s"], o["logf_s"].reshape(1, NB, TS, H), o["gla_s"])
```

```python
from contextlib import ExitStack

import numpy as np

import concourse.bass as bass
from concourse import mybir

F32 = mybir.dt.float32
F32R = mybir.dt.float32r
I32 = mybir.dt.int32
ALU = mybir.AluOpType
ACT = mybir.ActivationFunctionType
AX_X = mybir.AxisListType.X
ds = bass.ds

P = 128
D = 1024
SEQ = 1024
NB, TS = 8, 8
NSAMP = NB * TS
NT = SEQ + NSAMP
KT_ = D // P
H, HD = 8, 64
FW = H * HD
NHP = H // 2
GH, DK, DV = 4, 128, 256
CH = 64
RANK = 16
PAGE = 128
NPG = 32
PAST = NPG * PAGE
HALF = PAST // 2
NPHYS = NB * NPG + NB * NPG // 4
EPS = 1e-6
TAU = 16.0
BIG = 3.0e38
CHUNKS = [(0, 384), (384, 384), (768, 320)]
LASTP = SEQ - CHUNKS[2][0]
TT = SEQ // P

CONST_W = {}
_w = 0
for _n, _c in [("ident", 128), ("causal", 128), ("glamax", 128), ("glamin", 128), ("smpmax", 64),
               ("smpmin", 64), ("scan", 384), ("scan_last", 320), ("bdones", 128), ("rowmask", 8), ("newmask", 8)]:
    CONST_W[_n] = (_w, _c)
    _w += _c
NCONST = _w
VEC_W = {}
_w = 0
for _n, _c in [("ln_g", KT_), ("gq", 1), ("gk", 1), ("gla_g", 2), ("b_f", 1), ("b_a", GH)]:
    VEC_W[_n] = (_w, _c)
    _w += _c
NVEC = _w


def constants():
    c = np.zeros((P, NCONST), np.float32)

    def put(name, a):
        o, w = CONST_W[name]
        c[:a.shape[0], o:o + w] = a
    r = np.arange(P)
    put("ident", np.eye(P))
    put("causal", np.where(r[None, :] <= r[:, None], 0, -BIG))
    ok = (r[:, None] <= r[None, :]) & (r[:, None] // CH == r[None, :] // CH)
    put("glamax", np.where(ok, BIG, 0))
    put("glamin", np.where(ok, -BIG, 0))
    s = np.arange(NSAMP)
    ok = (s[:, None] <= s[None, :]) & (s[:, None] // TS == s[None, :] // TS)
    put("smpmax", np.where(ok, BIG, 0))
    put("smpmin", np.where(ok, -BIG, 0))
    scan = (np.arange(CHUNKS[0][1]) % CH != 0).astype(np.float32)
    put("scan", np.tile(scan, (P, 1)))
    put("scan_last", np.tile(np.concatenate([scan[:LASTP], s % TS != 0]), (P, 1)))
    put("bdones", (r[:, None] // HD == r[None, :] // HD).astype(np.float32))
    put("rowmask", (s[:, None] // TS == np.arange(NB)[None, :]).astype(np.float32))
    put("newmask", np.where(np.arange(TS)[None, :] <= (s % TS)[:, None], 0, -BIG))
    return c


def upto(i, per, k, base=0):
    return i * per + (base + max(k, 0) + 1)


def opened(eng, *sems):
    for s in sems:
        eng.sem_inc(s, 1)


def sigmoid_act(act, wait, inc, z, g):
    inc(act.activation(g, z, ACT.Abs), "g_abs")
    wait("g_abs")
    inc(act.activation(g, g, ACT.Exp, scale=-1.0), "g_exp")
    wait("g_exp")
    inc(act.activation(g, g, ACT.Ln, bias=1.0), "g_ln")
    wait("g_y")
    inc(act.activation(g, g, ACT.Exp), "g_sig")


def sigmoid_dve(dve, wait, inc, z, g):
    wait("g_ln")
    inc(dve.scalar_tensor_tensor(out=g, in0=z, scalar=0.0, in1=g, op0=ALU.min, op1=ALU.subtract), "g_y")


def fox_gla_step(nc, ins, outs, scratch):
    top = ExitStack()
    with top:
        def sem(name):
            return nc.alloc_semaphore(name=name)

        def sb(ctx, name, shape, dt=F32):
            return ctx.enter_context(nc.sbuf_tensor(name, shape, dt))

        psum = top.enter_context(nc.psum_tensor("psum", [P, 8 * 512], F32))
        bank = [psum[:, n * 512:(n + 1) * 512] for n in range(8)]

        con = sb(top, "con", [P, NCONST])
        vec = sb(top, "vec", [P, NVEC])

        def cc(name, rows=P):
            o, w = CONST_W[name]
            return con[0:rows, o:o + w]

        def vv(name, rows=P, col=0, n=1):
            o, _ = VEC_W[name]
            return vec[0:rows, o + col:o + col + n]

        epsb = sb(top, "epsb", [P, 1])
        gq8 = sb(top, "gq8", [P, 1])
        h_hi = sb(top, "h_hi", [P, KT_, NT], F32R)
        h_lo = sb(top, "h_lo", [P, KT_, NT], F32R)
        w_raw = [sb(top, f"w_raw{s}", [P, KT_, P]) for s in range(2)]
        w_hi = sb(top, "w_hi", [P, 2, KT_, P], F32R)
        w_lo = sb(top, "w_lo", [P, 2, KT_, P], F32R)
        os_fm = sb(top, "os_fm", [P, NHP, NSAMP])
        decode_ctx = top.enter_context(ExitStack())
        q_s = sb(decode_ctx, "q_s", [P, NHP, NSAMP])
        k_s_hi = sb(decode_ctx, "k_s_hi", [P, NHP, NSAMP], F32R)
        k_s_lo = sb(decode_ctx, "k_s_lo", [P, NHP, NSAMP], F32R)
        glr = sb(decode_ctx, "glr", [RANK, NT])
        newb = sb(decode_ctx, "newb", [NSAMP, NSAMP])

        stream = WeightStream(sem, ins["w_tiles"], w_raw, w_hi, w_lo, h_hi, h_lo, bank)
        with nc.cleanup_on_exit():
            build_inputs(nc, ins, outs, scratch, sem, sb, bank, con, vec, cc, vv, epsb, gq8, h_hi, h_lo, glr, stream)
        with nc.cleanup_on_exit():
            build_fox(nc, ins, outs, scratch, sem, sb, psum, bank, cc, vv, epsb, gq8, stream, os_fm, q_s, k_s_hi,
                      k_s_lo, newb)
        with nc.cleanup_on_exit():
            build_gla(nc, ins, outs, scratch, sem, sb, psum, bank, cc, vv, epsb, stream, os_fm, q_s, k_s_hi, k_s_lo,
                      newb, glr)
        decode_ctx.close()
        with nc.cleanup_on_exit():
            build_merge(nc, ins, outs, scratch, sem, sb, bank, stream, os_fm)


class WeightStream:

    def __init__(self, sem, dram, raw, hi, lo, h_hi, h_lo, bank):
        self.dram, self.raw, self.hi, self.lo = dram, raw, hi, lo
        self.h_hi, self.h_lo, self.bank = h_hi, h_lo, bank
        self.loaded = [sem(f"w_loaded{s}") for s in range(2)]
        self.const_in = sem("const_in")
        self.passed = sem("passed")
        self.hi_set, self.lo_set = sem("w_hi_set"), sem("w_lo_set")
        self.projected = sem("w_projected")
        self.z_read = sem("z_read")

    def phase(self, base, per, ring):
        self.base, self.per, self.ring = base, per, ring

    def pass_waits(self, eng):
        eng.sem_inc(self.passed, 1)

    def open_act(self, act):
        opened(act, self.hi_set)

    def open_dve(self, dve):
        opened(dve, self.lo_set, self.z_read)

    def open_pe(self, pe):
        opened(pe, self.projected)

    def load_first(self, sp, g):
        sp.dma_start(self.raw[g][:], self.dram[g]).then_inc(self.loaded[g], 16)

    def split_hi_first(self, act):
        act.wait_ge(self.loaded[0], 16)
        act.activation(self.hi[:, 0], self.raw[0][:], ACT.Copy).then_inc(self.hi_set, 1)

    def split_lo_first(self, dve):
        dve.wait_ge(self.hi_set, 2)
        dve.tensor_tensor(self.lo[:, 0], self.raw[0][:], self.hi[:, 0].bitcast(F32),
                          ALU.subtract).then_inc(self.lo_set, 1)

    def load(self, sp, i, n):
        sp.wait_ge(self.lo_set, upto(i, self.per, n + 1, self.base))
        sp.dma_start(self.raw[n % 2][:], self.dram[ds(i * self.per + (self.base + n + 2), 1)]
                     .rearrange("o p k c -> (o p) k c")).then_inc(self.loaded[n % 2], 16)

    def split_hi(self, act, i, n):
        s = (n + 1) % 2
        act.wait_ge(self.loaded[s], i * (self.per * 8) + 16 * ((self.base + n + 1) // 2 + 1))
        act.wait_ge(self.projected, i * (3 * self.per) + 3 * (self.base + n) + 1)
        act.activation(self.hi[:, s], self.raw[s][:], ACT.Copy).then_inc(self.hi_set, 1)

    def split_lo(self, dve, i, n):
        s = (n + 1) % 2
        dve.wait_ge(self.hi_set, upto(i, self.per, n + 2, self.base))
        dve.tensor_tensor(self.lo[:, s], self.raw[s][:], self.hi[:, s].bitcast(F32),
                          ALU.subtract).then_inc(self.lo_set, 1)

    def chunk(self, i, n, c):
        return upto(i, 3 * self.per, 3 * n + c + 1, 3 * self.base)

    def bank_of(self, n, c):
        return self.bank[self.ring[(3 * n + c) % len(self.ring)]][:, 0:CHUNKS[c][1]]

    def project(self, pe, i, n, c, ks=range(KT_)):
        t0, w = CHUNKS[c]
        s = n % 2
        if ks[0] == 0:
            pe.wait_ge(self.lo_set, upto(i, self.per, n + 1, self.base))
            pe.wait_ge(self.z_read, i * (3 * self.per) + 3 * self.base + max(3 * n + c + 1 - len(self.ring), 0) + 1)
        out = self.bank_of(n, c)
        for k in ks:
            for a, (wt, h) in enumerate(((self.hi, self.h_hi), (self.hi, self.h_lo), (self.lo, self.h_hi))):
                m = pe.matmul(out, wt[:, s, k, :], h[:, k, t0:t0 + w], start=(k == 0 and a == 0),
                              stop=(k == KT_ - 1 and a == 2))
        if ks[-1] == KT_ - 1:
            m.then_inc(self.projected, 1)


def build_inputs(nc, ins, outs, scratch, sem, sb, bank, con, vec, cc, vv, epsb, gq8, h_hi, h_lo, glr, stream):
    with ExitStack() as ctx:
        x_in = sb(ctx, "x_in", [P, TT + 1, D])
        hn = [sb(ctx, f"hn{s}", [P, D]) for s in range(2)]
        junk = sb(ctx, "x_junk", [P, D])
        hg = [sb(ctx, f"hg{s}", [P, 4, P]) for s in range(2)]
        stat = sb(ctx, "x_stat", [P, 2, 4])
        w_gate = sb(ctx, "w_gate", [P, KT_, 48])
        w_gate_hi = sb(ctx, "w_gate_hi", [P, KT_, 48], F32R)
        w_gate_lo = sb(ctx, "w_gate_lo", [P, KT_, 48], F32R)
        ffx = sb(ctx, "ffx", [H, NT])
        ffa = sb(ctx, "ffa", [H, NT])
        logf = sb(ctx, "logf", [H, NT])
        ones = sb(ctx, "ones_row", [H, SEQ])
        cum = sb(ctx, "cum", [H, NT])
        ncum = sb(ctx, "ncum", [H, SEQ])
        lft = sb(ctx, "logf_tok", [P, TT + 1, H])

        x_loaded = [sem(f"x_loaded{s}") for s in range(2)]
        const_in = stream.const_in
        eps_set, sq_sum, ms_ln, rms_inv = sem("eps_set"), sem("sq_sum"), sem("ms_ln"), sem("rms_inv")
        x_scaled, x_turned, x_gained, h_hi_set, h_lo_set = (sem(n) for n in
            ("x_scaled", "x_turned", "x_gained", "h_hi_set", "h_lo_set"))
        wg_zero, wg_in, wg_hi, wg_lo = sem("wg_zero"), sem("wg_in"), sem("wg_hi"), sem("wg_lo")
        gate_mm, ff_x, ff_ab, ff_exp, ff_ln, glr_set = (sem(n) for n in
            ("gate_mm", "ff_x", "ff_ab", "ff_exp", "ff_ln", "glr_set"))
        logf_set, cum_set, lf_turned, lf_tok, a_stored = (sem(n) for n in
            ("logf_set", "cum_set", "lf_turned", "lf_tok", "a_stored"))

        xp = ins["x_prompt"].rearrange("a l d -> (a l) d")
        xs = ins["x_sample"].rearrange("b l d -> (b l) d")
        def tile_of(i, s):
            last = isinstance(i, int) and i == TT // 2
            return i * 2 + s, i, s, NSAMP if last else P, i * (2 * P) + s * P

        def tiles(eng):
            with eng.Fori(0, TT // 2 - 1) as i:
                for s in range(2):
                    yield tile_of(i, s)
            for s in range(2):
                yield tile_of(TT // 2 - 1, s)
            yield tile_of(TT // 2, 0)

        def x_tile(t, n):
            return x_in[0:n, ds(t, 1), :].rearrange("p o d -> p (o d)")

        with nc.Block() as block:
            @block.sync
            def _(sp):
                sp.dma_start(con[:], ins["const"]).then_inc(const_in, 16)
                sp.dma_start(vec[:], ins["vecs"]).then_inc(const_in, 16)
                sp.wait_ge(wg_zero, 1)
                sp.dma_start(w_gate[:, :, 0:H], ins["w_ff"]).then_inc(wg_in, 16)
                sp.dma_start(w_gate[:, :, 32:32 + RANK], ins["w_lr"]).then_inc(wg_in, 16)
                for s in range(2):
                    sp.sem_inc(x_loaded[s], 16)
                for t, i, s, n, t0 in tiles(sp):
                    sp.wait_ge(x_loaded[s], i * 16 + 16)
                    src = xp[ds(t0, P), :] if n == P else xs
                    sp.dma_start(x_tile(t, n), src).then_inc(x_loaded[s], 16)
                for g in range(2):
                    stream.load_first(sp, g)
                sp.wait_ge(lf_tok, 2)
                sp.dma_start(outs["logf_p"].rearrange("(t p) h -> p t h", p=P), lft[:, 0:TT, :]).then_inc(a_stored, 16)
                sp.dma_start(outs["logf_s"], lft[0:NSAMP, TT, :]).then_inc(a_stored, 16)
                sp.wait_ge(cum_set, 3)
                sp.dma_start(scratch["cum"], cum[:, 0:SEQ]).then_inc(a_stored, 16)
                sp.dma_start(scratch["ncum"], ncum[:]).then_inc(a_stored, 16)
                sp.dma_start(scratch["cum_s"], cum[:, SEQ:NT]).then_inc(a_stored, 16)
                sp.dma_start(scratch["ones"], ones[0:1, :]).then_inc(a_stored, 16)
                sp.wait_ge(a_stored, 6 * 16)

            @block.gpsimd
            def _(pool):
                pool.memset(epsb[:], EPS).then_inc(eps_set, 1)
                pool.memset(w_gate[:], 0.0).then_inc(wg_zero, 1)
                pool.memset(ones[:], 1.0).then_inc(eps_set, 1)

            @block.scalar
            def _(act):
                act.preload_act_table_set("natural_log_exp_and_others")
                opened(act, sq_sum, ms_ln, rms_inv, h_hi_set)
                act.wait_ge(eps_set, 2)

                def stats(t, i, s, n, t0):
                    act.wait_ge(x_loaded[s], i * 16 + 32)
                    act.wait_ge(x_scaled, upto(i, 2, s - 1))
                    act.activation(junk[0:n, :], x_tile(t, n), ACT.Square,
                                   accum_out=stat[0:n, s, 0:1]).then_inc(sq_sum, 1)
                    act.wait_ge(sq_sum, upto(t, 1, 1))
                    act.activation(stat[0:n, s, 1:2], stat[0:n, s, 0:1], ACT.Ln, bias=epsb[0:n, :],
                                   scale=1.0 / D).then_inc(ms_ln, 1)
                    act.wait_ge(ms_ln, upto(t, 1, 1))
                    act.activation(stat[0:n, s, 2:3], stat[0:n, s, 1:2], ACT.Exp, scale=-0.5).then_inc(rms_inv, 1)

                stats(*tile_of(0, 0))
                for t, i, s, n, t0 in tiles(act):
                    if n == P:
                        stats(*tile_of(i + (s + 1) // 2, (s + 1) % 2))
                    for g in range(2):
                        act.wait_ge(x_gained, upto(t, 2, g + 1, 3))
                        act.activation(h_hi[:, 4 * g:4 * g + 4, ds(t0, n)], hg[g][:, :, 0:n], ACT.Copy).then_inc(h_hi_set, 1)
                stream.open_act(act)
                stream.split_hi_first(act)
                act.wait_ge(wg_in, 32)
                act.activation(w_gate_hi[:], w_gate[:], ACT.Copy).then_inc(wg_hi, 1)
                act.wait_ge(ff_ab, 1)
                act.activation(ffa[:], ffa[:], ACT.Exp, scale=-1.0).then_inc(ff_exp, 1)
                act.wait_ge(ff_exp, 1)
                act.activation(ffa[:], ffa[:], ACT.Ln, bias=1.0).then_inc(ff_ln, 1)

            @block.vector
            def _(dve):
                opened(dve, x_scaled, h_lo_set)
                dve.sem_inc(x_gained, 4)
                dve.wait_ge(const_in, 32)
                dve.tensor_scalar(gq8[:], vv("gq"), HD ** -0.5, None, ALU.mult)

                def scale(t, i, s, n, t0):
                    dve.wait_ge(rms_inv, upto(t, 1, 1))
                    dve.wait_ge(x_turned, upto(i, 4, 2 * (s - 1)))
                    dve.tensor_scalar(hn[s][0:n, :], x_tile(t, n), stat[0:n, s, 2:3], None, ALU.mult).then_inc(x_scaled, 1)

                scale(*tile_of(0, 0))
                for t, i, s, n, t0 in tiles(dve):
                    if n == P:
                        scale(*tile_of(i + (s + 1) // 2, (s + 1) % 2))
                    for g in range(2):
                        dve.wait_ge(x_turned, upto(t, 2, g + 1))
                        dve.wait_ge(h_lo_set, upto(t, 2, 0))
                        gain = vv("ln_g", P, 4 * g, 4).unsqueeze(2).to_broadcast([P, 4, n])
                        dve.tensor_tensor(hg[g][:, :, 0:n], bank[2 * s + g].rearrange("p (k t) -> p k t", k=4)[:, :, 0:n],
                                          gain, ALU.mult).then_inc(x_gained, 1)
                    for g in range(2):
                        dve.wait_ge(h_hi_set, upto(t, 2, g + 1))
                        dve.tensor_tensor(h_lo[:, 4 * g:4 * g + 4, ds(t0, n)], hg[g][:, :, 0:n],
                                          h_hi[:, 4 * g:4 * g + 4, ds(t0, n)].bitcast(F32), ALU.subtract).then_inc(h_lo_set, 1)
                stream.open_dve(dve)
                stream.split_lo_first(dve)
                dve.wait_ge(wg_hi, 1)
                dve.tensor_tensor(w_gate_lo[:], w_gate[:], w_gate_hi[:].bitcast(F32), ALU.subtract).then_inc(wg_lo, 1)
                for c, (t0, n) in enumerate(CHUNKS):
                    dve.wait_ge(gate_mm, c + 1)
                    dve.tensor_scalar(ffx[:, t0:t0 + n], bank[2 + c][0:H, 0:n], vv("b_f", H), None, ALU.add).then_inc(ff_x, 1)
                    dve.tensor_copy(glr[:, t0:t0 + n], bank[2 + c][32:32 + RANK, 0:n]).then_inc(glr_set, 1)
                dve.wait_ge(ff_x, 3)
                dve.scalar_tensor_tensor(out=ffa[:], in0=ffx[:], scalar=-1.0, in1=ffx[:], op0=ALU.mult, op1=ALU.max).then_inc(ff_ab, 1)
                dve.wait_ge(ff_ln, 1)
                dve.scalar_tensor_tensor(out=logf[:], in0=ffx[:], scalar=0.0, in1=ffa[:], op0=ALU.min,
                                         op1=ALU.subtract).then_inc(logf_set, 1)
                dve.wait_ge(logf_set, 1)
                dve.wait_ge(eps_set, 2)
                dve.tensor_tensor_scan(cum[:, 0:SEQ], ones[:], logf[:, 0:SEQ], 0.0, ALU.mult, ALU.add).then_inc(cum_set, 1)
                dve.tensor_tensor_scan(cum[:, SEQ:NT], cc("scan_last", H)[:, LASTP:], logf[:, SEQ:NT], 0.0, ALU.mult, ALU.add).then_inc(cum_set, 1)
                dve.wait_ge(cum_set, 2)
                dve.tensor_scalar(ncum[:], cum[:, 0:SEQ], -1.0, None, ALU.mult).then_inc(cum_set, 1)
                dve.wait_ge(lf_turned, 1)
                dve.tensor_copy(lft[:, 0:TT, :], bank[5][:, 0:TT * H].rearrange("p (t h) -> p t h", h=H)).then_inc(lf_tok, 1)
                dve.tensor_copy(lft[0:NSAMP, TT, :], bank[5][0:NSAMP, TT * H:(TT + 1) * H]).then_inc(lf_tok, 1)

            @block.tensor
            def _(pe):
                opened(pe, x_turned)
                stream.open_pe(pe)
                pe.wait_ge(const_in, 32)
                for t, i, s, n, t0 in tiles(pe):
                    pe.wait_ge(x_scaled, upto(t, 1, 1))
                    for g in range(2):
                        pe.wait_ge(x_gained, upto(t, 2, g))
                        for k in range(4):
                            kk = 4 * g + k
                            m = pe.transpose(bank[2 * s + g][:, k * P:k * P + n], hn[s][0:n, kk * P:(kk + 1) * P], cc("ident", n)[:, 0:n])
                        m.then_inc(x_turned, 1)
                pe.wait_ge(h_lo_set, upto(TT + 1, 2, 0))
                pe.wait_ge(wg_lo, 1)
                for c, (t0, n) in enumerate(CHUNKS):
                    for k in range(KT_):
                        for a, (w, h) in enumerate(((w_gate_hi, h_hi), (w_gate_hi, h_lo), (w_gate_lo, h_hi))):
                            m = pe.matmul(bank[2 + c][0:48, 0:n], w[:, k, :], h[:, k, t0:t0 + n],
                                          start=(k == 0 and a == 0), stop=(k == KT_ - 1 and a == 2))
                    m.then_inc(gate_mm, 1)
                pe.wait_ge(logf_set, 1)
                for t in range(TT + 1):
                    n = P if t < TT else NSAMP
                    m = pe.transpose(bank[5][0:n, t * H:(t + 1) * H], logf[:, t * P:t * P + n], cc("ident", H)[:, 0:H])
                m.then_inc(lf_turned, 1)


def build_fox(nc, ins, outs, scratch, sem, sb, psum, bank, cc, vv, epsb, gq8, stream, os_fm, q_s, k_s_hi, k_s_lo, newb):
    V, K, Q, G = range(4)
    U = 2 * TT
    PG = NPG // NHP
    with ExitStack() as ctx:
        ofox = sb(ctx, "ofox", [P, SEQ])
        v_fm = sb(ctx, "v_fm", [P, NT])
        v_tok = sb(ctx, "v_tok", [P, TT + 1, P])
        k_tok = sb(ctx, "k_tok", [P, TT + 1, P])
        ks_fm = sb(ctx, "ks_fm", [P, NSAMP])
        q_aug = sb(ctx, "q_aug", [P, 2, SEQ])
        k_aug = sb(ctx, "k_aug", [P, 2, SEQ])
        sq = sb(ctx, "sq", [P, 2, 384])
        inv = sb(ctx, "inv", [P, 2, 384])
        eg = sb(ctx, "eg", [P, 384])
        prob = [sb(ctx, f"prob{s}", [P, SEQ]) for s in range(2)]
        prob_t = [sb(ctx, f"prob_t{s}", [P, TT, P]) for s in range(2)]
        nmax = sb(ctx, "nmax", [P, 2])
        den = sb(ctx, "den", [P, 2])
        rden = sb(ctx, "rden", [P, 2])
        o_tok = sb(ctx, "o_tok", [P, 2, P])
        lfk = sb(ctx, "lfk", [P, PG, NB * H])
        lfc = sb(ctx, "lfc", [NB * H, PAST])
        total = sb(ctx, "total", [NB * H, 1])
        one = sb(ctx, "one", [P, 1])
        pages = sb(ctx, "pages", [1, NB * NPG], I32)

        names = ("v_turned v_tok_set k_turned k_tok_set squared norm_mm norm_ln norm_inv k_aug_set q_aug_set ks_set "
                 "ks_hi ks_lo g_abs g_exp g_ln g_y g_sig s_mm s_masked max_set exp_set p_turned pt_a pt_b pv_mm rden_set "
                 "o_set o_turned o_gated lf_turned2 lf_copied").split()
        S = {n: sem(n) for n in names}
        aug_zero, aug_in, aug_one, kv_stored, pg_in, lf_in = (sem(n) for n in ("aug_zero", "aug_in", "aug_one", "kv_stored", "pg_in", "lf_in"))
        one_set, past_cum, past_bias, fin_in, newb_set, b_stored, of_stored = (sem(n) for n in
            ("one_set", "past_cum", "past_bias", "fin_in", "newb_set", "b_stored", "of_stored"))
        stream.phase(0, 4, (0, 1, 6))
        kp = outs["k_p"].rearrange("a b (t p) h d -> p (a b t) (h d)", p=P)
        vp = outs["v_p"].rearrange("a b (t p) h d -> p (a b t) (h d)", p=P)
        ks = outs["k_s"].rearrange("a b t h d -> (a b t) (h d)")
        vs = outs["v_s"].rearrange("a b t h d -> (a b t) (h d)")

        def W(eng, name, i, per, k):
            eng.wait_ge(S[name], upto(i, per, k))

        def count(m, name):
            m.then_inc(S[name], 1)

        with nc.Block() as block:
            @block.sync
            def _(sp):
                sp.wait_ge(aug_zero, 2)
                for hh in range(2):
                    sp.dma_start(q_aug[HD:HD + 1, hh, :], scratch["ones"]).then_inc(aug_one, 16)
                    sp.dma_start(k_aug[HD + 1:HD + 2, hh, :], scratch["ones"]).then_inc(aug_one, 16)
                for t in range(TS):
                    sp.dma_start(newb[t:t + TS * (H - 1) + 1:TS, :], scratch["cum_s"]).then_inc(fin_in, 16)
                sp.sem_inc(kv_stored, 16)
                sp.sem_inc(of_stored, 16)
                with sp.Fori(0, NHP) as i:
                    W(sp, "s_mm", i, U, 0)
                    for hh in range(2):
                        sp.dma_start(q_aug[HD + 1:HD + 2, hh, :], scratch["cum"][ds(i * 2 + hh, 1), :]).then_inc(aug_in, 16)
                        sp.dma_start(k_aug[HD:HD + 1, hh, :], scratch["ncum"][ds(i * 2 + hh, 1), :]).then_inc(aug_in, 16)
                    for n in range(4):
                        stream.load(sp, i, n)
                        if n == Q:
                            W(sp, "v_tok_set", i, 3, 3)
                            sp.dma_start(vp[:, :, ds(i * P, P)], v_tok[:, 0:TT, :]).then_inc(kv_stored, 16)
                            sp.dma_start(vs[:, ds(i * P, P)], v_tok[0:NSAMP, TT, :]).then_inc(kv_stored, 16)
                    W(sp, "k_tok_set", i, 3, 3)
                    sp.dma_start(kp[:, :, ds(i * P, P)], k_tok[:, 0:TT, :]).then_inc(kv_stored, 16)
                    sp.dma_start(ks[:, ds(i * P, P)], k_tok[0:NSAMP, TT, :]).then_inc(kv_stored, 16)
                    W(sp, "o_gated", i, TT, TT)
                    sp.dma_start(scratch["ofox"][ds(i, 1)].rearrange("o p t -> (o p) t"), ofox[:]).then_inc(of_stored, 16)
                sp.wait_ge(of_stored, NHP * 16 + 16)
                sp.wait_ge(kv_stored, NHP * 64 + 16)
                sp.wait_ge(past_bias, 1)
                sp.dma_start(scratch["bias"], lfc[:]).then_inc(b_stored, 16)
                sp.wait_ge(b_stored, 16)

            @block.gpsimd
            def _(pool):
                pool.memset(one[:], 1.0).then_inc(one_set, 1)
                pool.dma_start(pages[:], ins["page_table"]).then_inc(pg_in, 16)
                pool.wait_ge(pg_in, 16)
                with pool.Fori(0, NHP) as i:
                    W(pool, "lf_turned2", i, 2, 0)
                    for g in range(PG):
                        for b in range(NB):
                            page = pool.value_load(pages[0:1, ds(i * PG + (b * NPG + g), 1)], min_val=0, max_val=NPHYS - 1)
                            pool.dma_start(lfk[:, g, b * H:(b + 1) * H], ins["cache_logf"][ds(page, 1)]
                                           .rearrange("o p h -> (o p) h")).then_inc(lf_in, 16)

            @block.scalar
            def _(act):
                opened(act, *(S[n] for n in ("v_tok_set", "k_tok_set", "squared", "norm_ln", "norm_inv", "ks_hi",
                                             "g_abs", "g_exp", "g_ln", "g_sig", "exp_set", "pt_b", "lf_copied")))

                def copy_out(i, tok, src, name, turned, b0):
                    for p in range(3):
                        if p == 0:
                            act.wait_ge(kv_stored, i * 64 + 16)
                        W(act, turned, i, 3, p + 1)
                        if p < 2:
                            act.activation(tok[:, 4 * p:4 * p + 4, :], src[b0 + p].rearrange("p (t c) -> p t c", t=4),
                                           ACT.Copy).then_inc(S[name], 1)
                        else:
                            act.activation(tok[0:NSAMP, TT, :], src[b0][0:NSAMP, 0:P], ACT.Copy).then_inc(S[name], 1)

                def exp(i, u):
                    n = (u // 2 + 1) * P
                    W(act, "max_set", i, U, u + 1)
                    W(act, "p_turned", i, U, u - 1)
                    W(act, "rden_set", i, U, u - 1)
                    act.activation(prob[u % 2][:, 0:n], psum[:, (2 + 2 * (u % 2)) * 512:][:, 0:n], ACT.Exp,
                                   bias=nmax[:, u % 2:u % 2 + 1], accum_out=den[:, u % 2:u % 2 + 1]).then_inc(S["exp_set"], 1)

                with act.Fori(0, NHP) as i:
                    for n in range(4):
                        stream.split_hi(act, i, n)
                        if n == K:
                            copy_out(i, v_tok, bank, "v_tok_set", "v_turned", 2)
                        for c, (t0, w) in enumerate(CHUNKS):
                            z = stream.bank_of(n, c)
                            if n == Q and c == 1:
                                copy_out(i, k_tok, bank, "k_tok_set", "k_turned", 4)
                            if n in (K, Q):
                                e = 3 * (n - K) + c
                                act.wait_ge(stream.projected, stream.chunk(i, n, c))
                                W(act, "norm_mm", i, 6, e - 1)
                                act.activation(sq[:, e % 2, 0:w], z, ACT.Square).then_inc(S["squared"], 1)
                                W(act, "norm_mm", i, 6, e + 1)
                                act.wait_ge(stream.z_read, i * 12 + 3 * n + c)
                                act.activation(inv[:, e % 2, 0:w], bank[7][:, 0:w], ACT.Ln, bias=epsb[:], scale=1.0 / HD)\
                                   .then_inc(S["norm_ln"], 1)
                                W(act, "norm_ln", i, 6, e + 1)
                                act.activation(inv[:, e % 2, 0:w], inv[:, e % 2, 0:w], ACT.Exp, scale=-0.5)\
                                   .then_inc(S["norm_inv"], 1)
                            if n == G:
                                act.wait_ge(stream.projected, stream.chunk(i, n, c))
                                act.wait_ge(stream.z_read, i * 12 + 3 * n + c + 1)
                                sigmoid_act(act, lambda name: W(act, name, i, 3, c + 1), count, z, eg[:, 0:w])
                        if n == K:
                            W(act, "ks_set", i, 1, 1)
                            act.activation(k_s_hi[:, ds(i, 1), :], ks_fm[:].unsqueeze(1), ACT.Copy).then_inc(S["ks_hi"], 1)
                    exp(i, 0)
                    for u in range(U):
                        if u + 1 < U:
                            exp(i, u + 1)
                        if u // 2 >= 4:
                            b = u - 8
                            W(act, "p_turned", i, U, u + 1)
                            W(act, "pv_mm", i, U, u - 1)
                            act.activation(prob_t[u % 2][:, 4:u // 2 + 1, :], bank[7][:, 0:(u // 2 - 3) * P]
                                           .rearrange("p (k q) -> p k q", q=P), ACT.Copy).then_inc(S["pt_b"], 1)
                    for p in range(2):
                        W(act, "lf_turned2", i, 2, p + 1)
                        act.activation(lfc[:, ds(i * (PG * P) + p * 512, 512)], bank[6 + p][0:NB * H, :], ACT.Copy)\
                           .then_inc(S["lf_copied"], 1)

            @block.vector
            def _(dve):
                opened(dve, *(S[n] for n in ("k_aug_set", "q_aug_set", "ks_set", "ks_lo", "g_y", "s_masked",
                                             "max_set", "pt_a", "rden_set", "o_set", "o_gated")))

                dve.memset(q_aug[HD:P], 0.0).then_inc(aug_zero, 1)
                dve.memset(k_aug[HD:P], 0.0).then_inc(aug_zero, 1)

                def head_rows(out, z, r, t0, gain, name, last):
                    w = min(CHUNKS[0][1], SEQ - t0)
                    for hh in range(2):
                        rows = slice(hh * HD, (hh + 1) * HD)
                        m = dve.scalar_tensor_tensor(out=out[0:HD, hh, t0:t0 + w], in0=z[rows, 0:w],
                                                     scalar=gain[rows], in1=r[rows, 0:w], op0=ALU.mult, op1=ALU.mult)
                        if hh == 0:
                            m.then_inc(S[name], 1)
                    if last:
                        m.then_inc(stream.z_read, 1)

                def smax(i, u):
                    qb, base = u // 2, (2 + 2 * (u % 2)) * 512
                    n = (qb + 1) * P
                    W(dve, "s_mm", i, U, u + 1)
                    diag = psum[:, base + qb * P:base + n]
                    dve.tensor_tensor(diag, diag, cc("causal"), ALU.add).then_inc(S["s_masked"], 1)
                    W(dve, "s_masked", i, U, u + 1)
                    W(dve, "exp_set", i, U, u - 1)
                    dve.tensor_reduce(nmax[:, u % 2:u % 2 + 1], psum[:, base:base + n], AX_X, ALU.max,
                                      negate=True).then_inc(S["max_set"], 1)

                def finish(i, u):
                    hh = u % 2
                    W(dve, "exp_set", i, U, u + 1)
                    dve.reciprocal(rden[:, hh:hh + 1], den[:, hh:hh + 1]).then_inc(S["rden_set"], 1)
                    W(dve, "rden_set", i, U, u + 1)
                    W(dve, "pv_mm", i, U, u + 1)
                    W(dve, "o_turned", i, TT, u // 2 - 1)
                    dve.tensor_scalar(o_tok[:, u // 2 % 2, hh * HD:(hh + 1) * HD], bank[hh][:, 0:HD],
                                      rden[:, hh:hh + 1], None, ALU.mult).then_inc(S["o_set"], 1)

                with dve.Fori(0, NHP) as i:
                    for n in range(4):
                        stream.split_lo(dve, i, n)
                        for c, (t0, w) in enumerate(CHUNKS):
                            z = stream.bank_of(n, c)
                            if n == V:
                                dve.wait_ge(stream.projected, stream.chunk(i, n, c))
                                W(dve, "v_turned", i, 3, 0)
                                dve.tensor_copy(v_fm[:, t0:t0 + w], z).then_inc(stream.z_read, 1)
                            if n in (K, Q):
                                e = 3 * (n - K) + c
                                r = inv[:, e % 2, 0:w]
                                W(dve, "norm_inv", i, 6, e + 1)
                                if c == 0:
                                    W(dve, "s_mm", i, U, 0)
                                if n == K:
                                    head_rows(k_aug, z, r, t0, vv("gk"), "k_aug_set", c < 2)
                                else:
                                    head_rows(q_aug, z, r, t0, gq8, "q_aug_set", c < 2)
                                if c == 2:
                                    z, r = z[:, LASTP:], r[:, LASTP:]
                                if c == 2 and n == K:
                                    W(dve, "k_turned", i, 3, 0)
                                    dve.scalar_tensor_tensor(out=ks_fm[:], in0=z, scalar=vv("gk"), in1=r, op0=ALU.mult,
                                                             op1=ALU.mult).then_inc(S["ks_set"], 1)
                                    W(dve, "ks_set", i, 1, 1)
                                    W(dve, "ks_hi", i, 1, 1)
                                    dve.tensor_tensor(k_s_lo[:, ds(i, 1), :], ks_fm[:].unsqueeze(1),
                                                      k_s_hi[:, ds(i, 1), :].bitcast(F32), ALU.subtract)\
                                       .then_inc(stream.z_read, 1)
                                elif c == 2:
                                    dve.scalar_tensor_tensor(out=q_s[:, ds(i, 1), :], in0=z.unsqueeze(1), scalar=gq8[:],
                                                             in1=r.unsqueeze(1), op0=ALU.mult, op1=ALU.mult)\
                                       .then_inc(stream.z_read, 1)
                            if n == G:
                                sigmoid_dve(dve, lambda name: W(dve, name, i, 3, c + 1), count, z, eg[:, 0:w])
                                W(dve, "g_sig", i, 3, c + 1)
                                if c == 0:
                                    dve.wait_ge(of_stored, i * 16 + 16)
                                if c == 2:
                                    dve.tensor_tensor(os_fm[:, ds(i, 1), :], z[:, LASTP:].unsqueeze(1),
                                                      eg[:, LASTP:w].unsqueeze(1), ALU.mult)
                                w = min(w, SEQ - t0)
                                dve.tensor_tensor(ofox[:, t0:t0 + w], z[:, 0:w], eg[:, 0:w], ALU.mult)\
                                   .then_inc(stream.z_read, 1)
                    smax(i, 0)
                    for u in range(U + 2):
                        if u + 1 < U:
                            smax(i, u + 1)
                        if u < U:
                            k = min(u // 2 + 1, 4)
                            W(dve, "p_turned", i, U, u + 1)
                            W(dve, "pv_mm", i, U, u - 1)
                            dve.tensor_copy(prob_t[u % 2][:, 0:k, :], bank[6][:, 0:k * P].rearrange("p (k q) -> p k q", q=P))\
                               .then_inc(S["pt_a"], 1)
                        if 1 <= u <= U:
                            finish(i, u - 1)
                        if u >= 2 and u % 2 == 1:
                            qb = (u - 2) // 2
                            W(dve, "o_turned", i, TT, qb + 1)
                            o = ofox[:, qb * P:(qb + 1) * P]
                            dve.tensor_tensor(o, bank[1][:, P:2 * P], o, ALU.mult).then_inc(S["o_gated"], 1)
                dve.wait_ge(one_set, 1)
                dve.wait_ge(S["lf_copied"], upto(NHP, 2, 0))
                dve.tensor_tensor_scan(lfc[:], one[0:NB * H, :].to_broadcast([NB * H, PAST]), lfc[:], 0.0, ALU.mult,
                                       ALU.add).then_inc(past_cum, 1)
                dve.wait_ge(past_cum, 1)
                dve.tensor_copy(total[:], lfc[:, PAST - 1:PAST]).then_inc(past_cum, 1)
                dve.wait_ge(past_cum, 2)
                dve.tensor_scalar(lfc[:], lfc[:], -1.0, total[:], ALU.mult, ALU.add).then_inc(past_bias, 1)
                dve.wait_ge(fin_in, 16 * TS)
                nb = newb[:].rearrange("r (b k) -> r b k", b=NB)
                dve.tensor_tensor(nb, cc("newmask", NSAMP).unsqueeze(1).to_broadcast([NSAMP, NB, TS]), nb,
                                  ALU.subtract).then_inc(newb_set, 1)

            @block.tensor
            def _(pe):
                opened(pe, *(S[n] for n in ("v_turned", "k_turned", "norm_mm", "s_mm", "p_turned", "pv_mm", "o_turned",
                                            "lf_turned2")))

                def turn_kv(i, src, name, done, b0):
                    for p in range(3):
                        W(pe, done, i, 3, p - 1 if p == 2 else 0)
                        stream.pass_waits(pe)
                        for t in (range(4 * p, 4 * p + 4) if p < 2 else [TT]):
                            out = bank[b0 + p % 2]
                            for o, a, ident in src(t):
                                n = P if t < TT else NSAMP
                                m = pe.transpose(out[0:n, (t % 4) * P + o:(t % 4) * P + o + ident.shape[1]], a, ident)
                        m.then_inc(S[name], 1)

                def scores(i, u):
                    qb, hh = u // 2, u % 2
                    W(pe, "exp_set", i, U, u - 1)
                    for c in range(0, qb + 1, 4):
                        n = min(4, qb + 1 - c) * P
                        b = 2 + 2 * hh + c // 4
                        m = pe.matmul(bank[b][:, 0:n], q_aug[:, hh, qb * P:(qb + 1) * P], k_aug[:, hh, c * P:c * P + n],
                                      start=True, stop=True)
                    m.then_inc(S["s_mm"], 1)

                def norm_sum(i, e):
                    w = CHUNKS[e % 3][1]
                    W(pe, "squared", i, 6, e + 1)
                    W(pe, "norm_ln", i, 6, e)
                    pe.matmul(bank[7][:, 0:w], cc("bdones"), sq[:, e % 2, 0:w], start=True, stop=True).then_inc(S["norm_mm"], 1)

                with pe.Fori(0, NHP) as i:
                    for n in range(4):
                        for c in range(3):
                            if n == V and c == 2:
                                W(pe, "lf_copied", i, 2, 0)
                            stream.project(pe, i, n, c)
                            if n == G and c == 0:
                                norm_sum(i, 5)
                            e = 3 * (n - K) + c - 1
                            if n in (K, Q) and e >= 0:
                                norm_sum(i, e)
                            if n == K and c == 0:
                                pe.wait_ge(stream.z_read, stream.chunk(i, V, 2))
                                W(pe, "exp_set", i, U, 0)
                                turn_kv(i, lambda t: [(0, v_fm[:, t * P:min((t + 1) * P, NT)], cc("ident"))],
                                        "v_turned", "v_tok_set", 2)
                            if n == Q and c == 1:
                                pe.wait_ge(stream.z_read, stream.chunk(i, K, 2))
                                turn_kv(i, lambda t: [(hh * HD, k_aug[0:HD, hh, t * P:(t + 1) * P], cc("ident", HD)[:, 0:HD])
                                                      for hh in range(2)] if t < TT else [(0, ks_fm[:], cc("ident"))],
                                        "k_turned", "k_tok_set", 4)
                    pe.wait_ge(stream.z_read, stream.chunk(i, Q, 2))
                    pe.wait_ge(aug_one, 64)
                    pe.wait_ge(aug_in, i * 64 + 64)
                    W(pe, "v_tok_set", i, 3, 3)
                    W(pe, "k_tok_set", i, 3, 3)
                    scores(i, 0)
                    for u in range(U + 2):
                        if u + 1 < U:
                            scores(i, u + 1)
                        if u < U:
                            W(pe, "exp_set", i, U, u + 1)
                            if u == 0:
                                pe.wait_ge(stream.z_read, stream.chunk(i, G, 2))
                            W(pe, "pt_a", i, U, u)
                            for k in range(u // 2 + 1):
                                if k == 4:
                                    W(pe, "pt_b", i, U - 8, u - 8)
                                m = pe.transpose(bank[6 + k // 4][:, (k % 4) * P:(k % 4 + 1) * P],
                                                 prob[u % 2][:, k * P:(k + 1) * P], cc("ident"))
                            m.then_inc(S["p_turned"], 1)
                        if 1 <= u <= U:
                            v = u - 1
                            W(pe, "pt_a", i, U, v + 1)
                            if v // 2 >= 4:
                                W(pe, "pt_b", i, U - 8, v - 7)
                            W(pe, "o_set", i, U, v - 1)
                            if v == 0:
                                pe.wait_ge(stream.z_read, stream.chunk(i, G, 2))
                            if v % 2:
                                W(pe, "o_gated", i, TT, v // 2)
                            for k in range(v // 2 + 1):
                                m = pe.matmul(bank[v % 2][:, 0:HD], prob_t[v % 2][:, k, :],
                                              v_tok[:, k, (v % 2) * HD:(v % 2 + 1) * HD], start=(k == 0), stop=(k == v // 2))
                            m.then_inc(S["pv_mm"], 1)
                        if u >= 2 and u % 2 == 1:
                            qb = (u - 2) // 2
                            W(pe, "o_set", i, U, 2 * qb + 2)
                            pe.transpose(bank[1][:, P:2 * P], o_tok[:, qb % 2, :], cc("ident")).then_inc(S["o_turned"], 1)
                    for p in range(2):
                        pe.wait_ge(lf_in, i * (PG * NB * 16) + PG * NB * 16)
                        W(pe, ("pt_a", "pt_b")[p], i, (U, U - 8)[p], (U, U - 8)[p])
                        stream.pass_waits(pe)
                        for g in range(4):
                            m = pe.transpose(bank[6 + p][0:NB * H, g * P:(g + 1) * P], lfk[:, 4 * p + g, :], cc("ident"))
                        m.then_inc(S["lf_turned2"], 1)
                    W(pe, "o_gated", i, TT, TT)


PARTS = 4


def schedule():
    V0, V1, Q, K, G0, G1 = range(6)
    cost = {"z": 0.95, "decay": 1.2, "vturn": 0.6, "kturn": 0.6, "att": 1.8, "o": 1.8, "og": 1.8, "satt": 1.8, "sstate": 3.0,
            "so": 1.5, "sog": 1.5}
    after = {(V1, 0, p + 1): [("vturn", 0, p)] for p in range(3)}
    after |= {(Q, 0, p + 1): [("vturn", 1, p)] for p in range(3)}
    after |= {(G0, 0, p + 1): [("kturn", p)] for p in range(3)}
    after[Q, 0, 3] = [("vturn", 1, 2), ("dec_neg",)]
    after[Q, 1, 1] = [("dec_diff",)]
    after[Q, 1, 3] = [("dec_end",)]
    other = [("start",)] + [("decay", c) for c in range(3)] + [("dec_last",)]
    evac = None
    for n in range(6):
        for c in range(3):
            for part in range(PARTS):
                other.append(("z", n, c, part))
                if part == 0 and evac:
                    other.append(evac)
                other += after.get((n, c, part), [])
            evac = ("evac", n, c)
    other.append(evac)
    gla = [x for t in range(TT) for x in (("att", t), ("o", t), ("og", t))]
    gla += [("satt",)] + [("sstate", r) for r in range(NB // 2)] + [("so",), ("sog",)]
    at = other.index(("evac", G1, 0)) + 1
    tail, other = other[at:], other[:at]
    while gla or tail:
        other += gla[:2]
        gla = gla[2:]
        if tail:
            other.append(tail.pop(0))
            while tail and tail[0][0] == "evac":
                other.append(tail.pop(0))
    decode = []
    for q in range(2):
        decode.append((("prep", q), 0))
        for p in range(NPG + 2):
            decode.append((("k", q, p), 1))
            decode += [((name, *a), 0) for at, name, a in ((1, "gate", (q - 1,)), (6, "vn_load", (q,)))
                       if at == p and a[0] >= 0]
        decode += [(("soft", q), 3), (("exp", q), 3)] + ([(("qbd", 1), 0)] if q == 0 else [])
        for g in range(NPG // 2 + 1):
            decode += [(("v", q, g), 1.2)] + [((name, q), 0) for at, name in ((2, "sum"), (8, "pn"), (10, "pnv")) if at == g]
        decode.append((("out", q), 2))
    decode.append((("gate", 1), 2))
    total = sum(c for _, c in decode)
    work = sum(cost.get(x[0], 0) for x in other)
    steps, done, placed = [], 0.0, 0.0
    for step, share in decode:
        steps.append(step)
        done += share * work / total
        while other and placed + cost.get(other[0][0], 0) <= done + 0.3:
            placed += cost.get(other[0][0], 0)
            steps.append(other.pop(0))
    return steps + other + [("end",)]


def build_gla(nc, ins, outs, scratch, sem, sb, psum, bank, cc, vv, epsb, stream, os_fm, q_s, k_s_hi, k_s_lo, newb, glr):
    V0, V1, Q, K, G0, G1 = range(6)
    GTS = TT + 1
    with ExitStack() as ctx:
        wa_all = sb(ctx, "wa_all", [RANK, GH, DK])
        wa = sb(ctx, "wa", [RANK, DK])
        ba = sb(ctx, "ba", [P, 1])
        t1 = sb(ctx, "t1", [P, 384])
        kdec = sb(ctx, "kdec", [P, NT])
        q_in = sb(ctx, "q_in", [P, NT])
        k_in = sb(ctx, "k_in", [P, NT])
        v_fm = k_in
        b_last = sb(ctx, "b_last", [P, SEQ // CH + NB])
        e_last = sb(ctx, "e_last", [P, SEQ // CH + NB])
        v_tok = sb(ctx, "gv_tok", [P, GTS, DV])
        k_tok = sb(ctx, "gk_tok", [P, GTS, DK])
        gate = sb(ctx, "gate", [P, 2, NT])
        state = sb(ctx, "state", [P, 3, DV])
        att = sb(ctx, "att", [P, P])
        o_n = sb(ctx, "o_n", [P, DV])
        ost = sb(ctx, "ost", [P, 3])
        s0 = sb(ctx, "s0", [P, 4, DV])
        s1 = sb(ctx, "s1", [P, 2, DV])
        q_diag = sb(ctx, "q_diag", [P, NB, NSAMP])
        k_row = sb(ctx, "k_row", [NSAMP, 4, DK])
        page = [sb(ctx, f"page{r}", [P, FW]) for r in range(8)]
        kv_hi = sb(ctx, "kv_hi", [P, 4, FW], F32R)
        kv_lo = sb(ctx, "kv_lo", [P, 4, FW], F32R)
        q_bd = sb(ctx, "q_bd", [P, NHP, 2, NSAMP], F32R)
        sc = sb(ctx, "sc", [P, HALF + TS])
        p_t = sb(ctx, "p_t", [P, 2, 2, 2, NSAMP], F32R)
        pn_t = sb(ctx, "pn_t", [TS, NSAMP])
        smst = sb(ctx, "smst", [P, 8])
        u_lo = sb(ctx, "u_lo", [NSAMP, FW])
        vn_raw = u_lo[0:TS, :]
        pages = sb(ctx, "pages2", [1, NB * NPG + 8], I32)

        per = {}
        for names, n in (("dc_mm dc_abs dc_exp dc_ln dc_min dc_y dc_cum", 3), ("v_turned vt_set", 6), ("kd_turned kd_set", 3),
                         ("bl_set", 2), ("eb_set en_set el_set dd_set ed_set ba_set wa_set st_zero", 1), ("kin_set", 3),
                         ("g_abs g_exp g_ln g_y g_sig", 6), ("att_mm att_min att_set o_mm", GTS), ("u_mm u_half", TT), ("st_set", 2 * TT),
                         ("ss_set sl_set sr_set on_set ot_mm g1_set gated", GTS), ("qd_set", 1), ("kr_set", NB),
                         ("su_mm", NB // 2), ("s1_set", NB), ("kt_mm kt_hi_set kt_lo_set sc_mm s_add1 s_add", 2 * NPG),
                         ("new_mm n_add1 n_add", 2), ("qb_hi", 4), ("qb_lo", 4), ("qb_hi_a", 2), ("pad_set", 2),
                         ("mx1 mx2 mx3 mx4 exp2 dn1 dn2 dn3", 2), ("pt_mm pt_hi pt_lo", NPG), ("pn_mm pn_set", 2),
                         ("v_hi_set pv", 2 * NPG), ("v_even_lo v_odd_lo", NPG), ("pvn u_set od_set od_mm od_g", 2)):
            for n_ in names.split():
                per[n_] = n
        S = {n: sem("c_" + n) for n in per}
        s0_in = [sem(f"s0_in{r}") for r in range(2)]
        page_in = [sem(f"page_landed{r}") for r in range(8)]
        sc_in, vn_in, wa_in, pg_in, s1_out, st_out, og_out, zero_set, qbd_zero, pad_zero = (sem(n) for n in
            ("sc_in", "vn_in", "wa_in", "pg_in2", "s1_out", "st_out", "og_out", "zero_set", "qbd_zero", "pad_zero"))
        stream.phase(TT * 2, 6, (0, 1))
        steps = schedule()

        def W(eng, name, i, k):
            eng.wait_ge(S[name], upto(i, per[name], k))

        def inc(m, name):
            m.then_inc(S[name], 1)

        def run(eng, handlers, i):
            reg = eng.alloc_register("turn")
            mine = [st for st in steps if st[0] in handlers]
            for n, st in enumerate(mine):
                if n % 6 == 0:
                    eng.reg_mov(reg, i)
                    turn = eng.snap(reg, min_val=0, max_val=GH - 1)
                handlers[st[0]](turn, *st[1:])

        def v_lo_name(m):
            return ("v_even_lo", "v_odd_lo")[m % 2]

        def wait_page(eng, i, q, x):
            eng.wait_ge(page_in[x % 8], i * (16 * 16) + 16 * (q * 8 + x // 8 + 1))

        def wait_k_slot(eng, i, q, p):
            if p >= 4:
                W(eng, "sc_mm", i, q * NPG + p - 3)
            else:
                W(eng, "pv", i, (q - 1) * NPG + NPG - 3 + p if q else 0)

        def wait_v_slot(eng, i, q, m):
            if m >= 4:
                W(eng, "pv", i, q * NPG + m - 3)
            else:
                W(eng, "sc_mm", i, q * NPG + NPG - 3 + m)

        rows = [slice(0, HD), slice(HD, P)]

        with nc.Block() as block:
            @block.sync
            def _(sp):
                sp.dma_start(pages[:, 0:NB * NPG], ins["page_table"]).then_inc(pg_in, 16)
                sp.dma_start(wa_all[:], ins["w_a2"].rearrange("g r c -> r g c")).then_inc(wa_in, 16)
                sp.wait_ge(pg_in, 16)
                sp.wait_ge(pad_zero, 1)
                for s in (st_out, og_out, s1_out):
                    sp.sem_inc(s, 16)

                def load(i, q, x):
                    y, u = (x - 8, q) if x >= 8 else (x + 56, q - 1)
                    if y < 0 or u < 0:
                        pass
                    elif y < NPG:
                        W(sp, "kt_mm", i, u * NPG + y + 1)
                    else:
                        W(sp, v_lo_name(y), i, u * (NPG // 2) + (y - NPG) // 2 + 1)
                    m = x - NPG
                    p = x if x < NPG else m // 2 + (NPG // 2) * (m % 2)
                    src = sp.value_load(pages[0:1, ds(i * (2 * NPG) + (q * NPG + p), 1)], min_val=0, max_val=NPHYS - 1)
                    cache = ins["cache_k" if x < NPG else "cache_v"]
                    sp.dma_start(page[x % 8][:], cache[ds(src, 1)].rearrange("o p c -> (o p) c")).then_inc(page_in[x % 8], 16)

                def prep(i, q):
                    W(sp, "pt_mm", i, NPG // 2 * q)
                    for half in range(2):
                        for h in range(H):
                            src = scratch["bias"][ds(i * (2 * H) + (q * H + h), 1), half * HALF:(half + 1) * HALF]
                            sp.dma_start(sc[half * NSAMP + h * TS:half * NSAMP + (h + 1) * TS, 0:HALF],
                                         src.to_broadcast([TS, HALF])).then_inc(sc_in, 16)

                def vn_load(i, q):
                    W(sp, "od_mm", i, q)
                    sp.dma_start(vn_raw, outs["v_s"].rearrange("a b t h d -> (a b) t (h d)")[ds(i * 2 + q, 1)]
                                 .rearrange("o t c -> (o t) c")).then_inc(vn_in, 16)

                def kstep(i, q, p):
                    if p < NPG:
                        load(i, q, p + 8)

                def vstep(i, q, g):
                    for x in (NPG + 8 + 2 * g, NPG + 9 + 2 * g):
                        if x < 2 * NPG:
                            load(i, q, x)
                        elif x < 2 * NPG + 8:
                            load(i, q + 1, x - 2 * NPG)

                def z(i, n, c, part):
                    if c == 0 and part == 1:
                        stream.load(sp, i, n)

                def state_in(i, r):
                    W(sp, "s1_set", i, 2 * r - 2)
                    for j in range(2):
                        src = ins["state"][2 * r + j, ds(i, 1)].rearrange("o k v -> (o k) v")
                        sp.dma_start(s0[:, 2 * (r % 2) + j, :], src).then_inc(s0_in[r % 2], 16)

                def state_out(i, r):
                    W(sp, "s1_set", i, 2 * r + 2)
                    for j in range(2):
                        dst = outs["gla_s"][0, 2 * r + j, ds(i, 1)].rearrange("o k v -> (o k) v")
                        sp.dma_start(dst, s1[:, j, :]).then_inc(s1_out, 16)

                def att_step(i, t):
                    if t == TT - 1:
                        state_in(i, 0)
                        state_in(i, 1)

                def satt(i):
                    W(sp, "st_set", i, 2 * TT)
                    dst = outs["gla_p"][0, 0, ds(i, 1)].rearrange("o k v -> (o k) v")
                    sp.dma_start(dst, state[:, 2 * TT % 3, :]).then_inc(st_out, 16)

                def sstate(i, r):
                    if r + 1 < NB // 2 and r > 0:
                        state_in(i, r + 1)
                    state_out(i, r)

                def end(i):
                    W(sp, "gated", i, GTS)
                    sp.dma_start(scratch["ogla"][ds(i, 1)].rearrange("o p a t -> (o p) a t"), gate[:]).then_inc(og_out, 16)

                for x in range(8):
                    load(0, 0, x)
                with sp.Fori(0, GH) as i:
                    run(sp, {"prep": prep, "vn_load": vn_load, "k": kstep, "v": vstep, "z": z, "att": att_step, "satt": satt,
                             "sstate": sstate, "end": end}, i)
                for x in range(8):
                    sp.wait_ge(page_in[x], GH * (16 * 16) + 16)
                sp.wait_ge(st_out, GH * 16 + 16)
                sp.wait_ge(og_out, GH * 16 + 16)
                sp.wait_ge(s1_out, GH * NB * 16 + 16)

            @block.gpsimd
            def _(pool):
                opened(pool, S["v_even_lo"])
                pool.memset(q_diag[:], 0.0).then_inc(zero_set, 1)

                def low(i, q, m):
                    W(pool, "v_hi_set", i, q * NPG + m + 1)
                    inc(pool.tensor_tensor(kv_lo[:, m % 4, :], page[m % 8][:], kv_hi[:, m % 4, :].bitcast(F32),
                                           ALU.subtract), "v_even_lo")

                def kstep(i, q, p):
                    if p == NPG:
                        low(i, q, 0)

                def vstep(i, q, g):
                    if 2 * g + 2 < NPG:
                        low(i, q, 2 * g + 2)

                with pool.Fori(0, GH) as i:
                    run(pool, {"k": kstep, "v": vstep}, i)

            @block.scalar
            def _(act):
                opened(act, *(S[n] for n in ("dc_abs dc_exp dc_ln vt_set kd_set eb_set en_set el_set ed_set g_abs g_exp g_ln g_sig ss_set "
                                             "sl_set sr_set kt_hi_set qb_hi exp2 pt_hi pn_set v_hi_set u_set").split()))
                A = act.activation

                def qbd(i, q):
                    W(act, "new_mm", i, q)
                    act.wait_ge(qbd_zero, 1)
                    for half in range(2):
                        dst = q_bd[rows[half]].rearrange("p a b c -> p (a b c)")[:, half * TS:]
                        inc(A(diag(dst, 2 * NSAMP + 2 * TS, NHP), q_s[rows[half], :, ds(i * (2 * TS) + q * TS, TS)], ACT.Copy), "qb_hi")

                def v_high(i, q, m):
                    wait_page(act, i, q, NPG + m)
                    wait_v_slot(act, i, q, m)
                    inc(A(kv_hi[:, m % 4, :], page[m % 8][:], ACT.Copy), "v_hi_set")

                def kstep(i, q, p):
                    if p < NPG:
                        n = q * NPG + p
                        W(act, "kt_mm", i, n + 1)
                        wait_k_slot(act, i, q, p)
                        inc(A(kv_hi[:, p % 4, :], bank[3 + n % 2], ACT.Copy), "kt_hi_set")
                    else:
                        v_high(i, q, p - NPG)

                def exp(i, q):
                    W(act, "mx4", i, q + 1)
                    inc(A(sc[:], sc[:], ACT.Exp, bias=smst[:, 2:3], accum_out=smst[:, 4:5]), "exp2")

                def vstep(i, q, g):
                    if g < NPG // 2:
                        u = q * (NPG // 2) + g
                        W(act, "pt_mm", i, u + 1)
                        W(act, "pv", i, 2 * u - 2)
                        inc(A(p_t[:, u % 2, :, 0, :], bank[3 + u % 2][:, 0:P].rearrange("p (h r) -> p h r", h=2),
                              ACT.Copy), "pt_hi")
                        for m in (2 * g + 2, 2 * g + 3):
                            if m < NPG:
                                v_high(i, q, m)
                def pn(i, q):
                    W(act, "pn_mm", i, q + 1)
                    W(act, "pvn", i, q)
                    inc(A(pn_t[:], bank[5][0:TS, 0:NSAMP], ACT.Copy), "pn_set")

                def out(i, q):
                    W(act, "pv", i, NPG * (q + 1))
                    W(act, "pvn", i, q + 1)
                    W(act, "dn3", i, q + 1)
                    W(act, "od_mm", i, q)
                    inc(A(u_lo[:], bank[6][NSAMP:P, :], ACT.Identity, scale=smst[NSAMP:P, 6:7]), "u_set")

                def decay(i, c):
                    w = CHUNKS[c][1]
                    W(act, "dc_mm", i, c + 1)
                    W(act, "ba_set", i, 1)
                    W(act, "dc_y", i, c)
                    act.wait_ge(stream.z_read, upto(i, 18, 0, 3 * 16))
                    inc(A(t1[:, 0:w], bank[2][:, 0:w], ACT.Abs, bias=ba[:]), "dc_abs")
                    W(act, "dc_abs", i, c + 1)
                    inc(A(t1[:, 0:w], t1[:, 0:w], ACT.Exp, scale=-1.0), "dc_exp")
                    W(act, "dc_exp", i, c + 1)
                    inc(A(t1[:, 0:w], t1[:, 0:w], ACT.Ln, bias=1.0), "dc_ln")

                def dec_last(i):
                    W(act, "dc_cum", i, 3)
                    W(act, "o_mm", i, 0)
                    inc(A(q_in[:], kdec[:], ACT.Exp, scale=1.0 / TAU), "eb_set")
                    W(act, "bl_set", i, 2)
                    W(act, "st_set", i, 0)
                    W(act, "s1_set", i, 0)
                    inc(A(e_last[:], b_last[:], ACT.Exp, scale=1.0 / TAU), "el_set")

                def dec_neg(i):
                    W(act, "v_turned", i, 6)
                    inc(A(k_in[:], kdec[:], ACT.Exp, scale=-1.0 / TAU), "en_set")

                def dec_end(i):
                    W(act, "dd_set", i, 1)
                    inc(A(kdec[:], kdec[:], ACT.Exp, scale=1.0 / TAU), "ed_set")

                def turned(i, dst, half, p, name, mm, k):
                    W(act, mm, i, k + 1)
                    b = bank[(2, 7, 2)[p]]
                    if p < 2:
                        inc(A(dst[:, 4 * p:4 * p + 4, half * P:(half + 1) * P], b.rearrange("p (t c) -> p t c", t=4), ACT.Copy), name)
                    else:
                        inc(A(dst[0:NSAMP, TT, half * P:(half + 1) * P], b[0:NSAMP, 0:P], ACT.Copy), name)

                def vturn(i, n, p):
                    turned(i, v_tok, n, p, "vt_set", "v_turned", 3 * n + p)

                def kturn(i, p):
                    turned(i, k_tok, 0, p, "kd_set", "kd_turned", p)

                def z(i, n, c, part):
                    if c == 0 and part == 1:
                        stream.split_hi(act, i, n)

                def evac(i, n, c):
                    if n >= G0:
                        w = CHUNKS[c][1]
                        act.wait_ge(stream.projected, stream.chunk(i, n, c))
                        act.wait_ge(stream.z_read, i * 18 + 3 * 16 + 3 * n + c + 1)
                        sigmoid_act(act, lambda name: W(act, name, i, 3 * (n - G0) + c + 1), inc, stream.bank_of(n, c), t1[:, 0:w])

                def ostat(i, t, w):
                    W(act, "o_mm", i, t + 1)
                    W(act, "ot_mm", i, t)
                    inc(A(o_n[0:w], bank[7][0:w, P:P + DV], ACT.Square, accum_out=ost[0:w, 0:1]), "ss_set")
                    W(act, "ss_set", i, t + 1)
                    inc(A(ost[0:w, 1:2], ost[0:w, 0:1], ACT.Ln, bias=epsb[0:w], scale=1.0 / DV), "sl_set")
                    W(act, "sl_set", i, t + 1)
                    inc(A(ost[0:w, 2:3], ost[0:w, 1:2], ACT.Exp, scale=-0.5), "sr_set")

                with act.Fori(0, GH) as i:
                    run(act, {"prep": lambda i, q: None if q else qbd(i, q), "qbd": qbd, "pn": pn, "k": kstep, "exp": exp, "v": vstep,
                              "out": out, "decay": decay, "dec_last": dec_last, "dec_neg": dec_neg, "dec_end": dec_end, "vturn": vturn, "kturn": kturn, "z": z, "evac": evac,
                              "o": lambda i, t: ostat(i, t, P), "so": lambda i: ostat(i, TT, NSAMP)}, i)

            @block.vector
            def _(dve):
                opened(dve, *(S[n] for n in ("dc_min dc_y dc_cum bl_set dd_set ba_set wa_set st_zero kin_set g_y att_min "
                                             "att_set st_set on_set g1_set gated qd_set kr_set s1_set kt_lo_set v_odd_lo s_add1 s_add n_add1 n_add "
                                             "pad_set qb_lo mx1 mx2 mx3 mx4 dn1 dn2 dn3 pt_lo od_set od_g").split()))
                dve.memset(pages[:, NB * NPG:].bitcast(F32), 0.0).then_inc(pad_zero, 1)
                dve.memset(q_bd[:].bitcast(F32), 0.0).then_inc(qbd_zero, 1)
                dve.wait_ge(qbd_zero, 1)
                T = dve.tensor_tensor

                def prep(i, q):
                    W(dve, "exp2", i, q)
                    stream.pass_waits(dve)
                    inc(dve.memset(sc[NSAMP:P, HALF:HALF + TS], -BIG), "pad_set")
                    if q == 0:
                        qbd(i, q)

                def qbd(i, q):
                    W(dve, "new_mm", i, q)
                    W(dve, "qb_hi", i, 2 * q + 2)
                    for half in range(2):
                        flat = q_bd[rows[half]].rearrange("p a b c -> p (a b c)")
                        hi = diag(flat[:, half * TS:], 2 * NSAMP + 2 * TS, NHP)
                        lo = diag(flat[:, NSAMP + half * TS:], 2 * NSAMP + 2 * TS, NHP)
                        inc(T(lo, q_s[rows[half], :, ds(i * (2 * TS) + q * TS, TS)], hi.bitcast(F32), ALU.subtract), "qb_lo")

                def v_low(i, q, m):
                    W(dve, "v_hi_set", i, q * NPG + m + 1)
                    inc(T(kv_lo[:, m % 4, :], page[m % 8][:], kv_hi[:, m % 4, :].bitcast(F32), ALU.subtract), "v_odd_lo")

                def kstep(i, q, p):
                    if p < NPG:
                        n = q * NPG + p
                        W(dve, "kt_hi_set", i, n + 1)
                        inc(T(kv_lo[:, p % 4, :], bank[3 + n % 2], kv_hi[:, p % 4, :].bitcast(F32), ALU.subtract), "kt_lo_set")
                    if p == NPG + 1:
                        v_low(i, q, 1)
                    if p >= 2:
                        n = q * NPG + p - 2
                        half, col = (p - 2) // (NPG // 2), (p - 2) % (NPG // 2) * PAGE
                        dst = sc[rows[half], col:col + PAGE]
                        if p == 2:
                            dve.wait_ge(sc_in, i * 512 + 256 * (q + 1))
                        W(dve, "sc_mm", i, n + 1)
                        inc(T(dst, bank[5 + n % 2][0:NSAMP, 0:PAGE], dst, ALU.add), "s_add1")
                        W(dve, "s_add1", i, n + 1)
                        inc(T(dst, bank[5 + n % 2][NSAMP:P, 0:PAGE], dst, ALU.add), "s_add")

                def soft(i, q):
                    new = sc[0:NSAMP, HALF:HALF + TS]
                    W(dve, "new_mm", i, q + 1)
                    inc(T(new, bank[5][0:NSAMP, 0:TS], newb[:, ds(i * (2 * TS) + q * TS, TS)], ALU.add), "n_add1")
                    W(dve, "n_add1", i, q + 1)
                    inc(T(new, bank[5][NSAMP:P, 0:TS], new, ALU.add), "n_add")
                    W(dve, "n_add", i, q + 1)
                    W(dve, "s_add", i, NPG * (q + 1))
                    W(dve, "pad_set", i, q + 1)
                    inc(dve.tensor_reduce(smst[:, 0:1], sc[:], AX_X, ALU.max), "mx1")
                    W(dve, "mx1", i, q + 1)
                    inc(dve.tensor_copy(smst[0:NSAMP, 1:2], smst[NSAMP:P, 0:1]), "mx2")
                    W(dve, "mx2", i, q + 1)
                    inc(dve.tensor_scalar(smst[0:NSAMP, 2:3], smst[0:NSAMP, 0:1], smst[0:NSAMP, 1:2], -1.0, ALU.max, ALU.mult), "mx3")
                    W(dve, "mx3", i, q + 1)
                    inc(dve.tensor_copy(smst[NSAMP:P, 2:3], smst[0:NSAMP, 2:3]), "mx4")

                def total(i, q):
                    W(dve, "exp2", i, q + 1)
                    inc(dve.tensor_copy(smst[0:NSAMP, 5:6], smst[NSAMP:P, 4:5]), "dn1")
                    W(dve, "dn1", i, q + 1)
                    inc(T(smst[0:NSAMP, 7:8], smst[0:NSAMP, 4:5], smst[0:NSAMP, 5:6], ALU.add), "dn2")
                    W(dve, "dn2", i, q + 1)
                    dve.reciprocal(smst[0:NSAMP, 6:7], smst[0:NSAMP, 7:8])
                    inc(dve.reciprocal(smst[NSAMP:P, 6:7], smst[0:NSAMP, 7:8]), "dn3")

                def vstep(i, q, g):
                    if g < NPG // 2:
                        u = q * (NPG // 2) + g
                        W(dve, "pt_hi", i, u + 1)
                        inc(T(p_t[:, u % 2, :, 1, :], bank[3 + u % 2][:, 0:P].rearrange("p (h r) -> p h r", h=2),
                              p_t[:, u % 2, :, 0, :].bitcast(F32), ALU.subtract), "pt_lo")
                        if 2 * g + 3 < NPG:
                            v_low(i, q, 2 * g + 3)

                def out(i, q):
                    W(dve, "u_set", i, q + 1)
                    inc(dve.scalar_tensor_tensor(out=u_lo[:], in0=bank[6][0:NSAMP, :], scalar=smst[0:NSAMP, 6:7], in1=u_lo[:],
                                                 op0=ALU.mult, op1=ALU.add), "od_set")

                def gate_out(i, q):
                    W(dve, "od_mm", i, q + 1)
                    for half in range(2):
                        src = diag(bank[5][rows[half], half * TS:], NSAMP + 2 * TS, NHP)
                        dst = os_fm[rows[half], :, ds(i * (2 * TS) + q * TS, TS)]
                        m = T(dst, src, dst, ALU.mult)
                    inc(m, "od_g")

                def start(i):
                    W(dve, "dc_ln", i, 0)
                    W(dve, "o_mm", i, 0)
                    o, _ = VEC_W["b_a"]
                    inc(dve.tensor_copy(ba[:], vv("b_a", P, 0, GH)[:, ds(i, 1)]), "ba_set")
                    W(dve, "dc_mm", i, 0)
                    dve.wait_ge(wa_in, 16)
                    inc(dve.tensor_copy(wa[:].unsqueeze(1), wa_all[:, ds(i, 1), :]), "wa_set")
                    W(dve, "ba_set", i, 1)
                    inc(dve.memset(state[:, 0, :], 0.0), "st_zero")

                def decay(i, c):
                    t0, w = CHUNKS[c]
                    y = kdec[:, t0:t0 + w]
                    W(dve, "dc_abs", i, c + 1)
                    W(dve, "kd_turned", i, 0)
                    inc(dve.tensor_scalar(y, bank[2][:, 0:w], ba[:], 0.0, ALU.add, ALU.min), "dc_min")
                    W(dve, "dc_min", i, c + 1)
                    W(dve, "dc_ln", i, c + 1)
                    inc(T(y, y, t1[:, 0:w], ALU.subtract), "dc_y")
                    W(dve, "dc_y", i, c + 1)
                    inc(dve.tensor_tensor_scan(y, cc("scan" if c < 2 else "scan_last"), y, 0.0, ALU.mult, ALU.add), "dc_cum")

                main = kdec[:, 0:SEQ].rearrange("p (c t) -> p c t", t=CH)
                tail = kdec[:, SEQ:NT].rearrange("p (c t) -> p c t", t=TS)
                np_ = SEQ // CH

                def dec_last(i):
                    W(dve, "dc_cum", i, 3)
                    W(dve, "el_set", i, 0)
                    inc(dve.tensor_copy(b_last[:, 0:np_].unsqueeze(2), main[:, :, CH - 1:CH]), "bl_set")
                    inc(dve.tensor_copy(b_last[:, np_:].unsqueeze(2), tail[:, :, TS - 1:TS]), "bl_set")

                def dec_diff(i):
                    W(dve, "bl_set", i, 2)
                    W(dve, "eb_set", i, 1)
                    W(dve, "en_set", i, 1)
                    T(main, b_last[:, 0:np_].unsqueeze(2).to_broadcast([P, np_, CH]), main, ALU.subtract)
                    inc(T(tail, b_last[:, np_:].unsqueeze(2).to_broadcast([P, NB, TS]), tail, ALU.subtract), "dd_set")

                def z(i, n, c, part):
                    if c == 0 and part == 1:
                        stream.split_lo(dve, i, n)

                def evac(i, n, c):
                    t0, w = CHUNKS[c]
                    zb = stream.bank_of(n, c)
                    dve.wait_ge(stream.projected, stream.chunk(i, n, c))
                    if n in (V0, V1):
                        W(dve, "v_turned", i, 3 * n)
                        W(dve, "att_mm", i, 0)
                        dve.tensor_copy(v_fm[:, t0:t0 + w], zb).then_inc(stream.z_read, 1)
                    if n == Q:
                        W(dve, "eb_set", i, 1)
                        dve.scalar_tensor_tensor(out=q_in[:, t0:t0 + w], in0=zb, scalar=DK ** -0.5, in1=q_in[:, t0:t0 + w],
                                                 op0=ALU.mult, op1=ALU.mult).then_inc(stream.z_read, 1)
                    if n == K:
                        W(dve, "ed_set", i, 1)
                        inc(T(k_in[:, t0:t0 + w], zb, k_in[:, t0:t0 + w], ALU.mult), "kin_set")
                        T(kdec[:, t0:t0 + w], zb, kdec[:, t0:t0 + w], ALU.mult).then_inc(stream.z_read, 1)
                    if n >= G0:
                        e = 3 * (n - G0) + c
                        sigmoid_dve(dve, lambda name: W(dve, name, i, e + 1), inc, zb, t1[:, 0:w])
                        W(dve, "g_sig", i, e + 1)
                        dve.wait_ge(og_out, i * 16 + 16)
                        T(gate[:, n - G0, t0:t0 + w], zb, t1[:, 0:w], ALU.mult).then_inc(stream.z_read, 1)

                def att_mask(i, t, w, hi, lo):
                    W(dve, "att_mm", i, t + 1)
                    W(dve, "o_mm", i, t)
                    inc(T(att[0:w, 0:w], bank[7][0:w, 0:w], cc(hi, w), ALU.min), "att_min")
                    W(dve, "att_min", i, t + 1)
                    inc(T(att[0:w, 0:w], att[0:w, 0:w], cc(lo, w), ALU.max), "att_set")

                def att_step(i, t):
                    att_mask(i, t, P, "glamax", "glamin")
                    W(dve, "u_mm", i, t + 1)
                    if t == 0:
                        W(dve, "el_set", i, 1)
                        W(dve, "st_zero", i, 1)
                        dve.wait_ge(st_out, i * 16 + 16)
                    for j in range(2):
                        c = 2 * t + j
                        W(dve, "st_set", i, c)
                        inc(dve.scalar_tensor_tensor(out=state[:, (c + 1) % 3, :], in0=state[:, c % 3, :], scalar=e_last[:, c:c + 1],
                                                     in1=bank[2][:, j * DV:(j + 1) * DV], op0=ALU.mult, op1=ALU.add), "st_set")

                def o_norm(i, t, w):
                    W(dve, "sr_set", i, t + 1)
                    W(dve, "ot_mm", i, t)
                    inc(dve.tensor_scalar(o_n[0:w], bank[7][0:w, P:P + DV], ost[0:w, 2:3], None, ALU.mult), "on_set")

                def og(i, t, w):
                    W(dve, "ot_mm", i, t + 1)
                    for j in range(2):
                        dst = gate[:, j, t * P:t * P + w]
                        m = dve.scalar_tensor_tensor(out=dst, in0=bank[7][:, (0, 3 * P)[j]:(0, 3 * P)[j] + w],
                                                     scalar=vv("gla_g", P, j), in1=dst, op0=ALU.mult, op1=ALU.mult)
                    inc(m, "gated")

                def satt(i):
                    att_mask(i, TT, NSAMP, "smpmax", "smpmin")
                    dve.wait_ge(zero_set, 1)
                    inc(dve.tensor_copy(diag(q_diag[:].rearrange("p b t -> p (b t)"), NSAMP + TS, NB),
                                        q_in[:, SEQ:NT].rearrange("p (b t) -> p b t", b=NB)), "qd_set")
                    rows_of(i, 0)

                def rows_of(i, r):
                    W(dve, "su_mm", i, r - 1)
                    for j in range(2):
                        b = 2 * r + j
                        inc(dve.tensor_scalar(k_row[:, 2 * (r % 2) + j, :], k_tok[0:NSAMP, TT, :], cc("rowmask", NSAMP)[:, b:b + 1], None,
                                              ALU.mult), "kr_set")

                def sstate(i, r):
                    if r + 1 < NB // 2:
                        rows_of(i, r + 1)
                    W(dve, "su_mm", i, r + 1)
                    dve.wait_ge(s1_out, i * 128 + 32 * r + 16)
                    for j in range(2):
                        b = 2 * r + j
                        c = SEQ // CH + b
                        inc(dve.scalar_tensor_tensor(out=s1[:, j, :], in0=s0[:, 2 * (r % 2) + j, :], scalar=e_last[:, c:c + 1],
                                                     in1=bank[2][:, j * DV:(j + 1) * DV], op0=ALU.mult, op1=ALU.add), "s1_set")

                with dve.Fori(0, GH) as i:
                    run(dve, {"sum": total, "prep": prep, "qbd": qbd, "k": kstep, "soft": soft, "v": vstep, "out": out, "gate": gate_out, "start": start,
                              "decay": decay, "dec_last": dec_last, "dec_diff": dec_diff, "z": z, "evac": evac, "att": att_step,
                              "o": lambda i, t: o_norm(i, t, P), "og": lambda i, t: og(i, t, P), "satt": satt,
                              "sstate": sstate, "so": lambda i: o_norm(i, TT, NSAMP), "sog": lambda i: og(i, TT, NSAMP)}, i)

            @block.tensor
            def _(pe):
                opened(pe, *(S[n] for n in ("dc_mm v_turned kd_turned att_mm o_mm u_mm u_half ot_mm su_mm kt_mm sc_mm new_mm pt_mm "
                                            "pn_mm pv pvn od_mm").split()))
                MM = pe.matmul

                def kstep(i, q, p):
                    if p < NPG:
                        n = q * NPG + p
                        wait_page(pe, i, q, p)
                        W(pe, "kt_lo_set", i, n - 1)
                        if p < 2:
                            W(pe, "pt_lo", i, q * (NPG // 2))
                        for hp in range(NHP):
                            m = pe.transpose(bank[3 + n % 2][:, hp * P:(hp + 1) * P], page[p % 8][:, hp * P:(hp + 1) * P], cc("ident"))
                        inc(m, "kt_mm")
                    if p >= 2:
                        n = q * NPG + p - 2
                        W(pe, "kt_lo_set", i, n + 1)
                        W(pe, "s_add", i, n - 1)
                        if p == 2:
                            W(pe, "qb_lo", i, 2 * q + 2)
                            W(pe, "od_g", i, q)
                        if p == 3:
                            W(pe, "od_set", i, q)
                        for k, kt in enumerate((kv_hi, kv_lo)):
                            for hp in range(NHP):
                                m = MM(bank[5 + n % 2][:, 0:PAGE], q_bd[:, hp].rearrange("p a c -> p (a c)"),
                                       kt[:, (p - 2) % 4, hp * P:(hp + 1) * P], start=(k == 0 and hp == 0), stop=(k == 1 and hp == 3))
                        inc(m, "sc_mm")

                def soft(i, q):
                    W(pe, "s_add", i, NPG * (q + 1) - 1)
                    b8 = ds(i * (2 * TS) + q * TS, TS)
                    for k, kt in enumerate((k_s_hi, k_s_lo)):
                        for hp in range(NHP):
                            m = MM(bank[5][:, 0:TS], q_bd[:, hp].rearrange("p a c -> p (a c)"), kt[:, hp, b8],
                                   start=(k == 0 and hp == 0), stop=(k == 1 and hp == 3))
                    inc(m, "new_mm")

                def vstep(i, q, g):
                    if g < NPG // 2:
                        u = q * (NPG // 2) + g
                        W(pe, "exp2", i, q + 1)
                        W(pe, "pt_lo", i, u - 1)
                        if g < 2:
                            W(pe, "kt_lo_set", i, NPG * (q + 1))
                        inc(pe.transpose(bank[3 + u % 2][:, 0:P], sc[:, g * P:(g + 1) * P], cc("ident")), "pt_mm")
                    if g >= 1:
                        u = q * (NPG // 2) + g - 1
                        W(pe, "pt_lo", i, u + 1)
                        for h in range(2):
                            page_ = 2 * (g - 1) + h
                            W(pe, v_lo_name(h), i, u + 1)
                            if g == 1:
                                W(pe, "s_add", i, NPG * (q + 1))
                            for k, v in enumerate((kv_hi, kv_lo)):
                                m = MM(bank[6], p_t[:, u % 2, h].rearrange("p a c -> p (a c)"), v[:, page_ % 4, :],
                                       start=(g == 1 and h == 0 and k == 0), stop=(page_ == NPG - 1 and k == 1))
                            inc(m, "pv")

                def pn(i, q):
                    W(pe, "n_add", i, q + 1)
                    stream.pass_waits(pe)
                    inc(pe.transpose(bank[5][0:TS, 0:NSAMP], sc[0:NSAMP, HALF:HALF + TS], cc("ident", NSAMP)[:, 0:NSAMP]), "pn_mm")

                def pnv(i, q):
                    W(pe, "pn_set", i, q + 1)
                    pe.wait_ge(vn_in, i * 32 + 16 * (q + 1))
                    stream.pass_waits(pe)
                    inc(MM(bank[6][0:NSAMP, :], pn_t[:], vn_raw, start=False, stop=False, skip_group_check=True), "pvn")

                def gate_out(i, q):
                    W(pe, "od_set", i, q + 1)
                    stream.pass_waits(pe)
                    for hp in range(NHP):
                        m = pe.transpose(bank[5][:, hp * NSAMP:(hp + 1) * NSAMP], u_lo[:, hp * P:(hp + 1) * P],
                                         cc("ident", NSAMP)[:, 0:NSAMP])
                    inc(m, "od_mm")

                def decay(i, c):
                    t0, w = CHUNKS[c]
                    W(pe, "wa_set", i, 1)
                    W(pe, "dc_min", i, c)
                    W(pe, "s1_set", i, 0)
                    stream.pass_waits(pe)
                    inc(MM(bank[2][:, 0:w], wa[:], glr[:, t0:t0 + w], start=True, stop=True), "dc_mm")

                def turn(i, src, p, name, done, k):
                    W(pe, done, i, k - 1)
                    if p == 0:
                        W(pe, "dc_min", i, 3)
                        W(pe, "gated", i, 0)
                    stream.pass_waits(pe)
                    for t in (range(4 * p, 4 * p + 4) if p < 2 else [TT]):
                        n = P if t < TT else NSAMP
                        m = pe.transpose(bank[(2, 7, 2)[p]][0:n, (t % 4) * P:(t % 4) * P + P], src[:, t * P:t * P + n], cc("ident"))
                    inc(m, name)

                def vturn(i, n, p):
                    pe.wait_ge(stream.z_read, stream.chunk(i, n, 2))
                    W(pe, "vt_set", i, 3 * n + p - 1)
                    turn(i, v_fm, p, "v_turned", "vt_set", 3 * n + p)

                def kturn(i, p):
                    pe.wait_ge(stream.z_read, stream.chunk(i, K, 2))
                    W(pe, "vt_set", i, 6)
                    turn(i, kdec, p, "kd_turned", "kd_set", p)

                def z(i, n, c, part):
                    stream.project(pe, i, n, c, range(part * KT_ // PARTS, (part + 1) * KT_ // PARTS))

                def att_step(i, t):
                    if t == 0:
                        W(pe, "vt_set", i, 6)
                        W(pe, "kd_set", i, 3)
                        W(pe, "kin_set", i, 3)
                    tok = slice(t * P, (t + 1) * P)
                    W(pe, "st_set", i, 2 * t)
                    for j in range(2):
                        if j == 1:
                            W(pe, "gated", i, t)
                            inc(MM(bank[7][:, 0:P], k_in[:, tok], q_in[:, tok], start=True, stop=True), "att_mm")
                            W(pe, "u_half", i, t + 1)
                        m = MM(bank[2][:, j * DV:(j + 1) * DV], k_tok[rows[j], t, :], v_tok[rows[j], t, :], start=True, stop=True)
                        inc(m, ("u_half", "u_mm")[j])

                def o_step(i, t):
                    W(pe, "att_set", i, t + 1)
                    MM(bank[7][:, P:P + DV], att[:], v_tok[:, t, :], start=True, stop=False, skip_group_check=True)
                    W(pe, "st_set", i, 2 * t + 1)
                    for j in range(2):
                        c = 2 * t + j
                        m = MM(bank[7][rows[j], P:P + DV], q_in[:, c * CH:(c + 1) * CH], state[:, c % 3, :], start=False,
                               stop=(j == 1), skip_group_check=True)
                    inc(m, "o_mm")

                def og(i, t, w):
                    W(pe, "on_set", i, t + 1)
                    stream.pass_waits(pe)
                    for j in range(2):
                        m = pe.transpose(bank[7][:, (0, 3 * P)[j]:(0, 3 * P)[j] + w], o_n[0:w, j * P:(j + 1) * P],
                                         cc("ident", w)[:, 0:w])
                    inc(m, "ot_mm")

                def satt(i):
                    W(pe, "gated", i, TT)
                    stream.pass_waits(pe)
                    inc(MM(bank[7][0:NSAMP, 0:NSAMP], k_in[:, SEQ:NT], q_in[:, SEQ:NT], start=True, stop=True), "att_mm")

                def sstate(i, r):
                    if r == 0:
                        W(pe, "att_set", i, TT + 1)
                        W(pe, "qd_set", i, 1)
                        W(pe, "st_set", i, 2 * TT)
                        stream.pass_waits(pe)
                        MM(bank[7][0:NSAMP, P:P + DV], att[0:NSAMP, 0:NSAMP], v_tok[0:NSAMP, TT, :], start=True, stop=False,
                           skip_group_check=True)
                    pe.wait_ge(s0_in[r % 2], i * 64 + 32 * (r // 2 + 1))
                    W(pe, "s1_set", i, 2 * r)
                    W(pe, "kr_set", i, 2 * r + 2)
                    stream.pass_waits(pe)
                    for j in range(2):
                        m = MM(bank[7][0:NSAMP, P:P + DV], q_diag[:, 2 * r + j, :], s0[:, 2 * (r % 2) + j, :], start=False,
                               stop=(r == 3 and j == 1), skip_group_check=True)
                    if r == 3:
                        inc(m, "o_mm")
                    for j in range(2):
                        m = MM(bank[2][:, j * DV:(j + 1) * DV], k_row[:, 2 * (r % 2) + j, :], v_tok[0:NSAMP, TT, :], start=True, stop=True)
                    inc(m, "su_mm")

                with pe.Fori(0, GH) as i:
                    run(pe, {"k": kstep, "soft": soft, "v": vstep, "pn": pn, "pnv": pnv, "gate": gate_out, "decay": decay, "vturn": vturn,
                             "kturn": kturn, "z": z, "att": att_step, "o": o_step, "og": lambda i, t: og(i, t, P),
                             "satt": satt, "sstate": sstate, "sog": lambda i: og(i, TT, NSAMP)}, i)


def build_merge(nc, ins, outs, scratch, sem, sb, bank, stream, os_fm):
    NA, NBR, HW = NHP, 2 * GH, D // 2
    YT = TT + 1
    with ExitStack() as ctx:
        fox_o = sb(ctx, "fox_o", [P, NA, NT])
        gla_o = sb(ctx, "gla_o", [P, NBR, NT])
        m_fm = sb(ctx, "m_fm", [P, KT_, NT])
        up_a = sb(ctx, "up_a", [P, NA, P])
        up_b = sb(ctx, "up_b", [P, NBR, P])
        g_a = sb(ctx, "g_a", [P, NT])
        g_b = sb(ctx, "g_b", [P, NT])
        x_ring = fox_o[:, 0:2, :].rearrange("p a t -> p (a t)")
        y_ring = fox_o[:, 2:4, :].rearrange("p a t -> p (a t)")

        per = {"g_abs": 12, "g_exp": 12, "g_ln": 12, "g_y": 12, "g_sig": 12, "a_mm": 6, "b_mm": 6, "a_read": 6, "b_read": 6, "m_set": 6,
               "y_mm": YT, "y_set": YT}
        S = {n: sem("d_" + n) for n in per}
        o_in, up_a_in, up_b_in, w_in, os_in = (sem(n) for n in ("o_in", "up_a_in", "up_b_in", "w_out_in", "os_in"))
        x_in = [sem(f"xr_in{t}") for t in range(3)]
        y_out = [sem(f"y_out{t}") for t in range(3)]
        stream.phase(TT * 2 + 6 * GH, 4, (0, 1))
        xp = ins["x_prompt"].rearrange("a l d -> (a l) d")
        xs = ins["x_sample"].rearrange("b l d -> (b l) d")
        yp = outs["y_p"].rearrange("a l d -> (a l) d")
        ys = outs["y_s"].rearrange("b l d -> (b l) d")

        def W(eng, name, i, k):
            eng.wait_ge(S[name], upto(i, per[name], k))

        def inc(m, name):
            m.then_inc(S[name], 1)

        def ring(r, t):
            return r[:, t % 3 * HW:(t % 3 + 1) * HW]

        with nc.Block() as block:
            @block.sync
            def _(sp):
                for k in range(NA):
                    sp.dma_start(fox_o[:, k, 0:SEQ], scratch["ofox"][k]).then_inc(o_in, 16)
                for k in range(GH):
                    sp.dma_start(gla_o[:, 2 * k:2 * k + 2, :], scratch["ogla"][k]).then_inc(o_in, 16)
                with sp.Fori(0, KT_ // 2) as i:
                    for s in range(2):
                        W(sp, "a_mm", i, 3 * s)
                        sp.dma_start(up_a[:], ins["w_up_a"][ds(i * 2 + s, 1)].rearrange("o p k c -> (o p) k c")).then_inc(up_a_in, 16)
                        W(sp, "b_mm", i, 3 * s)
                        sp.dma_start(up_b[:], ins["w_up_b"][ds(i * 2 + s, 1)].rearrange("o p k c -> (o p) k c")).then_inc(up_b_in, 16)
                        for n in range(2):
                            stream.load(sp, i, 2 * s + n)
                W(sp, "b_mm", KT_ // 2, 0)
                W(sp, "a_mm", KT_ // 2, 0)
                for h in range(2):
                    sp.dma_start(gla_o[:, :, h * HW:(h + 1) * HW], ins["w_out"][:, :, h * HW:(h + 1) * HW]).then_inc(w_in, 16)
                    sp.wait_ge(w_in, 16 * (h + 1))
                for t in range(3):
                    sp.sem_inc(y_out[t], 16)

                with sp.Fori(0, 2) as h:
                    W(sp, "y_set", h, 0)

                    def load_x(t):
                        src = xp[t * P:(t + 1) * P, ds(h * HW, HW)] if t < TT else xs[:, ds(h * HW, HW)]
                        sp.dma_start(ring(x_ring, t)[0:P if t < TT else NSAMP], src).then_inc(x_in[t % 3], 16)
                    for t in range(3):
                        load_x(t)
                    for t in range(YT):
                        W(sp, "y_set", h, t + 1)
                        dst = yp[t * P:(t + 1) * P, ds(h * HW, HW)] if t < TT else ys[:, ds(h * HW, HW)]
                        sp.dma_start(dst, ring(y_ring, t)[0:P if t < TT else NSAMP]).then_inc(y_out[t % 3], 16)
                        if t + 3 < YT:
                            load_x(t + 3)
                for t in range(3):
                    sp.wait_ge(y_out[t], 16 + 2 * (YT // 3) * 16)

            @block.scalar
            def _(act):
                opened(act, *(S[n] for n in ("g_abs", "g_exp", "g_ln", "g_sig")))
                act.activation(fox_o[:, :, SEQ:NT], os_fm[:], ACT.Copy).then_inc(os_in, 1)
                with act.Fori(0, KT_ // 2) as i:
                    for s in range(2):
                        for n, g in enumerate((g_a, g_b)):
                            stream.split_hi(act, i, 2 * s + n)
                            for c, (t0, w) in enumerate(CHUNKS):
                                act.wait_ge(stream.projected, stream.chunk(i, 2 * s + n, c))
                                W(act, "m_set", i, 3 * (s - 1) + c + 1 if s else 0)
                                sigmoid_act(act, lambda name: W(act, name, i, 6 * s + 3 * n + c + 1), inc,
                                            stream.bank_of(2 * s + n, c), g[:, t0:t0 + w])

            @block.vector
            def _(dve):
                opened(dve, *(S[n] for n in ("g_y", "a_read", "b_read", "m_set", "y_set")))
                with dve.Fori(0, KT_ // 2) as i:
                    for s in range(2):
                        for n, g in enumerate((g_a, g_b)):
                            stream.split_lo(dve, i, 2 * s + n)
                            for c, (t0, w) in enumerate(CHUNKS):
                                sigmoid_dve(dve, lambda name: W(dve, name, i, 6 * s + 3 * n + c + 1), inc,
                                            stream.bank_of(2 * s + n, c), g[:, t0:t0 + w])
                                W(dve, "g_y", i, 6 * s + 3 * n + c + 1)
                                dve.sem_inc(stream.z_read, 1)
                        for c, (t0, w) in enumerate(CHUNKS):
                            e = 3 * s + c
                            W(dve, "g_sig", i, 6 * s + 3 + c + 1)
                            W(dve, "a_mm", i, e + 1)
                            inc(dve.tensor_tensor(g_a[:, t0:t0 + w], bank[2 + c][:, 0:w], g_a[:, t0:t0 + w], ALU.mult), "a_read")
                            W(dve, "b_mm", i, e + 1)
                            inc(dve.tensor_tensor(g_b[:, t0:t0 + w], bank[5 + c][:, 0:w], g_b[:, t0:t0 + w], ALU.mult), "b_read")
                            W(dve, "a_read", i, e + 1)
                            W(dve, "b_read", i, e + 1)
                            inc(dve.tensor_tensor(m_fm[:, ds(i * 2 + s, 1), t0:t0 + w], g_a[:, t0:t0 + w].unsqueeze(1),
                                                  g_b[:, t0:t0 + w].unsqueeze(1), ALU.add), "m_set")
                with dve.Fori(0, 2) as h:
                    for t in range(YT):
                        n = P if t < TT else NSAMP
                        W(dve, "y_mm", h, t + 1)
                        dve.wait_ge(x_in[t % 3], h * (YT // 3 * 16) + (t // 3 + 1) * 16)
                        dve.wait_ge(y_out[t % 3], h * (YT // 3 * 16) + (t // 3 + 1) * 16)
                        inc(dve.tensor_tensor(ring(y_ring, t)[0:n], bank[2 + t % 3][0:n, 0:HW], ring(x_ring, t)[0:n], ALU.add), "y_set")

            @block.tensor
            def _(pe):
                opened(pe, *(S[n] for n in ("a_mm", "b_mm", "y_mm")))
                with pe.Fori(0, KT_ // 2) as i:
                    for s in range(2):
                        for n in range(2):
                            for c in range(3):
                                stream.project(pe, i, 2 * s + n, c)
                        pe.wait_ge(os_in, 1)
                        pe.wait_ge(o_in, (NA + GH) * 16)
                        for c, (t0, w) in enumerate(CHUNKS):
                            for name, read, b0, wt, o, nk in (("a_mm", "a_read", 2, up_a, fox_o, NA),
                                                              ("b_mm", "b_read", 5, up_b, gla_o, NBR)):
                                if c == 0:
                                    pe.wait_ge(up_a_in if nk == NA else up_b_in, i * 32 + (s + 1) * 16)
                                W(pe, read, i, 3 * s + c - 2 if s else 0)
                                if s:
                                    W(pe, read, i, c + 1)
                                for k in range(nk):
                                    m = pe.matmul(bank[b0 + c][:, 0:w], wt[:, k, :], o[:, k, t0:t0 + w], start=(k == 0), stop=(k == nk - 1))
                                inc(m, name)
                with pe.Fori(0, 2) as h:
                    W(pe, "m_set", KT_ // 2, 0)
                    pe.wait_ge(w_in, h * 16 + 16)
                    for t in range(YT):
                        n = P if t < TT else NSAMP
                        W(pe, "y_set", h, t - 2)
                        stream.pass_waits(pe)
                        for k in range(KT_):
                            m = pe.matmul(bank[2 + t % 3][0:n, 0:HW], m_fm[:, k, t * P:t * P + n], gla_o[:, k, ds(h * HW, HW)],
                                          start=(k == 0), stop=(k == KT_ - 1))
                        inc(m, "y_mm")


def diag(flat, step, n):
    return bass.AP(flat.tensor, flat.offset, [list(flat.ap[0]), [step, n], [1, TS]])


_OUTS = {"y_p": (1, SEQ, D), "y_s": (NB, TS, D), "k_p": (1, 1, SEQ, H, HD), "v_p": (1, 1, SEQ, H, HD),
         "logf_p": (SEQ, H), "gla_p": (1, 1, GH, DK, DV), "k_s": (1, NB, TS, H, HD), "v_s": (1, NB, TS, H, HD),
         "logf_s": (NSAMP, H), "gla_s": (1, NB, GH, DK, DV)}


def kernel(x_prompt, x_sample, cache_k, cache_v, cache_logf, state_gla, page_table, ln_g, w_in, fox_b_f,
           q_norm_g, k_norm_g, gla_w_a2, gla_b_a, gla_norm_g, w_up_a, w_up_b, w_out):
    import concourse.bacc as bacc
    from concourse.bass_utils import run_bass_kernel_spmd as run

    def f(a):
        return np.ascontiguousarray(a)

    w = np.asarray(w_in)[0].reshape(KT_, P, -1).transpose(1, 0, 2)
    at = dict(zip(("fq", "fk", "fv", "ff", "fg", "gq", "gk", "gv", "glr", "gg", "ma", "mb"),
                  np.concatenate([[0], np.cumsum((FW, FW, FW, H, FW, GH * DK, GH * DK, GH * DV, RANK, GH * DV, D))])))

    def tile(name, j):
        c = at[name] + j * P
        return w[:, :, c:c + P]

    order = [(n, j) for j in range(NHP) for n in ("fv", "fk", "fq", "fg")]
    order += [t for g in range(GH) for t in (("gv", 2 * g), ("gv", 2 * g + 1), ("gq", g), ("gk", g),
                                             ("gg", 2 * g), ("gg", 2 * g + 1))]
    order += [(n, j) for j in range(KT_) for n in ("ma", "mb")]
    order += [("ma", 0), ("mb", 0)]
    vecs = np.zeros((P, NVEC), np.float32)

    def put(name, a):
        o, c = VEC_W[name]
        vecs[:a.shape[0], o:o + c] = a
    put("ln_g", np.asarray(ln_g)[0].reshape(KT_, P).T)
    put("gq", np.tile(np.asarray(q_norm_g)[0], 2)[:, None])
    put("gk", np.tile(np.asarray(k_norm_g)[0], 2)[:, None])
    put("gla_g", np.asarray(gla_norm_g)[0].reshape(2, P).T)
    put("b_f", np.asarray(fox_b_f)[0][:, None])
    put("b_a", np.asarray(gla_b_a)[0].reshape(GH, DK).T)
    arrays = {
        "x_prompt": x_prompt, "x_sample": x_sample, "const": constants(), "vecs": vecs,
        "w_ff": w[:, :, at["ff"]:at["ff"] + H], "w_lr": w[:, :, at["glr"]:at["glr"] + RANK],
        "w_tiles": np.stack([tile(n, j) for n, j in order]),
        "w_up_a": np.asarray(w_up_a)[0].reshape(NHP, P, KT_, P).transpose(2, 1, 0, 3),
        "w_up_b": np.asarray(w_up_b)[0].reshape(KT_, P, KT_, P).transpose(2, 1, 0, 3),
        "w_out": np.asarray(w_out)[0].reshape(KT_, P, D).transpose(1, 0, 2),
        "cache_k": np.asarray(cache_k).reshape(NPHYS, PAGE, FW), "cache_v": np.asarray(cache_v).reshape(NPHYS, PAGE, FW),
        "cache_logf": np.asarray(cache_logf).reshape(NPHYS, PAGE, H),
        "state": np.asarray(state_gla)[0], "page_table": np.asarray(page_table).reshape(1, NB * NPG),
        "w_a2": np.asarray(gla_w_a2)[0].reshape(RANK, GH, DK).transpose(1, 0, 2),
    }
    nc = bacc.Bacc("TRN2", target_bir_lowering=False, num_devices=1)
    feeds, ins, outs = {}, {}, {}
    for name, a in arrays.items():
        a = f(a)
        feeds[f"in_{name}"] = a
        ins[name] = nc.dram_tensor(f"in_{name}", a.shape, mybir.dt.from_np(a.dtype), kind="ExternalInput").ap()
    for name, shape in _OUTS.items():
        outs[name] = nc.dram_tensor(f"out_{name}", shape, F32, kind="ExternalOutput").ap()
    scratch = {name: nc.dram_tensor(f"tmp_{name}", shape, F32, kind="Internal").ap() for name, shape in
               {"cum": (H, SEQ), "ncum": (H, SEQ), "cum_s": (H, NSAMP), "ones": (1, SEQ), "ofox": (NHP, P, SEQ),
                "bias": (NB * H, PAST), "ogla": (GH, P, 2, NT)}.items()}
    fox_gla_step(nc, ins, outs, scratch)
    r = run(nc, [feeds], core_ids=[0]).results[0]
    o = {n: r[f"out_{n}"] for n in _OUTS}
    return (o["y_p"], o["y_s"], o["k_p"], o["v_p"], o["logf_p"].reshape(1, 1, SEQ, H), o["gla_p"],
            o["k_s"], o["v_s"], o["logf_s"].reshape(1, NB, TS, H), o["gla_s"])
```

```python
from contextlib import ExitStack

import numpy as np

import concourse.bass as bass
from concourse import mybir

F32 = mybir.dt.float32
F32R = mybir.dt.float32r
I32 = mybir.dt.int32
ALU = mybir.AluOpType
ACT = mybir.ActivationFunctionType
AX_X = mybir.AxisListType.X
ds = bass.ds

P = 128
D = 1024
SEQ = 1024
NB, TS = 8, 8
NSAMP = NB * TS
NT = SEQ + NSAMP
KT_ = D // P
H, HD = 8, 64
FW = H * HD
NHP = H // 2
GH, DK, DV = 4, 128, 256
CH = 64
RANK = 16
PAGE = 128
NPG = 32
PAST = NPG * PAGE
HALF = PAST // 2
NPHYS = NB * NPG + NB * NPG // 4
EPS = 1e-6
TAU = 16.0
BIG = 3.0e38
CHUNKS = [(0, 384), (384, 384), (768, 320)]
LASTP = SEQ - CHUNKS[2][0]
TT = SEQ // P

CONST_W = {}
_w = 0
for _n, _c in [("ident", 128), ("causal", 128), ("glamax", 128), ("glamin", 128), ("smpmax", 64),
               ("smpmin", 64), ("scan", 384), ("scan_last", 320), ("bdones", 128), ("rowmask", 8), ("newmask", 8)]:
    CONST_W[_n] = (_w, _c)
    _w += _c
NCONST = _w
VEC_W = {}
_w = 0
for _n, _c in [("ln_g", KT_), ("gq", 1), ("gk", 1), ("gla_g", 2), ("b_f", 1), ("b_a", GH)]:
    VEC_W[_n] = (_w, _c)
    _w += _c
NVEC = _w


def constants():
    c = np.zeros((P, NCONST), np.float32)

    def put(name, a):
        o, w = CONST_W[name]
        c[:a.shape[0], o:o + w] = a
    r = np.arange(P)
    put("ident", np.eye(P))
    put("causal", np.where(r[None, :] <= r[:, None], 0, -BIG))
    ok = (r[:, None] <= r[None, :]) & (r[:, None] // CH == r[None, :] // CH)
    put("glamax", np.where(ok, BIG, 0))
    put("glamin", np.where(ok, -BIG, 0))
    s = np.arange(NSAMP)
    ok = (s[:, None] <= s[None, :]) & (s[:, None] // TS == s[None, :] // TS)
    put("smpmax", np.where(ok, BIG, 0))
    put("smpmin", np.where(ok, -BIG, 0))
    scan = (np.arange(CHUNKS[0][1]) % CH != 0).astype(np.float32)
    put("scan", np.tile(scan, (P, 1)))
    put("scan_last", np.tile(np.concatenate([scan[:LASTP], s % TS != 0]), (P, 1)))
    put("bdones", (r[:, None] // HD == r[None, :] // HD).astype(np.float32))
    put("rowmask", (s[:, None] // TS == np.arange(NB)[None, :]).astype(np.float32))
    put("newmask", np.where(np.arange(TS)[None, :] <= (s % TS)[:, None], 0, -BIG))
    return c


def upto(i, per, k, base=0):
    return i * per + (base + max(k, 0) + 1)


def opened(eng, *sems):
    for s in sems:
        eng.sem_inc(s, 1)


def sigmoid_act(act, wait, inc, z, g, split=False):
    inc(act.activation(g, z, ACT.Abs), "g_abs")
    wait("g_abs")
    inc(act.activation(g, g, ACT.Exp, scale=-1.0), "g_exp")
    wait("g_exp")
    inc(act.activation(g, g, ACT.Ln, bias=1.0), "g_ln")
    if not split:
        sigmoid_act_end(act, wait, inc, g)


def sigmoid_act_end(act, wait, inc, g):
    wait("g_y")
    inc(act.activation(g, g, ACT.Exp), "g_sig")


def sigmoid_dve(dve, wait, inc, z, g):
    wait("g_ln")
    inc(dve.scalar_tensor_tensor(out=g, in0=z, scalar=0.0, in1=g, op0=ALU.min, op1=ALU.subtract), "g_y")


def fox_gla_step(nc, ins, outs, scratch):
    top = ExitStack()
    with top:
        def sem(name):
            return nc.alloc_semaphore(name=name)

        def sb(ctx, name, shape, dt=F32):
            return ctx.enter_context(nc.sbuf_tensor(name, shape, dt))

        psum = top.enter_context(nc.psum_tensor("psum", [P, 8 * 512], F32))
        bank = [psum[:, n * 512:(n + 1) * 512] for n in range(8)]

        con = sb(top, "con", [P, NCONST])
        vec = sb(top, "vec", [P, NVEC])

        def cc(name, rows=P):
            o, w = CONST_W[name]
            return con[0:rows, o:o + w]

        def vv(name, rows=P, col=0, n=1):
            o, _ = VEC_W[name]
            return vec[0:rows, o + col:o + col + n]

        epsb = sb(top, "epsb", [P, 1])
        gq8 = sb(top, "gq8", [P, 1])
        h_hi = sb(top, "h_hi", [P, KT_, NT], F32R)
        h_lo = sb(top, "h_lo", [P, KT_, NT], F32R)
        w_raw = [sb(top, f"w_raw{s}", [P, KT_, P]) for s in range(2)]
        w_hi = sb(top, "w_hi", [P, 2, KT_, P], F32R)
        w_lo = sb(top, "w_lo", [P, 2, KT_, P], F32R)
        os_fm = sb(top, "os_fm", [P, NHP, NSAMP])
        decode_ctx = top.enter_context(ExitStack())
        q_s = sb(decode_ctx, "q_s", [P, NHP, NSAMP])
        k_s_hi = sb(decode_ctx, "k_s_hi", [P, NHP, NSAMP], F32R)
        k_s_lo = sb(decode_ctx, "k_s_lo", [P, NHP, NSAMP], F32R)
        glr = sb(decode_ctx, "glr", [RANK, NT])
        newb = sb(decode_ctx, "newb", [NSAMP, NSAMP])

        stream = WeightStream(sem, ins["w_tiles"], w_raw, w_hi, w_lo, h_hi, h_lo, bank)
        with nc.cleanup_on_exit():
            build_inputs(nc, ins, outs, scratch, sem, sb, bank, con, vec, cc, vv, epsb, gq8, h_hi, h_lo, glr, stream)
        with nc.cleanup_on_exit():
            build_fox(nc, ins, outs, scratch, sem, sb, psum, bank, cc, vv, epsb, gq8, stream, os_fm, q_s, k_s_hi,
                      k_s_lo, newb)
        with nc.cleanup_on_exit():
            build_gla(nc, ins, outs, scratch, sem, sb, psum, bank, cc, vv, epsb, stream, os_fm, q_s, k_s_hi, k_s_lo,
                      newb, glr)
        decode_ctx.close()
        with nc.cleanup_on_exit():
            build_merge(nc, ins, outs, scratch, sem, sb, bank, cc, stream, os_fm)


class WeightStream:

    def __init__(self, sem, dram, raw, hi, lo, h_hi, h_lo, bank):
        self.dram, self.raw, self.hi, self.lo = dram, raw, hi, lo
        self.h_hi, self.h_lo, self.bank = h_hi, h_lo, bank
        self.loaded = [sem(f"w_loaded{s}") for s in range(2)]
        self.const_in = sem("const_in")
        self.passed = sem("passed")
        self.hi_set, self.lo_set = sem("w_hi_set"), sem("w_lo_set")
        self.projected = sem("w_projected")
        self.z_read = sem("z_read")

    def phase(self, base, per, ring):
        self.base, self.per, self.ring = base, per, ring

    def pass_waits(self, eng):
        eng.sem_inc(self.passed, 1)

    def open_act(self, act):
        opened(act, self.hi_set)

    def open_dve(self, dve):
        opened(dve, self.lo_set, self.z_read)

    def open_pe(self, pe):
        opened(pe, self.projected)

    def load_first(self, sp, g):
        sp.dma_start(self.raw[g][:], self.dram[g]).then_inc(self.loaded[g], 16)

    def split_hi_first(self, act):
        act.wait_ge(self.loaded[0], 16)
        act.activation(self.hi[:, 0], self.raw[0][:], ACT.Copy).then_inc(self.hi_set, 1)

    def split_lo_first(self, dve):
        dve.wait_ge(self.hi_set, 2)
        dve.tensor_tensor(self.lo[:, 0], self.raw[0][:], self.hi[:, 0].bitcast(F32),
                          ALU.subtract).then_inc(self.lo_set, 1)

    def load(self, sp, i, n):
        sp.wait_ge(self.lo_set, upto(i, self.per, n + 1, self.base))
        sp.dma_start(self.raw[n % 2][:], self.dram[ds(i * self.per + (self.base + n + 2), 1)]
                     .rearrange("o p k c -> (o p) k c")).then_inc(self.loaded[n % 2], 16)

    def split_hi(self, act, i, n):
        s = (n + 1) % 2
        act.wait_ge(self.loaded[s], i * (self.per * 8) + 16 * ((self.base + n + 1) // 2 + 1))
        act.wait_ge(self.projected, i * (3 * self.per) + 3 * (self.base + n) + 1)
        act.activation(self.hi[:, s], self.raw[s][:], ACT.Copy).then_inc(self.hi_set, 1)

    def split_lo(self, dve, i, n):
        s = (n + 1) % 2
        dve.wait_ge(self.hi_set, upto(i, self.per, n + 2, self.base))
        dve.tensor_tensor(self.lo[:, s], self.raw[s][:], self.hi[:, s].bitcast(F32),
                          ALU.subtract).then_inc(self.lo_set, 1)

    def chunk(self, i, n, c):
        return upto(i, 3 * self.per, 3 * n + c + 1, 3 * self.base)

    def bank_of(self, n, c):
        return self.bank[self.ring[(3 * n + c) % len(self.ring)]][:, 0:CHUNKS[c][1]]

    def project(self, pe, i, n, c, ks=range(KT_)):
        t0, w = CHUNKS[c]
        s = n % 2
        if ks[0] == 0:
            pe.wait_ge(self.lo_set, upto(i, self.per, n + 1, self.base))
            pe.wait_ge(self.z_read, i * (3 * self.per) + 3 * self.base + max(3 * n + c + 1 - len(self.ring), 0) + 1)
        out = self.bank_of(n, c)
        for k in ks:
            for a, (wt, h) in enumerate(((self.hi, self.h_hi), (self.hi, self.h_lo), (self.lo, self.h_hi))):
                m = pe.matmul(out, wt[:, s, k, :], h[:, k, t0:t0 + w], start=(k == 0 and a == 0),
                              stop=(k == KT_ - 1 and a == 2))
        if ks[-1] == KT_ - 1:
            m.then_inc(self.projected, 1)


def build_inputs(nc, ins, outs, scratch, sem, sb, bank, con, vec, cc, vv, epsb, gq8, h_hi, h_lo, glr, stream):
    with ExitStack() as ctx:
        x_in = sb(ctx, "x_in", [P, TT + 1, D])
        hn = [sb(ctx, f"hn{s}", [P, D]) for s in range(2)]
        junk = sb(ctx, "x_junk", [P, D])
        hg = [sb(ctx, f"hg{s}", [P, 4, P]) for s in range(2)]
        stat = sb(ctx, "x_stat", [P, 2, 4])
        w_gate = sb(ctx, "w_gate", [P, KT_, 48])
        w_gate_hi = sb(ctx, "w_gate_hi", [P, KT_, 48], F32R)
        w_gate_lo = sb(ctx, "w_gate_lo", [P, KT_, 48], F32R)
        ffx = sb(ctx, "ffx", [H, NT])
        ffa = sb(ctx, "ffa", [H, NT])
        logf = sb(ctx, "logf", [H, NT])
        ones = sb(ctx, "ones_row", [H, SEQ])
        cum = sb(ctx, "cum", [H, NT])
        ncum = sb(ctx, "ncum", [H, SEQ])
        lft = sb(ctx, "logf_tok", [P, TT + 1, H])

        x_loaded = [sem(f"x_loaded{s}") for s in range(2)]
        const_in = stream.const_in
        eps_set, sq_sum, ms_ln, rms_inv = sem("eps_set"), sem("sq_sum"), sem("ms_ln"), sem("rms_inv")
        x_scaled, x_turned, x_gained, h_hi_set, h_lo_set = (sem(n) for n in
            ("x_scaled", "x_turned", "x_gained", "h_hi_set", "h_lo_set"))
        wg_zero, wg_in, wg_hi, wg_lo = sem("wg_zero"), sem("wg_in"), sem("wg_hi"), sem("wg_lo")
        gate_mm, ff_x, ff_ab, ff_exp, ff_ln, glr_set = (sem(n) for n in
            ("gate_mm", "ff_x", "ff_ab", "ff_exp", "ff_ln", "glr_set"))
        logf_set, cum_set, lf_turned, lf_tok, a_stored = (sem(n) for n in
            ("logf_set", "cum_set", "lf_turned", "lf_tok", "a_stored"))

        xp = ins["x_prompt"].rearrange("a l d -> (a l) d")
        xs = ins["x_sample"].rearrange("b l d -> (b l) d")
        def tile_of(i, s):
            last = isinstance(i, int) and i == TT // 2
            return i * 2 + s, i, s, NSAMP if last else P, i * (2 * P) + s * P

        def tiles(eng):
            with eng.Fori(0, TT // 2 - 1) as i:
                for s in range(2):
                    yield tile_of(i, s)
            for s in range(2):
                yield tile_of(TT // 2 - 1, s)
            yield tile_of(TT // 2, 0)

        def x_tile(t, n):
            return x_in[0:n, ds(t, 1), :].rearrange("p o d -> p (o d)")

        with nc.Block() as block:
            @block.sync
            def _(sp):
                sp.dma_start(con[:], ins["const"]).then_inc(const_in, 16)
                sp.dma_start(vec[:], ins["vecs"]).then_inc(const_in, 16)
                sp.wait_ge(wg_zero, 1)
                sp.dma_start(w_gate[:, :, 0:H], ins["w_ff"]).then_inc(wg_in, 16)
                sp.dma_start(w_gate[:, :, 32:32 + RANK], ins["w_lr"]).then_inc(wg_in, 16)
                for s in range(2):
                    sp.sem_inc(x_loaded[s], 16)
                for t, i, s, n, t0 in tiles(sp):
                    sp.wait_ge(x_loaded[s], i * 16 + 16)
                    src = xp[ds(t0, P), :] if n == P else xs
                    sp.dma_start(x_tile(t, n), src).then_inc(x_loaded[s], 16)
                for g in range(2):
                    stream.load_first(sp, g)
                sp.wait_ge(lf_tok, 2)
                sp.dma_start(outs["logf_p"].rearrange("(t p) h -> p t h", p=P), lft[:, 0:TT, :]).then_inc(a_stored, 16)
                sp.dma_start(outs["logf_s"], lft[0:NSAMP, TT, :]).then_inc(a_stored, 16)
                sp.wait_ge(cum_set, 3)
                sp.dma_start(scratch["cum"], cum[:, 0:SEQ]).then_inc(a_stored, 16)
                sp.dma_start(scratch["ncum"], ncum[:]).then_inc(a_stored, 16)
                sp.dma_start(scratch["cum_s"], cum[:, SEQ:NT]).then_inc(a_stored, 16)
                sp.dma_start(scratch["ones"], ones[0:1, :]).then_inc(a_stored, 16)
                sp.wait_ge(a_stored, 6 * 16)

            @block.gpsimd
            def _(pool):
                pool.memset(epsb[:], EPS).then_inc(eps_set, 1)
                pool.memset(w_gate[:], 0.0).then_inc(wg_zero, 1)
                pool.memset(ones[:], 1.0).then_inc(eps_set, 1)

            @block.scalar
            def _(act):
                act.preload_act_table_set("natural_log_exp_and_others")
                opened(act, sq_sum, ms_ln, rms_inv, h_hi_set)
                act.wait_ge(eps_set, 2)

                def stats(t, i, s, n, t0):
                    act.wait_ge(x_loaded[s], i * 16 + 32)
                    act.wait_ge(x_scaled, upto(i, 2, s - 1))
                    act.activation(junk[0:n, :], x_tile(t, n), ACT.Square,
                                   accum_out=stat[0:n, s, 0:1]).then_inc(sq_sum, 1)
                    act.wait_ge(sq_sum, upto(t, 1, 1))
                    act.activation(stat[0:n, s, 1:2], stat[0:n, s, 0:1], ACT.Ln, bias=epsb[0:n, :],
                                   scale=1.0 / D).then_inc(ms_ln, 1)
                    act.wait_ge(ms_ln, upto(t, 1, 1))
                    act.activation(stat[0:n, s, 2:3], stat[0:n, s, 1:2], ACT.Exp, scale=-0.5).then_inc(rms_inv, 1)

                stats(*tile_of(0, 0))
                for t, i, s, n, t0 in tiles(act):
                    if n == P:
                        stats(*tile_of(i + (s + 1) // 2, (s + 1) % 2))
                    for g in range(2):
                        act.wait_ge(x_gained, upto(t, 2, g + 1, 3))
                        act.activation(h_hi[:, 4 * g:4 * g + 4, ds(t0, n)], hg[g][:, :, 0:n], ACT.Copy).then_inc(h_hi_set, 1)
                stream.open_act(act)
                stream.split_hi_first(act)
                act.wait_ge(wg_in, 32)
                act.activation(w_gate_hi[:], w_gate[:], ACT.Copy).then_inc(wg_hi, 1)
                act.wait_ge(ff_ab, 1)
                act.activation(ffa[:], ffa[:], ACT.Exp, scale=-1.0).then_inc(ff_exp, 1)
                act.wait_ge(ff_exp, 1)
                act.activation(ffa[:], ffa[:], ACT.Ln, bias=1.0).then_inc(ff_ln, 1)

            @block.vector
            def _(dve):
                opened(dve, x_scaled, h_lo_set)
                dve.sem_inc(x_gained, 4)
                dve.wait_ge(const_in, 32)
                dve.tensor_scalar(gq8[:], vv("gq"), HD ** -0.5, None, ALU.mult)

                def scale(t, i, s, n, t0):
                    dve.wait_ge(rms_inv, upto(t, 1, 1))
                    dve.wait_ge(x_turned, upto(i, 4, 2 * (s - 1)))
                    dve.tensor_scalar(hn[s][0:n, :], x_tile(t, n), stat[0:n, s, 2:3], None, ALU.mult).then_inc(x_scaled, 1)

                scale(*tile_of(0, 0))
                for t, i, s, n, t0 in tiles(dve):
                    if n == P:
                        scale(*tile_of(i + (s + 1) // 2, (s + 1) % 2))
                    for g in range(2):
                        dve.wait_ge(x_turned, upto(t, 2, g + 1))
                        dve.wait_ge(h_lo_set, upto(t, 2, 0))
                        gain = vv("ln_g", P, 4 * g, 4).unsqueeze(2).to_broadcast([P, 4, n])
                        dve.tensor_tensor(hg[g][:, :, 0:n], bank[2 * s + g].rearrange("p (k t) -> p k t", k=4)[:, :, 0:n],
                                          gain, ALU.mult).then_inc(x_gained, 1)
                    for g in range(2):
                        dve.wait_ge(h_hi_set, upto(t, 2, g + 1))
                        dve.tensor_tensor(h_lo[:, 4 * g:4 * g + 4, ds(t0, n)], hg[g][:, :, 0:n],
                                          h_hi[:, 4 * g:4 * g + 4, ds(t0, n)].bitcast(F32), ALU.subtract).then_inc(h_lo_set, 1)
                stream.open_dve(dve)
                stream.split_lo_first(dve)
                dve.wait_ge(wg_hi, 1)
                dve.tensor_tensor(w_gate_lo[:], w_gate[:], w_gate_hi[:].bitcast(F32), ALU.subtract).then_inc(wg_lo, 1)
                for c, (t0, n) in enumerate(CHUNKS):
                    dve.wait_ge(gate_mm, c + 1)
                    dve.tensor_scalar(ffx[:, t0:t0 + n], bank[2 + c][0:H, 0:n], vv("b_f", H), None, ALU.add).then_inc(ff_x, 1)
                    dve.tensor_copy(glr[:, t0:t0 + n], bank[2 + c][32:32 + RANK, 0:n]).then_inc(glr_set, 1)
                dve.wait_ge(ff_x, 3)
                dve.scalar_tensor_tensor(out=ffa[:], in0=ffx[:], scalar=-1.0, in1=ffx[:], op0=ALU.mult, op1=ALU.max).then_inc(ff_ab, 1)
                dve.wait_ge(ff_ln, 1)
                dve.scalar_tensor_tensor(out=logf[:], in0=ffx[:], scalar=0.0, in1=ffa[:], op0=ALU.min,
                                         op1=ALU.subtract).then_inc(logf_set, 1)
                dve.wait_ge(logf_set, 1)
                dve.wait_ge(eps_set, 2)
                dve.tensor_tensor_scan(cum[:, 0:SEQ], ones[:], logf[:, 0:SEQ], 0.0, ALU.mult, ALU.add).then_inc(cum_set, 1)
                dve.tensor_tensor_scan(cum[:, SEQ:NT], cc("scan_last", H)[:, LASTP:], logf[:, SEQ:NT], 0.0, ALU.mult, ALU.add).then_inc(cum_set, 1)
                dve.wait_ge(cum_set, 2)
                dve.tensor_scalar(ncum[:], cum[:, 0:SEQ], -1.0, None, ALU.mult).then_inc(cum_set, 1)
                dve.wait_ge(lf_turned, 1)
                dve.tensor_copy(lft[:, 0:TT, :], bank[5][:, 0:TT * H].rearrange("p (t h) -> p t h", h=H)).then_inc(lf_tok, 1)
                dve.tensor_copy(lft[0:NSAMP, TT, :], bank[5][0:NSAMP, TT * H:(TT + 1) * H]).then_inc(lf_tok, 1)

            @block.tensor
            def _(pe):
                opened(pe, x_turned)
                stream.open_pe(pe)
                pe.wait_ge(const_in, 32)
                for t, i, s, n, t0 in tiles(pe):
                    pe.wait_ge(x_scaled, upto(t, 1, 1))
                    for g in range(2):
                        pe.wait_ge(x_gained, upto(t, 2, g))
                        for k in range(4):
                            kk = 4 * g + k
                            m = pe.transpose(bank[2 * s + g][:, k * P:k * P + n], hn[s][0:n, kk * P:(kk + 1) * P], cc("ident", n)[:, 0:n])
                        m.then_inc(x_turned, 1)
                pe.wait_ge(h_lo_set, upto(TT + 1, 2, 0))
                pe.wait_ge(wg_lo, 1)
                for c, (t0, n) in enumerate(CHUNKS):
                    for k in range(KT_):
                        for a, (w, h) in enumerate(((w_gate_hi, h_hi), (w_gate_hi, h_lo), (w_gate_lo, h_hi))):
                            m = pe.matmul(bank[2 + c][0:48, 0:n], w[:, k, :], h[:, k, t0:t0 + n],
                                          start=(k == 0 and a == 0), stop=(k == KT_ - 1 and a == 2))
                    m.then_inc(gate_mm, 1)
                pe.wait_ge(logf_set, 1)
                for t in range(TT + 1):
                    n = P if t < TT else NSAMP
                    m = pe.transpose(bank[5][0:n, t * H:(t + 1) * H], logf[:, t * P:t * P + n], cc("ident", H)[:, 0:H])
                m.then_inc(lf_turned, 1)


def build_fox(nc, ins, outs, scratch, sem, sb, psum, bank, cc, vv, epsb, gq8, stream, os_fm, q_s, k_s_hi, k_s_lo, newb):
    V, K, Q, G = range(4)
    U = 2 * TT
    PG = NPG // NHP
    with ExitStack() as ctx:
        ofox = sb(ctx, "ofox", [P, SEQ])
        v_fm = sb(ctx, "v_fm", [P, NT])
        v_tok = sb(ctx, "v_tok", [P, TT + 1, P])
        k_tok = sb(ctx, "k_tok", [P, TT + 1, P])
        ks_fm = sb(ctx, "ks_fm", [P, NSAMP])
        q_aug = sb(ctx, "q_aug", [P, 2, SEQ])
        k_aug = sb(ctx, "k_aug", [P, 2, SEQ])
        sq = sb(ctx, "sq", [P, 2, 384])
        inv = sb(ctx, "inv", [P, 2, 384])
        eg = sb(ctx, "eg", [P, 384])
        prob = [sb(ctx, f"prob{s}", [P, SEQ]) for s in range(2)]
        prob_t = [sb(ctx, f"prob_t{s}", [P, TT, P]) for s in range(2)]
        nmax = sb(ctx, "nmax", [P, 2])
        den = sb(ctx, "den", [P, 2])
        rden = sb(ctx, "rden", [P, 2])
        o_tok = sb(ctx, "o_tok", [P, 2, P])
        lfk = sb(ctx, "lfk", [P, PG, NB * H])
        lfc = sb(ctx, "lfc", [NB * H, PAST])
        total = sb(ctx, "total", [NB * H, 1])
        one = sb(ctx, "one", [P, 1])
        pages = sb(ctx, "pages", [1, NB * NPG], I32)

        names = ("v_turned v_tok_set k_turned k_tok_set squared norm_mm norm_ln norm_inv k_aug_set q_aug_set ks_set "
                 "ks_hi ks_lo g_abs g_exp g_ln g_y g_sig g_used s_mm s_masked max_set exp_set p_turned pt_a pt_b pv_mm rden_set "
                 "o_set o_turned o_gated lf_turned2 lf_copied").split()
        S = {n: sem(n) for n in names}
        aug_zero, aug_in, aug_one, kv_stored, pg_in, lf_in = (sem(n) for n in ("aug_zero", "aug_in", "aug_one", "kv_stored", "pg_in", "lf_in"))
        one_set, past_cum, past_bias, fin_in, newb_set, b_stored, of_stored = (sem(n) for n in
            ("one_set", "past_cum", "past_bias", "fin_in", "newb_set", "b_stored", "of_stored"))
        stream.phase(0, 4, (6, 0, 1))
        kp = outs["k_p"].rearrange("a b (t p) h d -> p (a b t) (h d)", p=P)
        vp = outs["v_p"].rearrange("a b (t p) h d -> p (a b t) (h d)", p=P)
        ks = outs["k_s"].rearrange("a b t h d -> (a b t) (h d)")
        vs = outs["v_s"].rearrange("a b t h d -> (a b t) (h d)")

        def W(eng, name, i, per, k):
            eng.wait_ge(S[name], upto(i, per, k))

        def count(m, name):
            m.then_inc(S[name], 1)

        with nc.Block() as block:
            @block.sync
            def _(sp):
                sp.wait_ge(aug_zero, 2)
                for hh in range(2):
                    sp.dma_start(q_aug[HD:HD + 1, hh, :], scratch["ones"]).then_inc(aug_one, 16)
                    sp.dma_start(k_aug[HD + 1:HD + 2, hh, :], scratch["ones"]).then_inc(aug_one, 16)
                for t in range(TS):
                    sp.dma_start(newb[t:t + TS * (H - 1) + 1:TS, :], scratch["cum_s"]).then_inc(fin_in, 16)
                sp.sem_inc(kv_stored, 16)
                sp.sem_inc(of_stored, 16)
                with sp.Fori(0, NHP) as i:
                    W(sp, "s_mm", i, U, 0)
                    for hh in range(2):
                        sp.dma_start(q_aug[HD + 1:HD + 2, hh, :], scratch["cum"][ds(i * 2 + hh, 1), :]).then_inc(aug_in, 16)
                        sp.dma_start(k_aug[HD:HD + 1, hh, :], scratch["ncum"][ds(i * 2 + hh, 1), :]).then_inc(aug_in, 16)
                    for n in range(4):
                        stream.load(sp, i, n)
                        if n == Q:
                            W(sp, "v_tok_set", i, 3, 3)
                            sp.dma_start(vp[:, :, ds(i * P, P)], v_tok[:, 0:TT, :]).then_inc(kv_stored, 16)
                            sp.dma_start(vs[:, ds(i * P, P)], v_tok[0:NSAMP, TT, :]).then_inc(kv_stored, 16)
                    W(sp, "k_tok_set", i, 3, 3)
                    sp.dma_start(kp[:, :, ds(i * P, P)], k_tok[:, 0:TT, :]).then_inc(kv_stored, 16)
                    sp.dma_start(ks[:, ds(i * P, P)], k_tok[0:NSAMP, TT, :]).then_inc(kv_stored, 16)
                    W(sp, "o_gated", i, TT, TT)
                    sp.dma_start(scratch["ofox"][ds(i, 1)].rearrange("o p t -> (o p) t"), ofox[:]).then_inc(of_stored, 16)
                sp.wait_ge(of_stored, NHP * 16 + 16)
                sp.wait_ge(kv_stored, NHP * 64 + 16)
                sp.wait_ge(past_bias, 1)
                sp.dma_start(scratch["bias"], lfc[:]).then_inc(b_stored, 16)
                sp.wait_ge(b_stored, 16)

            @block.gpsimd
            def _(pool):
                pool.memset(one[:], 1.0).then_inc(one_set, 1)
                pool.dma_start(pages[:], ins["page_table"]).then_inc(pg_in, 16)
                pool.wait_ge(pg_in, 16)
                with pool.Fori(0, NHP) as i:
                    W(pool, "lf_turned2", i, 2, 0)
                    for g in range(PG):
                        for b in range(NB):
                            page = pool.value_load(pages[0:1, ds(i * PG + (b * NPG + g), 1)], min_val=0, max_val=NPHYS - 1)
                            pool.dma_start(lfk[:, g, b * H:(b + 1) * H], ins["cache_logf"][ds(page, 1)]
                                           .rearrange("o p h -> (o p) h")).then_inc(lf_in, 16)

            @block.scalar
            def _(act):
                opened(act, *(S[n] for n in ("v_tok_set", "k_tok_set", "squared", "norm_ln", "norm_inv", "ks_hi",
                                             "g_abs", "g_exp", "g_ln", "g_sig", "exp_set", "pt_b", "lf_copied")))

                def copy_out(i, tok, src, name, turned, b0):
                    for p in range(3):
                        if p == 0:
                            act.wait_ge(kv_stored, i * 64 + 16)
                        W(act, turned, i, 3, p + 1)
                        if p < 2:
                            act.activation(tok[:, 4 * p:4 * p + 4, :], src[b0 + p].rearrange("p (t c) -> p t c", t=4),
                                           ACT.Copy).then_inc(S[name], 1)
                        else:
                            act.activation(tok[0:NSAMP, TT, :], src[b0][0:NSAMP, 0:P], ACT.Copy).then_inc(S[name], 1)

                def exp(i, u):
                    n = (u // 2 + 1) * P
                    W(act, "max_set", i, U, u + 1)
                    W(act, "p_turned", i, U, u - 1)
                    W(act, "rden_set", i, U, u - 1)
                    act.activation(prob[u % 2][:, 0:n], psum[:, (2 + 2 * (u % 2)) * 512:][:, 0:n], ACT.Exp,
                                   bias=nmax[:, u % 2:u % 2 + 1], accum_out=den[:, u % 2:u % 2 + 1]).then_inc(S["exp_set"], 1)

                with act.Fori(0, NHP) as i:
                    for n in range(4):
                        stream.split_hi(act, i, n)
                        if n == K:
                            copy_out(i, v_tok, bank, "v_tok_set", "v_turned", 2)
                        for c, (t0, w) in enumerate(CHUNKS):
                            z = stream.bank_of(n, c)
                            if n == Q and c == 1:
                                copy_out(i, k_tok, bank, "k_tok_set", "k_turned", 4)
                            if n in (K, Q):
                                e = 3 * (n - K) + c
                                act.wait_ge(stream.projected, stream.chunk(i, n, c))
                                W(act, "norm_mm", i, 6, e - 1)
                                act.activation(sq[:, e % 2, 0:w], z, ACT.Square).then_inc(S["squared"], 1)
                                W(act, "norm_mm", i, 6, e + 1)
                                act.wait_ge(stream.z_read, i * 12 + 3 * n + c)
                                act.activation(inv[:, e % 2, 0:w], bank[7][:, 0:w], ACT.Ln, bias=epsb[:], scale=1.0 / HD)\
                                   .then_inc(S["norm_ln"], 1)
                                W(act, "norm_ln", i, 6, e + 1)
                                act.activation(inv[:, e % 2, 0:w], inv[:, e % 2, 0:w], ACT.Exp, scale=-0.5)\
                                   .then_inc(S["norm_inv"], 1)
                            if n == G and c == 0:
                                act.wait_ge(stream.projected, stream.chunk(i, n, c))
                                W(act, "g_used", i, 2, 0)
                                sigmoid_act(act, lambda name: W(act, name, i, 3, 1), count, z, eg[:, 0:w])
                            if n == G and c == 1:
                                exp(i, 0)
                                exp(i, 1)
                        if n == K:
                            W(act, "ks_set", i, 1, 1)
                            act.activation(k_s_hi[:, ds(i, 1), :], ks_fm[:].unsqueeze(1), ACT.Copy).then_inc(S["ks_hi"], 1)
                    for u in range(U):
                        if 1 < u + 1 < U:
                            exp(i, u + 1)
                        if u in (2, 5):
                            c = u // 2
                            act.wait_ge(stream.z_read, stream.chunk(i, G, c))
                            W(act, "g_used", i, 2, c - 1)
                            sigmoid_act(act, lambda name: W(act, name, i, 3, c + 1), count, inv[:, c - 1, 0:CHUNKS[c][1]],
                                        eg[:, 0:CHUNKS[c][1]], split=True)
                        if u in (3, 6):
                            c = u // 3
                            sigmoid_act_end(act, lambda name: W(act, name, i, 3, c + 1), count, eg[:, 0:CHUNKS[c][1]])
                        if u // 2 >= 4:
                            b = u - 8
                            W(act, "p_turned", i, U, u + 1)
                            W(act, "pv_mm", i, U, u - 1)
                            act.activation(prob_t[u % 2][:, 4:u // 2 + 1, :], bank[7][:, 0:(u // 2 - 3) * P]
                                           .rearrange("p (k q) -> p k q", q=P), ACT.Copy).then_inc(S["pt_b"], 1)
                    for p in range(2):
                        W(act, "lf_turned2", i, 2, p + 1)
                        act.activation(lfc[:, ds(i * (PG * P) + p * 512, 512)], bank[2 + p][0:NB * H, :], ACT.Copy)\
                           .then_inc(S["lf_copied"], 1)

            @block.vector
            def _(dve):
                opened(dve, *(S[n] for n in ("k_aug_set", "q_aug_set", "ks_set", "ks_lo", "g_y", "g_used", "s_masked",
                                             "max_set", "pt_a", "rden_set", "o_set", "o_gated")))

                dve.memset(q_aug[HD:P], 0.0).then_inc(aug_zero, 1)
                dve.memset(k_aug[HD:P], 0.0).then_inc(aug_zero, 1)

                def head_rows(out, z, r, t0, gain, name, last):
                    w = min(CHUNKS[0][1], SEQ - t0)
                    for hh in range(2):
                        rows = slice(hh * HD, (hh + 1) * HD)
                        m = dve.scalar_tensor_tensor(out=out[0:HD, hh, t0:t0 + w], in0=z[rows, 0:w],
                                                     scalar=gain[rows], in1=r[rows, 0:w], op0=ALU.mult, op1=ALU.mult)
                        if hh == 0:
                            m.then_inc(S[name], 1)
                    if last:
                        m.then_inc(stream.z_read, 1)

                def smax(i, u):
                    qb, base = u // 2, (2 + 2 * (u % 2)) * 512
                    n = (qb + 1) * P
                    W(dve, "s_mm", i, U, u + 1)
                    diag = psum[:, base + qb * P:base + n]
                    dve.tensor_tensor(diag, diag, cc("causal"), ALU.add).then_inc(S["s_masked"], 1)
                    W(dve, "s_masked", i, U, u + 1)
                    W(dve, "exp_set", i, U, u - 1)
                    dve.tensor_reduce(nmax[:, u % 2:u % 2 + 1], psum[:, base:base + n], AX_X, ALU.max,
                                      negate=True).then_inc(S["max_set"], 1)

                def finish(i, u):
                    hh = u % 2
                    W(dve, "exp_set", i, U, u + 1)
                    dve.reciprocal(rden[:, hh:hh + 1], den[:, hh:hh + 1]).then_inc(S["rden_set"], 1)
                    W(dve, "rden_set", i, U, u + 1)
                    W(dve, "pv_mm", i, U, u + 1)
                    W(dve, "o_turned", i, TT, u // 2 - 1)
                    dve.tensor_scalar(o_tok[:, u // 2 % 2, hh * HD:(hh + 1) * HD], bank[hh][:, 0:HD],
                                      rden[:, hh:hh + 1], None, ALU.mult).then_inc(S["o_set"], 1)

                with dve.Fori(0, NHP) as i:
                    for n in range(4):
                        stream.split_lo(dve, i, n)
                        for c, (t0, w) in enumerate(CHUNKS):
                            z = stream.bank_of(n, c)
                            if n == V:
                                dve.wait_ge(stream.projected, stream.chunk(i, n, c))
                                W(dve, "v_turned", i, 3, 0)
                                dve.tensor_copy(v_fm[:, t0:t0 + w], z).then_inc(stream.z_read, 1)
                            if n in (K, Q):
                                e = 3 * (n - K) + c
                                r = inv[:, e % 2, 0:w]
                                W(dve, "norm_inv", i, 6, e + 1)
                                if c == 0:
                                    W(dve, "s_mm", i, U, 0)
                                if n == K:
                                    head_rows(k_aug, z, r, t0, vv("gk"), "k_aug_set", c < 2)
                                else:
                                    head_rows(q_aug, z, r, t0, gq8, "q_aug_set", c < 2)
                                if c == 2:
                                    z, r = z[:, LASTP:], r[:, LASTP:]
                                if c == 2 and n == K:
                                    W(dve, "k_turned", i, 3, 0)
                                    dve.scalar_tensor_tensor(out=ks_fm[:], in0=z, scalar=vv("gk"), in1=r, op0=ALU.mult,
                                                             op1=ALU.mult).then_inc(S["ks_set"], 1)
                                    W(dve, "ks_set", i, 1, 1)
                                    W(dve, "ks_hi", i, 1, 1)
                                    dve.tensor_tensor(k_s_lo[:, ds(i, 1), :], ks_fm[:].unsqueeze(1),
                                                      k_s_hi[:, ds(i, 1), :].bitcast(F32), ALU.subtract)\
                                       .then_inc(stream.z_read, 1)
                                elif c == 2:
                                    dve.scalar_tensor_tensor(out=q_s[:, ds(i, 1), :], in0=z.unsqueeze(1), scalar=gq8[:],
                                                             in1=r.unsqueeze(1), op0=ALU.mult, op1=ALU.mult)\
                                       .then_inc(stream.z_read, 1)
                            if n == G and c == 0:
                                sigmoid_dve(dve, lambda name: W(dve, name, i, 3, 1), count, z, eg[:, 0:w])
                                W(dve, "g_sig", i, 3, 1)
                                dve.wait_ge(of_stored, i * 16 + 16)
                                dve.tensor_tensor(ofox[:, t0:t0 + w], z, eg[:, 0:w], ALU.mult).then_inc(stream.z_read, 1)
                            if n == G and c:
                                if c == 1:
                                    smax(i, 0)
                                    smax(i, 1)
                                dve.wait_ge(stream.projected, stream.chunk(i, n, c))
                                dve.tensor_copy(inv[:, c - 1, 0:w], z).then_inc(stream.z_read, 1)
                    for u in range(U + 2):
                        if 1 < u + 1 < U:
                            smax(i, u + 1)
                        if u in (3, 6):
                            c = u // 3
                            w = CHUNKS[c][1]
                            sigmoid_dve(dve, lambda name: W(dve, name, i, 3, c + 1), count, inv[:, c - 1, 0:w], eg[:, 0:w])
                        if u in (4, 7):
                            c = u // 3
                            t0, w = CHUNKS[c]
                            z = inv[:, c - 1, 0:w]
                            W(dve, "g_sig", i, 3, c + 1)
                            if c == 2:
                                dve.tensor_tensor(os_fm[:, ds(i, 1), :], z[:, LASTP:].unsqueeze(1),
                                                  eg[:, LASTP:w].unsqueeze(1), ALU.mult)
                            w = min(w, SEQ - t0)
                            dve.tensor_tensor(ofox[:, t0:t0 + w], z[:, 0:w], eg[:, 0:w], ALU.mult).then_inc(S["g_used"], 1)
                        if u < U:
                            k = min(u // 2 + 1, 4)
                            W(dve, "p_turned", i, U, u + 1)
                            W(dve, "pv_mm", i, U, u - 1)
                            dve.tensor_copy(prob_t[u % 2][:, 0:k, :], bank[6][:, 0:k * P].rearrange("p (k q) -> p k q", q=P))\
                               .then_inc(S["pt_a"], 1)
                        if 1 <= u <= U:
                            finish(i, u - 1)
                        if u >= 2 and u % 2 == 1:
                            qb = (u - 2) // 2
                            W(dve, "o_turned", i, TT, qb + 1)
                            o = ofox[:, qb * P:(qb + 1) * P]
                            dve.tensor_tensor(o, bank[1][:, P:2 * P], o, ALU.mult).then_inc(S["o_gated"], 1)
                dve.wait_ge(one_set, 1)
                dve.wait_ge(S["lf_copied"], upto(NHP, 2, 0))
                dve.tensor_tensor_scan(lfc[:], one[0:NB * H, :].to_broadcast([NB * H, PAST]), lfc[:], 0.0, ALU.mult,
                                       ALU.add).then_inc(past_cum, 1)
                dve.wait_ge(past_cum, 1)
                dve.tensor_copy(total[:], lfc[:, PAST - 1:PAST]).then_inc(past_cum, 1)
                dve.wait_ge(past_cum, 2)
                dve.tensor_scalar(lfc[:], lfc[:], -1.0, total[:], ALU.mult, ALU.add).then_inc(past_bias, 1)
                dve.wait_ge(fin_in, 16 * TS)
                nb = newb[:].rearrange("r (b k) -> r b k", b=NB)
                dve.tensor_tensor(nb, cc("newmask", NSAMP).unsqueeze(1).to_broadcast([NSAMP, NB, TS]), nb,
                                  ALU.subtract).then_inc(newb_set, 1)

            @block.tensor
            def _(pe):
                opened(pe, *(S[n] for n in ("v_turned", "k_turned", "norm_mm", "s_mm", "p_turned", "pv_mm", "o_turned",
                                            "lf_turned2")))

                def turn_kv(i, src, name, done, b0):
                    for p in range(3):
                        W(pe, done, i, 3, p - 1 if p == 2 else 0)
                        stream.pass_waits(pe)
                        for t in (range(4 * p, 4 * p + 4) if p < 2 else [TT]):
                            out = bank[b0 + p % 2]
                            for o, a, ident in src(t):
                                n = P if t < TT else NSAMP
                                m = pe.transpose(out[0:n, (t % 4) * P + o:(t % 4) * P + o + ident.shape[1]], a, ident)
                        m.then_inc(S[name], 1)

                def scores(i, u):
                    qb, hh = u // 2, u % 2
                    W(pe, "exp_set", i, U, u - 1)
                    for c in range(0, qb + 1, 4):
                        n = min(4, qb + 1 - c) * P
                        b = 2 + 2 * hh + c // 4
                        m = pe.matmul(bank[b][:, 0:n], q_aug[:, hh, qb * P:(qb + 1) * P], k_aug[:, hh, c * P:c * P + n],
                                      start=True, stop=True)
                    m.then_inc(S["s_mm"], 1)

                def norm_sum(i, e):
                    w = CHUNKS[e % 3][1]
                    W(pe, "squared", i, 6, e + 1)
                    W(pe, "norm_ln", i, 6, e)
                    pe.matmul(bank[7][:, 0:w], cc("bdones"), sq[:, e % 2, 0:w], start=True, stop=True).then_inc(S["norm_mm"], 1)

                with pe.Fori(0, NHP) as i:
                    for n in range(4):
                        for c in range(3):
                            if n == G and c == 2:
                                pe.wait_ge(stream.z_read, stream.chunk(i, Q, 2))
                                pe.wait_ge(aug_one, 64)
                                pe.wait_ge(aug_in, i * 64 + 64)
                                W(pe, "v_tok_set", i, 3, 3)
                                W(pe, "k_tok_set", i, 3, 3)
                                scores(i, 0)
                                scores(i, 1)
                            stream.project(pe, i, n, c)
                            if n == G and c == 0:
                                norm_sum(i, 5)
                            e = 3 * (n - K) + c - 1
                            if n in (K, Q) and e >= 0:
                                norm_sum(i, e)
                            if n == K and c == 0:
                                pe.wait_ge(stream.z_read, stream.chunk(i, V, 2))
                                W(pe, "exp_set", i, U, 0)
                                W(pe, "lf_copied", i, 2, 0)
                                turn_kv(i, lambda t: [(0, v_fm[:, t * P:min((t + 1) * P, NT)], cc("ident"))],
                                        "v_turned", "v_tok_set", 2)
                            if n == Q and c == 1:
                                pe.wait_ge(stream.z_read, stream.chunk(i, K, 2))
                                turn_kv(i, lambda t: [(hh * HD, k_aug[0:HD, hh, t * P:(t + 1) * P], cc("ident", HD)[:, 0:HD])
                                                      for hh in range(2)] if t < TT else [(0, ks_fm[:], cc("ident"))],
                                        "k_turned", "k_tok_set", 4)
                    for u in range(U + 2):
                        if 1 < u + 1 < U:
                            scores(i, u + 1)
                        if u < U:
                            W(pe, "exp_set", i, U, u + 1)
                            if u == 0:
                                pe.wait_ge(stream.z_read, stream.chunk(i, G, 0))
                            W(pe, "pt_a", i, U, u)
                            for k in range(u // 2 + 1):
                                if k == 4:
                                    W(pe, "pt_b", i, U - 8, u - 8)
                                m = pe.transpose(bank[6 + k // 4][:, (k % 4) * P:(k % 4 + 1) * P],
                                                 prob[u % 2][:, k * P:(k + 1) * P], cc("ident"))
                            m.then_inc(S["p_turned"], 1)
                        if 1 <= u <= U:
                            v = u - 1
                            W(pe, "pt_a", i, U, v + 1)
                            if v // 2 >= 4:
                                W(pe, "pt_b", i, U - 8, v - 7)
                            W(pe, "o_set", i, U, v - 1)
                            if v < 2:
                                pe.wait_ge(stream.z_read, stream.chunk(i, G, 1 + v))
                            if v % 2:
                                W(pe, "o_gated", i, TT, v // 2)
                            for k in range(v // 2 + 1):
                                m = pe.matmul(bank[v % 2][:, 0:HD], prob_t[v % 2][:, k, :],
                                              v_tok[:, k, (v % 2) * HD:(v % 2 + 1) * HD], start=(k == 0), stop=(k == v // 2))
                            m.then_inc(S["pv_mm"], 1)
                        if u >= 2 and u % 2 == 1:
                            qb = (u - 2) // 2
                            W(pe, "o_set", i, U, 2 * qb + 2)
                            pe.transpose(bank[1][:, P:2 * P], o_tok[:, qb % 2, :], cc("ident")).then_inc(S["o_turned"], 1)
                    for p in range(2):
                        pe.wait_ge(lf_in, i * (PG * NB * 16) + PG * NB * 16)
                        W(pe, "exp_set", i, U, U)
                        stream.pass_waits(pe)
                        for g in range(4):
                            m = pe.transpose(bank[2 + p][0:NB * H, g * P:(g + 1) * P], lfk[:, 4 * p + g, :], cc("ident"))
                        m.then_inc(S["lf_turned2"], 1)
                    W(pe, "o_gated", i, TT, TT)


PARTS = 4


def schedule():
    V0, V1, Q, K, G0, G1 = range(6)
    cost = {"z": 0.95, "decay": 1.2, "vturn": 0.6, "kturn": 0.6, "att": 1.8, "o": 1.8, "og": 1.8, "satt": 1.8, "sstate": 4.0,
            "so": 1.5, "sog": 1.5}
    after = {(V1, 0, p + 1): [("vturn", 0, p)] for p in range(3)}
    after |= {(Q, 0, p + 1): [("vturn", 1, p)] for p in range(3)}
    after |= {(G0, 0, p + 1): [("kturn", p)] for p in range(3)}
    after[Q, 0, 3] = [("vturn", 1, 2), ("dec_neg",)]
    after[Q, 1, 1] = [("dec_diff",)]
    after[Q, 1, 3] = [("dec_end",)]
    other = [("start",)] + [("decay", c) for c in range(3)] + [("dec_last",)]
    evac = None
    for n in range(6):
        for c in range(3):
            for part in range(PARTS):
                other.append(("z", n, c, part))
                if part == 0 and evac:
                    other.append(evac)
                other += after.get((n, c, part), [])
            evac = ("evac", n, c)
    other.append(evac)
    gla = [x for t in range(TT) for x in (("att", t), ("o", t), ("og", t))]
    gla += [("satt",)] + [("sstate", r) for r in range(NB // 2)] + [("so",), ("sog",)]
    at = other.index(("evac", G1, 0)) + 1
    late, other = other[at:], other[:at]

    decode = []
    for q in range(2):
        decode.append((("prep", q), 0))
        for p in range(NPG + 2):
            decode.append((("k", q, p), 1))
            decode += [((name, *a), 0) for at, name, a in ((1, "gate", (q - 1,)), (6, "vn_load", (q,)))
                       if at == p and a[0] >= 0]
        decode += [(("soft", q), 3), (("exp", q), 3)] + ([(("qbd", 1), 0)] if q == 0 else [])
        for g in range(NPG // 2 + 2):
            decode += [(("v", q, g), 1.1)] + [((name, q), 0) for at, name in ((2, "sum"), (8, "pn"), (10, "pnv")) if at == g]
        decode.append((("out", q), 2))
    decode.append((("gate", 1), 2))
    total = sum(c for _, c in decode)
    work = sum(cost.get(x[0], 0) for x in other + late + gla)
    steps, done, placed = [], 0.0, 0.0
    for step, share in decode:
        steps.append(step)
        done += share * work / total
        while other or late or gla:
            queue = other or (late if late and (share > 1.5 or not gla) else gla) or late
            if queue is gla and gla[0][0] == "og" and ("evac", G1, gla[0][1] // 3) in late:
                queue = late
            if placed + cost.get(queue[0][0], 0) > done + 0.3:
                break
            placed += cost.get(queue[0][0], 0)
            steps.append(queue.pop(0))
    other += late + gla
    return steps + other + [("end",)]


def build_gla(nc, ins, outs, scratch, sem, sb, psum, bank, cc, vv, epsb, stream, os_fm, q_s, k_s_hi, k_s_lo, newb, glr):
    V0, V1, Q, K, G0, G1 = range(6)
    GTS = TT + 1
    with ExitStack() as ctx:
        wa = sb(ctx, "wa", [RANK, DK])
        ba = sb(ctx, "ba", [P, 1])
        t1 = sb(ctx, "t1", [P, 384])
        kdec = sb(ctx, "kdec", [P, NT])
        q_in = sb(ctx, "q_in", [P, NT])
        k_in = sb(ctx, "k_in", [P, NT])
        v_fm = k_in
        b_last = sb(ctx, "b_last", [P, SEQ // CH + NB])
        e_last = sb(ctx, "e_last", [P, SEQ // CH + NB])
        v_tok = sb(ctx, "gv_tok", [P, GTS, DV])
        k_tok = sb(ctx, "gk_tok", [P, GTS, DK])
        gate = sb(ctx, "gate", [P, 2, NT])
        state = sb(ctx, "state", [P, 3, DV])
        att = sb(ctx, "att", [P, P])
        o_n = sb(ctx, "o_n", [P, DV])
        ost = sb(ctx, "ost", [P, 3])
        s0 = sb(ctx, "s0", [P, 3, 2, DV])
        q_diag = sb(ctx, "q_diag", [P, NB, NSAMP])
        k_row = sb(ctx, "k_row", [NSAMP, 4, DK])
        page = [sb(ctx, f"page{r}", [P, FW]) for r in range(8)]
        kv_hi = sb(ctx, "kv_hi", [P, 2, NHP, 2, P], F32R)
        kv_lo = sb(ctx, "kv_lo", [P, 2, NHP, 2, P], F32R)
        q_bd = sb(ctx, "q_bd", [P, NHP, 2, NSAMP], F32R)
        sc = sb(ctx, "sc", [P, HALF + TS])
        p_t = sb(ctx, "p_t", [P, 3, 2, 2, NSAMP], F32R)
        pn_t = sb(ctx, "pn_t", [TS, NSAMP])
        smst = sb(ctx, "smst", [P, 8])
        shared = sb(ctx, "shared", [P, FW])
        u_lo = shared[0:NSAMP]
        vn_raw = shared[0:TS]
        wa_all = shared[NSAMP:NSAMP + RANK].rearrange("p (g c) -> p g c", g=GH)
        pages = sb(ctx, "pages2", [1, NB * NPG + 8], I32)

        per = {}
        for names, n in (("dc_mm dc_abs dc_exp dc_ln dc_min dc_y dc_cum", 3), ("v_turned vt_set", 6), ("kd_turned kd_set", 3),
                         ("bl_set", 2), ("eb_set en_set el_set dd_set ed_set ba_set wa_set st_zero", 1), ("kin_set", 3),
                         ("g_abs g_exp g_ln g_y g_sig", 6), ("att_mm att_min att_set o_mm", GTS), ("u_mm u_half", TT), ("st_set", 2 * TT),
                         ("ss_set sl_set sr_set on_set ot_mm gated", GTS), ("qd_set", 1), ("kr_set", NB),
                         ("su_mm", NB // 2), ("s1_set", NB), ("kt_mm kt_hi_set kt_lo_set", 2 * NPG),
                         ("sc_mm s_add1 s_add", NPG),
                         ("new_mm n_add1 n_add", 2), ("qb_hi", 4), ("qb_lo", 4), ("pad_set", 2),
                         ("mx1 mx2 mx3 mx4 exp2 dn1 dn2 dn3", 2), ("pt_mm pt_hi pt_lo", NPG), ("pn_mm pn_set", 2),
                         ("v_hi_set pv", 2 * NPG), ("v_even_lo v_odd_lo", NPG), ("pvn u_set od_set od_mm od_g", 2)):
            for n_ in names.split():
                per[n_] = n
        S = {n: sem("c_" + n) for n in per}
        s0_in = [sem(f"s0_in{r}") for r in range(3)]
        s1_out = [sem(f"s1_out{r}") for r in range(3)]
        page_in = [sem(f"page_landed{r}") for r in range(8)]
        sc_in, vn_in, wa_in, pg_in, st_out, og_out, zero_set, qbd_zero, pad_zero = (sem(n) for n in
            ("sc_in", "vn_in", "wa_in", "pg_in2", "st_out", "og_out", "zero_set", "qbd_zero", "pad_zero"))
        stream.phase(TT * 2, 6, (0, 1))
        steps = schedule()

        def W(eng, name, i, k):
            eng.wait_ge(S[name], upto(i, per[name], k))

        def inc(m, name):
            m.then_inc(S[name], 1)

        def run(eng, handlers, i):
            reg = eng.alloc_register("turn")
            mine = [st for st in steps if st[0] in handlers]
            for n, st in enumerate(mine):
                if n % 6 == 0:
                    eng.reg_mov(reg, i)
                    turn = eng.snap(reg, min_val=0, max_val=GH - 1)
                handlers[st[0]](turn, *st[1:])

        def v_lo_name(m):
            return ("v_even_lo", "v_odd_lo")[m % 2]

        def kv(t, m):
            return t[:, m // 2 % 2, :, m % 2, :]

        def quarters(a):
            return a.rearrange("p (k c) -> p k c", k=NHP)

        def wait_page(eng, i, q, x):
            eng.wait_ge(page_in[x % 8], i * (16 * 16) + 16 * (q * 8 + x // 8 + 1))

        def split_at(g):
            return 2 if g == 0 else 2 * g if 2 <= g < NPG // 2 else None

        def slot_uses(r):
            return 2 if r % 3 == 0 else 1

        def wait_k_slot(eng, i, q, p):
            if p >= 4:
                W(eng, "sc_mm", i, q * (NPG // 2) + p // 2 - 1)
            else:
                W(eng, "pv", i, (q - 1) * NPG + NPG - 3 + p if q else 0)

        def wait_v_slot(eng, i, q, m):
            if m >= 4:
                W(eng, "pv", i, q * NPG + m - 3)
            else:
                W(eng, "sc_mm", i, q * (NPG // 2) + NPG // 2 - 1 + m // 2)

        rows = [slice(0, HD), slice(HD, P)]

        with nc.Block() as block:
            @block.sync
            def _(sp):
                sp.dma_start(pages[:, 0:NB * NPG], ins["page_table"]).then_inc(pg_in, 16)
                sp.dma_start(wa_all, ins["w_a2"].rearrange("g r c -> r g c")).then_inc(wa_in, 16)
                sp.wait_ge(pg_in, 16)
                sp.wait_ge(pad_zero, 1)
                for s in (st_out, og_out, *s1_out):
                    sp.sem_inc(s, 16)

                def load(i, q, x):
                    y, u = (x - 8, q) if x >= 8 else (x + 56, q - 1)
                    if y < 0 or u < 0:
                        pass
                    elif y < NPG:
                        W(sp, "kt_mm", i, u * NPG + y + 1)
                    else:
                        W(sp, v_lo_name(y), i, u * (NPG // 2) + (y - NPG) // 2 + 1)
                    m = x - NPG
                    p = x if x < NPG else m // 2 + (NPG // 2) * (m % 2)
                    src = sp.value_load(pages[0:1, ds(i * (2 * NPG) + (q * NPG + p), 1)], min_val=0, max_val=NPHYS - 1)
                    cache = ins["cache_k" if x < NPG else "cache_v"]
                    sp.dma_start(page[x % 8][:], cache[ds(src, 1)].rearrange("o p c -> (o p) c")).then_inc(page_in[x % 8], 16)

                def prep(i, q):
                    W(sp, "pt_mm", i, NPG // 2 * q)
                    for half in range(2):
                        for h in range(H):
                            src = scratch["bias"][ds(i * (2 * H) + (q * H + h), 1), half * HALF:(half + 1) * HALF]
                            sp.dma_start(sc[half * NSAMP + h * TS:half * NSAMP + (h + 1) * TS, 0:HALF],
                                         src.to_broadcast([TS, HALF])).then_inc(sc_in, 16)

                def vn_load(i, q):
                    W(sp, "od_mm", i, q)
                    sp.dma_start(vn_raw, outs["v_s"].rearrange("a b t h d -> (a b) t (h d)")[ds(i * 2 + q, 1)]
                                 .rearrange("o t c -> (o t) c")).then_inc(vn_in, 16)

                def kstep(i, q, p):
                    if p < NPG:
                        load(i, q, p + 8)

                def vstep(i, q, g):
                    for x in (NPG + 8 + 2 * g, NPG + 9 + 2 * g):
                        if x < 2 * NPG:
                            load(i, q, x)
                        elif x < 2 * NPG + 8:
                            load(i, q + 1, x - 2 * NPG)

                def z(i, n, c, part):
                    if c == 0 and part == 1:
                        stream.load(sp, i, n)

                def state_in(i, r):
                    sp.wait_ge(s1_out[r % 3], i * (32 * slot_uses(r)) + 32 * (r // 3) + 16)
                    for j in range(2):
                        src = ins["state"][2 * r + j, ds(i, 1)].rearrange("o k v -> (o k) v")
                        sp.dma_start(s0[:, r % 3, j, :], src).then_inc(s0_in[r % 3], 16)

                def state_out(i, r):
                    W(sp, "s1_set", i, 2 * r + 2)
                    for j in range(2):
                        dst = outs["gla_s"][0, 2 * r + j, ds(i, 1)].rearrange("o k v -> (o k) v")
                        sp.dma_start(dst, s0[:, r % 3, j, :]).then_inc(s1_out[r % 3], 16)

                def att_step(i, t):
                    if t == TT - 1:
                        for r in range(3):
                            state_in(i, r)

                def satt(i):
                    W(sp, "st_set", i, 2 * TT)
                    dst = outs["gla_p"][0, 0, ds(i, 1)].rearrange("o k v -> (o k) v")
                    sp.dma_start(dst, state[:, 2 * TT % 3, :]).then_inc(st_out, 16)

                def sstate(i, r):
                    state_out(i, r)
                    if r == 1:
                        state_in(i, 3)

                def end(i):
                    W(sp, "gated", i, GTS)
                    sp.dma_start(scratch["ogla"][ds(i, 1)].rearrange("o p a t -> (o p) a t"), gate[:]).then_inc(og_out, 16)

                for x in range(8):
                    load(0, 0, x)
                with sp.Fori(0, GH) as i:
                    run(sp, {"prep": prep, "vn_load": vn_load, "k": kstep, "v": vstep, "z": z, "att": att_step, "satt": satt,
                             "sstate": sstate, "end": end}, i)
                for x in range(8):
                    sp.wait_ge(page_in[x], GH * (16 * 16) + 16)
                sp.wait_ge(st_out, GH * 16 + 16)
                sp.wait_ge(og_out, GH * 16 + 16)
                for r in range(3):
                    sp.wait_ge(s1_out[r], GH * 32 * slot_uses(r) + 16)

            @block.gpsimd
            def _(pool):
                opened(pool, S["v_even_lo"])
                pool.memset(q_diag[:], 0.0).then_inc(zero_set, 1)

                def low(i, q, m):
                    W(pool, "v_hi_set", i, q * NPG + m + 1)
                    inc(pool.tensor_tensor(kv(kv_lo, m), quarters(page[m % 8][:]), kv(kv_hi, m).bitcast(F32),
                                           ALU.subtract), "v_even_lo")

                def kstep(i, q, p):
                    if p == NPG:
                        low(i, q, 0)

                def vstep(i, q, g):
                    if split_at(g):
                        low(i, q, split_at(g))

                with pool.Fori(0, GH) as i:
                    run(pool, {"k": kstep, "v": vstep}, i)

            @block.scalar
            def _(act):
                opened(act, *(S[n] for n in ("dc_abs dc_exp dc_ln vt_set kd_set eb_set en_set el_set ed_set g_abs g_exp g_ln g_sig ss_set "
                                             "sl_set sr_set kt_hi_set qb_hi exp2 pt_hi pn_set v_hi_set u_set").split()))
                A = act.activation

                def qbd(i, q):
                    W(act, "new_mm", i, q)
                    act.wait_ge(qbd_zero, 1)
                    for half in range(2):
                        dst = q_bd[rows[half]].rearrange("p a b c -> p (a b c)")[:, half * TS:]
                        inc(A(diag(dst, 2 * NSAMP + 2 * TS, NHP), q_s[rows[half], :, ds(i * (2 * TS) + q * TS, TS)], ACT.Copy), "qb_hi")

                def v_high(i, q, m):
                    wait_page(act, i, q, NPG + m)
                    wait_v_slot(act, i, q, m)
                    inc(A(kv(kv_hi, m), quarters(page[m % 8][:]), ACT.Copy), "v_hi_set")

                def kstep(i, q, p):
                    if p < NPG:
                        n = q * NPG + p
                        W(act, "kt_mm", i, n + 1)
                        wait_k_slot(act, i, q, p)
                        inc(A(kv(kv_hi, p), quarters(bank[3 + n % 2]), ACT.Copy), "kt_hi_set")
                    else:
                        v_high(i, q, p - NPG)

                def exp(i, q):
                    W(act, "mx4", i, q + 1)
                    inc(A(sc[:], sc[:], ACT.Exp, bias=smst[:, 2:3], accum_out=smst[:, 4:5]), "exp2")

                def vstep(i, q, g):
                    if g < NPG // 2:
                        u = q * (NPG // 2) + g
                        W(act, "pt_mm", i, u + 1)
                        W(act, "pv", i, max(2 * u - 4, NPG * q))
                        inc(A(p_t[:, g % 3, :, 0, :], bank[3 + u % 2][:, 0:P].rearrange("p (h r) -> p h r", h=2),
                              ACT.Copy), "pt_hi")
                        if split_at(g):
                            v_high(i, q, split_at(g))
                            v_high(i, q, split_at(g) + 1)
                def pn(i, q):
                    W(act, "pn_mm", i, q + 1)
                    W(act, "pvn", i, q)
                    inc(A(pn_t[:], bank[5][0:TS, 0:NSAMP], ACT.Copy), "pn_set")

                def out(i, q):
                    W(act, "pv", i, NPG * (q + 1))
                    W(act, "pvn", i, q + 1)
                    W(act, "dn3", i, q + 1)
                    W(act, "od_mm", i, q)
                    inc(A(u_lo, bank[6][NSAMP:P, :], ACT.Identity, scale=smst[NSAMP:P, 6:7]), "u_set")

                def decay(i, c):
                    w = CHUNKS[c][1]
                    W(act, "dc_mm", i, c + 1)
                    W(act, "ba_set", i, 1)
                    W(act, "dc_y", i, c)
                    act.wait_ge(stream.z_read, upto(i, 18, 0, 3 * 16))
                    inc(A(t1[:, 0:w], bank[2][:, 0:w], ACT.Abs, bias=ba[:]), "dc_abs")
                    W(act, "dc_abs", i, c + 1)
                    inc(A(t1[:, 0:w], t1[:, 0:w], ACT.Exp, scale=-1.0), "dc_exp")
                    W(act, "dc_exp", i, c + 1)
                    inc(A(t1[:, 0:w], t1[:, 0:w], ACT.Ln, bias=1.0), "dc_ln")

                def dec_last(i):
                    W(act, "dc_cum", i, 3)
                    W(act, "o_mm", i, 0)
                    inc(A(q_in[:], kdec[:], ACT.Exp, scale=1.0 / TAU), "eb_set")
                    W(act, "bl_set", i, 2)
                    W(act, "st_set", i, 0)
                    W(act, "s1_set", i, 0)
                    inc(A(e_last[:], b_last[:], ACT.Exp, scale=1.0 / TAU), "el_set")

                def dec_neg(i):
                    W(act, "v_turned", i, 6)
                    inc(A(k_in[:], kdec[:], ACT.Exp, scale=-1.0 / TAU), "en_set")

                def dec_end(i):
                    W(act, "dd_set", i, 1)
                    inc(A(kdec[:], kdec[:], ACT.Exp, scale=1.0 / TAU), "ed_set")

                def turned(i, dst, half, p, name, mm, k):
                    W(act, mm, i, k + 1)
                    b = bank[(2, 7, 2)[p]]
                    if p < 2:
                        inc(A(dst[:, 4 * p:4 * p + 4, half * P:(half + 1) * P], b.rearrange("p (t c) -> p t c", t=4), ACT.Copy), name)
                    else:
                        inc(A(dst[0:NSAMP, TT, half * P:(half + 1) * P], b[0:NSAMP, 0:P], ACT.Copy), name)

                def vturn(i, n, p):
                    turned(i, v_tok, n, p, "vt_set", "v_turned", 3 * n + p)

                def kturn(i, p):
                    turned(i, k_tok, 0, p, "kd_set", "kd_turned", p)

                def z(i, n, c, part):
                    if c == 0 and part == 1:
                        stream.split_hi(act, i, n)

                def evac(i, n, c):
                    if n >= G0:
                        w = CHUNKS[c][1]
                        act.wait_ge(stream.projected, stream.chunk(i, n, c))
                        act.wait_ge(stream.z_read, i * 18 + 3 * 16 + 3 * n + c + 1)
                        sigmoid_act(act, lambda name: W(act, name, i, 3 * (n - G0) + c + 1), inc, stream.bank_of(n, c), t1[:, 0:w])

                def ostat(i, t, w):
                    W(act, "o_mm", i, t + 1)
                    W(act, "ot_mm", i, t)
                    inc(A(o_n[0:w], bank[7][0:w, P:P + DV], ACT.Square, accum_out=ost[0:w, 0:1]), "ss_set")
                    W(act, "ss_set", i, t + 1)
                    inc(A(ost[0:w, 1:2], ost[0:w, 0:1], ACT.Ln, bias=epsb[0:w], scale=1.0 / DV), "sl_set")
                    W(act, "sl_set", i, t + 1)
                    inc(A(ost[0:w, 2:3], ost[0:w, 1:2], ACT.Exp, scale=-0.5), "sr_set")

                with act.Fori(0, GH) as i:
                    run(act, {"prep": lambda i, q: None if q else qbd(i, q), "qbd": qbd, "pn": pn, "k": kstep, "exp": exp, "v": vstep,
                              "out": out, "decay": decay, "dec_last": dec_last, "dec_neg": dec_neg, "dec_end": dec_end, "vturn": vturn, "kturn": kturn, "z": z, "evac": evac,
                              "o": lambda i, t: ostat(i, t, P), "so": lambda i: ostat(i, TT, NSAMP)}, i)

            @block.vector
            def _(dve):
                opened(dve, *(S[n] for n in ("dc_min dc_y dc_cum bl_set dd_set ba_set wa_set st_zero kin_set g_y att_min "
                                             "att_set st_set on_set gated qd_set kr_set s1_set kt_lo_set v_odd_lo s_add1 s_add n_add1 n_add "
                                             "pad_set qb_lo mx1 mx2 mx3 mx4 dn1 dn2 dn3 pt_lo od_set od_g").split()))
                dve.memset(pages[:, NB * NPG:].bitcast(F32), 0.0).then_inc(pad_zero, 1)
                dve.memset(q_bd[:].bitcast(F32), 0.0).then_inc(qbd_zero, 1)
                dve.wait_ge(qbd_zero, 1)
                T = dve.tensor_tensor

                def prep(i, q):
                    W(dve, "exp2", i, q)
                    stream.pass_waits(dve)
                    inc(dve.memset(sc[NSAMP:P, HALF:HALF + TS], -BIG), "pad_set")
                    if q == 0:
                        qbd(i, q)

                def qbd(i, q):
                    W(dve, "new_mm", i, q)
                    W(dve, "qb_hi", i, 2 * q + 2)
                    for half in range(2):
                        flat = q_bd[rows[half]].rearrange("p a b c -> p (a b c)")
                        hi = diag(flat[:, half * TS:], 2 * NSAMP + 2 * TS, NHP)
                        lo = diag(flat[:, NSAMP + half * TS:], 2 * NSAMP + 2 * TS, NHP)
                        inc(T(lo, q_s[rows[half], :, ds(i * (2 * TS) + q * TS, TS)], hi.bitcast(F32), ALU.subtract), "qb_lo")

                def v_low(i, q, m):
                    W(dve, "v_hi_set", i, q * NPG + m + 1)
                    inc(T(kv(kv_lo, m), quarters(page[m % 8][:]), kv(kv_hi, m).bitcast(F32), ALU.subtract), "v_odd_lo")

                def kstep(i, q, p):
                    if p < NPG:
                        n = q * NPG + p
                        W(dve, "kt_hi_set", i, n + 1)
                        inc(T(kv(kv_lo, p), quarters(bank[3 + n % 2]), kv(kv_hi, p).bitcast(F32), ALU.subtract), "kt_lo_set")
                    if p == NPG + 1:
                        v_low(i, q, 1)
                    if p >= 3 and p % 2:
                        j = (p - 3) // 2
                        n = q * (NPG // 2) + j
                        half, col = j // (NPG // 4), j % (NPG // 4) * 2 * PAGE
                        dst = sc[rows[half], col:col + 2 * PAGE]
                        if p == 3:
                            dve.wait_ge(sc_in, i * 512 + 256 * (q + 1))
                        W(dve, "sc_mm", i, n + 1)
                        inc(T(dst, bank[5 + n % 2][0:NSAMP, 0:2 * PAGE], dst, ALU.add), "s_add1")
                        W(dve, "s_add1", i, n + 1)
                        inc(T(dst, bank[5 + n % 2][NSAMP:P, 0:2 * PAGE], dst, ALU.add), "s_add")

                def soft(i, q):
                    new = sc[0:NSAMP, HALF:HALF + TS]
                    W(dve, "new_mm", i, q + 1)
                    inc(T(new, bank[5][0:NSAMP, 0:TS], newb[:, ds(i * (2 * TS) + q * TS, TS)], ALU.add), "n_add1")
                    W(dve, "n_add1", i, q + 1)
                    inc(T(new, bank[5][NSAMP:P, 0:TS], new, ALU.add), "n_add")
                    W(dve, "n_add", i, q + 1)
                    W(dve, "s_add", i, NPG // 2 * (q + 1))
                    W(dve, "pad_set", i, q + 1)
                    inc(dve.tensor_reduce(smst[:, 0:1], sc[:], AX_X, ALU.max), "mx1")
                    W(dve, "mx1", i, q + 1)
                    inc(dve.tensor_copy(smst[0:NSAMP, 1:2], smst[NSAMP:P, 0:1]), "mx2")
                    W(dve, "mx2", i, q + 1)
                    inc(dve.tensor_scalar(smst[0:NSAMP, 2:3], smst[0:NSAMP, 0:1], smst[0:NSAMP, 1:2], -1.0, ALU.max, ALU.mult), "mx3")
                    W(dve, "mx3", i, q + 1)
                    inc(dve.tensor_copy(smst[NSAMP:P, 2:3], smst[0:NSAMP, 2:3]), "mx4")

                def total(i, q):
                    W(dve, "exp2", i, q + 1)
                    inc(dve.tensor_copy(smst[0:NSAMP, 5:6], smst[NSAMP:P, 4:5]), "dn1")
                    W(dve, "dn1", i, q + 1)
                    inc(T(smst[0:NSAMP, 7:8], smst[0:NSAMP, 4:5], smst[0:NSAMP, 5:6], ALU.add), "dn2")
                    W(dve, "dn2", i, q + 1)
                    dve.reciprocal(smst[0:NSAMP, 6:7], smst[0:NSAMP, 7:8])
                    inc(dve.reciprocal(smst[NSAMP:P, 6:7], smst[0:NSAMP, 7:8]), "dn3")

                def vstep(i, q, g):
                    if g < NPG // 2:
                        u = q * (NPG // 2) + g
                        W(dve, "pt_hi", i, u + 1)
                        inc(T(p_t[:, g % 3, :, 1, :], bank[3 + u % 2][:, 0:P].rearrange("p (h r) -> p h r", h=2),
                              p_t[:, g % 3, :, 0, :].bitcast(F32), ALU.subtract), "pt_lo")
                        if split_at(g):
                            v_low(i, q, split_at(g) + 1)

                def out(i, q):
                    W(dve, "u_set", i, q + 1)
                    inc(dve.scalar_tensor_tensor(out=u_lo, in0=bank[6][0:NSAMP, :], scalar=smst[0:NSAMP, 6:7], in1=u_lo,
                                                 op0=ALU.mult, op1=ALU.add), "od_set")

                def gate_out(i, q):
                    W(dve, "od_mm", i, q + 1)
                    for half in range(2):
                        src = diag(bank[5][rows[half], half * TS:], NSAMP + 2 * TS, NHP)
                        dst = os_fm[rows[half], :, ds(i * (2 * TS) + q * TS, TS)]
                        m = T(dst, src, dst, ALU.mult)
                    inc(m, "od_g")

                def start(i):
                    W(dve, "dc_ln", i, 0)
                    W(dve, "o_mm", i, 0)
                    o, _ = VEC_W["b_a"]
                    inc(dve.tensor_copy(ba[:], vv("b_a", P, 0, GH)[:, ds(i, 1)]), "ba_set")
                    W(dve, "dc_mm", i, 0)
                    dve.wait_ge(wa_in, 16)
                    inc(dve.tensor_copy(wa[:].unsqueeze(1), wa_all[:, ds(i, 1), :]), "wa_set")
                    W(dve, "ba_set", i, 1)
                    inc(dve.memset(state[:, 0, :], 0.0), "st_zero")

                def decay(i, c):
                    t0, w = CHUNKS[c]
                    y = kdec[:, t0:t0 + w]
                    W(dve, "dc_abs", i, c + 1)
                    W(dve, "kd_turned", i, 0)
                    inc(dve.tensor_scalar(y, bank[2][:, 0:w], ba[:], 0.0, ALU.add, ALU.min), "dc_min")
                    W(dve, "dc_min", i, c + 1)
                    W(dve, "dc_ln", i, c + 1)
                    inc(T(y, y, t1[:, 0:w], ALU.subtract), "dc_y")
                    W(dve, "dc_y", i, c + 1)
                    inc(dve.tensor_tensor_scan(y, cc("scan" if c < 2 else "scan_last"), y, 0.0, ALU.mult, ALU.add), "dc_cum")

                main = kdec[:, 0:SEQ].rearrange("p (c t) -> p c t", t=CH)
                tail = kdec[:, SEQ:NT].rearrange("p (c t) -> p c t", t=TS)
                np_ = SEQ // CH

                def dec_last(i):
                    W(dve, "dc_cum", i, 3)
                    W(dve, "el_set", i, 0)
                    inc(dve.tensor_copy(b_last[:, 0:np_].unsqueeze(2), main[:, :, CH - 1:CH]), "bl_set")
                    inc(dve.tensor_copy(b_last[:, np_:].unsqueeze(2), tail[:, :, TS - 1:TS]), "bl_set")

                def dec_diff(i):
                    W(dve, "bl_set", i, 2)
                    W(dve, "eb_set", i, 1)
                    W(dve, "en_set", i, 1)
                    T(main, b_last[:, 0:np_].unsqueeze(2).to_broadcast([P, np_, CH]), main, ALU.subtract)
                    inc(T(tail, b_last[:, np_:].unsqueeze(2).to_broadcast([P, NB, TS]), tail, ALU.subtract), "dd_set")

                def z(i, n, c, part):
                    if c == 0 and part == 1:
                        stream.split_lo(dve, i, n)

                def evac(i, n, c):
                    t0, w = CHUNKS[c]
                    zb = stream.bank_of(n, c)
                    dve.wait_ge(stream.projected, stream.chunk(i, n, c))
                    if n in (V0, V1):
                        W(dve, "v_turned", i, 3 * n)
                        W(dve, "att_mm", i, 0)
                        dve.tensor_copy(v_fm[:, t0:t0 + w], zb).then_inc(stream.z_read, 1)
                    if n == Q:
                        W(dve, "eb_set", i, 1)
                        dve.scalar_tensor_tensor(out=q_in[:, t0:t0 + w], in0=zb, scalar=DK ** -0.5, in1=q_in[:, t0:t0 + w],
                                                 op0=ALU.mult, op1=ALU.mult).then_inc(stream.z_read, 1)
                    if n == K:
                        W(dve, "ed_set", i, 1)
                        inc(T(k_in[:, t0:t0 + w], zb, k_in[:, t0:t0 + w], ALU.mult), "kin_set")
                        T(kdec[:, t0:t0 + w], zb, kdec[:, t0:t0 + w], ALU.mult).then_inc(stream.z_read, 1)
                    if n >= G0:
                        e = 3 * (n - G0) + c
                        sigmoid_dve(dve, lambda name: W(dve, name, i, e + 1), inc, zb, t1[:, 0:w])
                        W(dve, "g_sig", i, e + 1)
                        dve.wait_ge(og_out, i * 16 + 16)
                        T(gate[:, n - G0, t0:t0 + w], zb, t1[:, 0:w], ALU.mult).then_inc(stream.z_read, 1)

                def att_mask(i, t, w, hi, lo):
                    W(dve, "att_mm", i, t + 1)
                    W(dve, "o_mm", i, t)
                    inc(T(att[0:w, 0:w], bank[7][0:w, 0:w], cc(hi, w), ALU.min), "att_min")
                    W(dve, "att_min", i, t + 1)
                    inc(T(att[0:w, 0:w], att[0:w, 0:w], cc(lo, w), ALU.max), "att_set")

                def att_step(i, t):
                    att_mask(i, t, P, "glamax", "glamin")
                    W(dve, "u_mm", i, t + 1)
                    if t == 0:
                        W(dve, "el_set", i, 1)
                        W(dve, "st_zero", i, 1)
                        dve.wait_ge(st_out, i * 16 + 16)
                    for j in range(2):
                        c = 2 * t + j
                        W(dve, "st_set", i, c)
                        inc(dve.scalar_tensor_tensor(out=state[:, (c + 1) % 3, :], in0=state[:, c % 3, :], scalar=e_last[:, c:c + 1],
                                                     in1=bank[2][:, j * DV:(j + 1) * DV], op0=ALU.mult, op1=ALU.add), "st_set")

                def o_norm(i, t, w):
                    W(dve, "sr_set", i, t + 1)
                    W(dve, "ot_mm", i, t)
                    inc(dve.tensor_scalar(o_n[0:w], bank[7][0:w, P:P + DV], ost[0:w, 2:3], None, ALU.mult), "on_set")

                def og(i, t, w):
                    W(dve, "ot_mm", i, t + 1)
                    for j in range(2):
                        dst = gate[:, j, t * P:t * P + w]
                        m = dve.scalar_tensor_tensor(out=dst, in0=bank[7][:, (0, 3 * P)[j]:(0, 3 * P)[j] + w],
                                                     scalar=vv("gla_g", P, j), in1=dst, op0=ALU.mult, op1=ALU.mult)
                    inc(m, "gated")

                def satt(i):
                    att_mask(i, TT, NSAMP, "smpmax", "smpmin")
                    dve.wait_ge(zero_set, 1)
                    inc(dve.tensor_copy(diag(q_diag[:].rearrange("p b t -> p (b t)"), NSAMP + TS, NB),
                                        q_in[:, SEQ:NT].rearrange("p (b t) -> p b t", b=NB)), "qd_set")
                    rows_of(i, 0)

                def rows_of(i, r):
                    W(dve, "su_mm", i, r - 1)
                    for j in range(2):
                        b = 2 * r + j
                        inc(dve.tensor_scalar(k_row[:, 2 * (r % 2) + j, :], k_tok[0:NSAMP, TT, :], cc("rowmask", NSAMP)[:, b:b + 1], None,
                                              ALU.mult), "kr_set")

                def sstate(i, r):
                    if r + 1 < NB // 2:
                        rows_of(i, r + 1)
                    W(dve, "su_mm", i, r + 1)
                    for j in range(2):
                        b = 2 * r + j
                        c = SEQ // CH + b
                        inc(dve.scalar_tensor_tensor(out=s0[:, r % 3, j, :], in0=s0[:, r % 3, j, :], scalar=e_last[:, c:c + 1],
                                                     in1=bank[2][:, j * DV:(j + 1) * DV], op0=ALU.mult, op1=ALU.add), "s1_set")

                with dve.Fori(0, GH) as i:
                    run(dve, {"sum": total, "prep": prep, "qbd": qbd, "k": kstep, "soft": soft, "v": vstep, "out": out, "gate": gate_out, "start": start,
                              "decay": decay, "dec_last": dec_last, "dec_diff": dec_diff, "z": z, "evac": evac, "att": att_step,
                              "o": lambda i, t: o_norm(i, t, P), "og": lambda i, t: og(i, t, P), "satt": satt,
                              "sstate": sstate, "so": lambda i: o_norm(i, TT, NSAMP), "sog": lambda i: og(i, TT, NSAMP)}, i)

            @block.tensor
            def _(pe):
                opened(pe, *(S[n] for n in ("dc_mm v_turned kd_turned att_mm o_mm u_mm u_half ot_mm su_mm kt_mm sc_mm new_mm pt_mm "
                                            "pn_mm pv pvn od_mm").split()))
                MM = pe.matmul

                def kstep(i, q, p):
                    if p < NPG:
                        n = q * NPG + p
                        wait_page(pe, i, q, p)
                        W(pe, "kt_lo_set", i, n - 1)
                        if p < 2:
                            W(pe, "pt_lo", i, q * (NPG // 2))
                        for hp in range(NHP):
                            m = pe.transpose(bank[3 + n % 2][:, hp * P:(hp + 1) * P], page[p % 8][:, hp * P:(hp + 1) * P], cc("ident"))
                        inc(m, "kt_mm")
                    if p >= 3 and p % 2:
                        j = (p - 3) // 2
                        n = q * (NPG // 2) + j
                        W(pe, "kt_lo_set", i, q * NPG + 2 * j + 2)
                        W(pe, "s_add", i, n - 1)
                        if j == 0:
                            W(pe, "qb_lo", i, 2 * q + 2)
                            W(pe, "od_g", i, q)
                        if j == 1:
                            W(pe, "od_set", i, q)
                        for k, kt in enumerate((kv_hi, kv_lo)):
                            for hp in range(NHP):
                                m = MM(bank[5 + n % 2][:, 0:2 * PAGE], q_bd[:, hp].rearrange("p a c -> p (a c)"),
                                       kt[:, j % 2, hp].rearrange("p a c -> p (a c)"), start=(k == 0 and hp == 0), stop=(k == 1 and hp == 3))
                        inc(m, "sc_mm")

                def soft(i, q):
                    W(pe, "s_add", i, NPG // 2 * (q + 1) - 1)
                    b8 = ds(i * (2 * TS) + q * TS, TS)
                    for k, kt in enumerate((k_s_hi, k_s_lo)):
                        for hp in range(NHP):
                            m = MM(bank[5][:, 0:TS], q_bd[:, hp].rearrange("p a c -> p (a c)"), kt[:, hp, b8],
                                   start=(k == 0 and hp == 0), stop=(k == 1 and hp == 3))
                    inc(m, "new_mm")

                def vstep(i, q, g):
                    if g < NPG // 2:
                        u = q * (NPG // 2) + g
                        W(pe, "exp2", i, q + 1)
                        W(pe, "pt_lo", i, u - 1)
                        if g < 2:
                            W(pe, "kt_lo_set", i, NPG * (q + 1))
                        inc(pe.transpose(bank[3 + u % 2][:, 0:P], sc[:, g * P:(g + 1) * P], cc("ident")), "pt_mm")
                    if g >= 2:
                        u = q * (NPG // 2) + g - 2
                        W(pe, "pt_lo", i, u + 1)
                        for h in range(2):
                            page_ = 2 * (g - 2) + h
                            W(pe, v_lo_name(h), i, u + 1)
                            if g == 2:
                                W(pe, "s_add", i, NPG // 2 * (q + 1))
                            for k, v in enumerate((kv_hi, kv_lo)):
                                m = MM(quarters(bank[6]), p_t[:, (g - 2) % 3, h].rearrange("p a c -> p (a c)"), kv(v, page_),
                                       start=(g == 2 and h == 0 and k == 0), stop=(page_ == NPG - 1 and k == 1))
                            inc(m, "pv")

                def pn(i, q):
                    W(pe, "n_add", i, q + 1)
                    stream.pass_waits(pe)
                    inc(pe.transpose(bank[5][0:TS, 0:NSAMP], sc[0:NSAMP, HALF:HALF + TS], cc("ident", NSAMP)[:, 0:NSAMP]), "pn_mm")

                def pnv(i, q):
                    W(pe, "pn_set", i, q + 1)
                    pe.wait_ge(vn_in, i * 32 + 16 * (q + 1))
                    stream.pass_waits(pe)
                    inc(MM(bank[6][0:NSAMP, :], pn_t[:], vn_raw, start=False, stop=False, skip_group_check=True), "pvn")

                def gate_out(i, q):
                    W(pe, "od_set", i, q + 1)
                    stream.pass_waits(pe)
                    for hp in range(NHP):
                        m = pe.transpose(bank[5][:, hp * NSAMP:(hp + 1) * NSAMP], u_lo[:, hp * P:(hp + 1) * P],
                                         cc("ident", NSAMP)[:, 0:NSAMP])
                    inc(m, "od_mm")

                def decay(i, c):
                    t0, w = CHUNKS[c]
                    W(pe, "wa_set", i, 1)
                    W(pe, "dc_min", i, c)
                    W(pe, "s1_set", i, 0)
                    stream.pass_waits(pe)
                    inc(MM(bank[2][:, 0:w], wa[:], glr[:, t0:t0 + w], start=True, stop=True), "dc_mm")

                def turn(i, src, p, name, done, k):
                    W(pe, done, i, k - 1)
                    if p == 0:
                        W(pe, "dc_min", i, 3)
                        W(pe, "gated", i, 0)
                    stream.pass_waits(pe)
                    for t in (range(4 * p, 4 * p + 4) if p < 2 else [TT]):
                        n = P if t < TT else NSAMP
                        m = pe.transpose(bank[(2, 7, 2)[p]][0:n, (t % 4) * P:(t % 4) * P + P], src[:, t * P:t * P + n], cc("ident"))
                    inc(m, name)

                def vturn(i, n, p):
                    pe.wait_ge(stream.z_read, stream.chunk(i, n, 2))
                    W(pe, "vt_set", i, 3 * n + p - 1)
                    turn(i, v_fm, p, "v_turned", "vt_set", 3 * n + p)

                def kturn(i, p):
                    pe.wait_ge(stream.z_read, stream.chunk(i, K, 2))
                    W(pe, "vt_set", i, 6)
                    turn(i, kdec, p, "kd_turned", "kd_set", p)

                def z(i, n, c, part):
                    stream.project(pe, i, n, c, range(part * KT_ // PARTS, (part + 1) * KT_ // PARTS))

                def att_step(i, t):
                    if t == 0:
                        W(pe, "vt_set", i, 6)
                        W(pe, "kd_set", i, 3)
                        W(pe, "kin_set", i, 3)
                    tok = slice(t * P, (t + 1) * P)
                    W(pe, "st_set", i, 2 * t)
                    for j in range(2):
                        if j == 1:
                            W(pe, "gated", i, t)
                            inc(MM(bank[7][:, 0:P], k_in[:, tok], q_in[:, tok], start=True, stop=True), "att_mm")
                            W(pe, "u_half", i, t + 1)
                        m = MM(bank[2][:, j * DV:(j + 1) * DV], k_tok[rows[j], t, :], v_tok[rows[j], t, :], start=True, stop=True)
                        inc(m, ("u_half", "u_mm")[j])

                def o_step(i, t):
                    W(pe, "att_set", i, t + 1)
                    MM(bank[7][:, P:P + DV], att[:], v_tok[:, t, :], start=True, stop=False, skip_group_check=True)
                    W(pe, "st_set", i, 2 * t + 1)
                    for j in range(2):
                        c = 2 * t + j
                        m = MM(bank[7][rows[j], P:P + DV], q_in[:, c * CH:(c + 1) * CH], state[:, c % 3, :], start=False,
                               stop=(j == 1), skip_group_check=True)
                    inc(m, "o_mm")

                def og(i, t, w):
                    W(pe, "on_set", i, t + 1)
                    stream.pass_waits(pe)
                    for j in range(2):
                        m = pe.transpose(bank[7][:, (0, 3 * P)[j]:(0, 3 * P)[j] + w], o_n[0:w, j * P:(j + 1) * P],
                                         cc("ident", w)[:, 0:w])
                    inc(m, "ot_mm")

                def satt(i):
                    W(pe, "gated", i, TT)
                    stream.pass_waits(pe)
                    inc(MM(bank[7][0:NSAMP, 0:NSAMP], k_in[:, SEQ:NT], q_in[:, SEQ:NT], start=True, stop=True), "att_mm")

                def sstate(i, r):
                    if r == 0:
                        W(pe, "att_set", i, TT + 1)
                        W(pe, "qd_set", i, 1)
                        W(pe, "st_set", i, 2 * TT)
                        stream.pass_waits(pe)
                        MM(bank[7][0:NSAMP, P:P + DV], att[0:NSAMP, 0:NSAMP], v_tok[0:NSAMP, TT, :], start=True, stop=False,
                           skip_group_check=True)
                    pe.wait_ge(s0_in[r % 3], i * (32 * slot_uses(r)) + 32 * (r // 3 + 1))
                    W(pe, "s1_set", i, 2 * r)
                    W(pe, "kr_set", i, 2 * r + 2)
                    stream.pass_waits(pe)
                    for j in range(2):
                        m = MM(bank[7][0:NSAMP, P:P + DV], q_diag[:, 2 * r + j, :], s0[:, r % 3, j, :], start=False,
                               stop=(r == 3 and j == 1), skip_group_check=True)
                    if r == 3:
                        inc(m, "o_mm")
                    for j in range(2):
                        m = MM(bank[2][:, j * DV:(j + 1) * DV], k_row[:, 2 * (r % 2) + j, :], v_tok[0:NSAMP, TT, :], start=True, stop=True)
                    inc(m, "su_mm")

                with pe.Fori(0, GH) as i:
                    run(pe, {"k": kstep, "soft": soft, "v": vstep, "pn": pn, "pnv": pnv, "gate": gate_out, "decay": decay, "vturn": vturn,
                             "kturn": kturn, "z": z, "att": att_step, "o": o_step, "og": lambda i, t: og(i, t, P),
                             "satt": satt, "sstate": sstate, "sog": lambda i: og(i, TT, NSAMP)}, i)


def build_merge(nc, ins, outs, scratch, sem, sb, bank, cc, stream, os_fm):
    NA, NBR = NHP, 2 * GH
    MT = KT_ // 2
    with ExitStack() as ctx:
        fox_o = sb(ctx, "fox_o", [P, NA, NT])
        gla_o = sb(ctx, "gla_o", [P, NBR, NT])
        m_fm = sb(ctx, "m_fm", [P, KT_, NT])
        up_a = sb(ctx, "up_a", [P, NA, P])
        up_b = sb(ctx, "up_b", [P, NBR, P])
        g_a = sb(ctx, "g_a", [P, NT])
        g_b = sb(ctx, "g_b", [P, NT])
        flat = gla_o[:].rearrange("p a t -> p (a t)")
        yw = (TT + 1) * P
        y_fm = [flat[:, s * NT:(s + 1) * NT] for s in range(2)]
        x_tok, y_tok = ([flat[:, 2 * NT + (2 * a + s) * yw:2 * NT + (2 * a + s + 1) * yw].rearrange("p (t c) -> p t c", c=P)
                         for s in range(2)] for a in range(2))

        per = {"g_abs": 12, "g_exp": 12, "g_ln": 12, "g_y": 12, "g_sig": 12, "a_mm": 6, "b_mm": 6, "a_read": 6, "b_read": 6, "m_set": 6,
               "y_turned": 6, "y_set": 6}
        S = {n: sem("d_" + n) for n in per}
        o_in, up_a_in, up_b_in, os_in, m_hi, m_lo, m_lo_last = (sem(n) for n in
            ("o_in", "up_a_in", "up_b_in", "os_in", "m_hi", "m_lo", "m_lo_last"))
        x_in = [sem(f"xr_in{s}") for s in range(2)]
        y_out = [sem(f"y_out{s}") for s in range(2)]
        base = 4 * NHP + 6 * GH

        def gates_phase():
            stream.phase(base, 4, (0, 1))

        def output_phase():
            stream.phase(base + 2 * KT_, 2, (0, 1))

        xp = ins["x_prompt"].rearrange("a l d -> (a l) d")
        xs = ins["x_sample"].rearrange("b l d -> (b l) d")
        yp = outs["y_p"].rearrange("a l d -> (a l) d")
        ys = outs["y_s"].rearrange("b l d -> (b l) d")

        def W(eng, name, i, k):
            eng.wait_ge(S[name], upto(i, per[name], k))

        def inc(m, name):
            m.then_inc(S[name], 1)

        with nc.Block() as block:
            @block.sync
            def _(sp):
                for k in range(NA):
                    sp.dma_start(fox_o[:, k, 0:SEQ], scratch["ofox"][k]).then_inc(o_in, 16)
                for k in range(GH):
                    sp.dma_start(gla_o[:, 2 * k:2 * k + 2, :], scratch["ogla"][k]).then_inc(o_in, 16)
                gates_phase()
                with sp.Fori(0, MT) as i:
                    for s in range(2):
                        W(sp, "a_mm", i, 3 * s)
                        sp.dma_start(up_a[:], ins["w_up_a"][ds(i * 2 + s, 1)].rearrange("o p k c -> (o p) k c")).then_inc(up_a_in, 16)
                        W(sp, "b_mm", i, 3 * s)
                        sp.dma_start(up_b[:], ins["w_up_b"][ds(i * 2 + s, 1)].rearrange("o p k c -> (o p) k c")).then_inc(up_b_in, 16)
                        for n in range(2):
                            stream.load(sp, i, 2 * s + n)
                W(sp, "b_mm", MT, 0)
                output_phase()
                for s in range(2):
                    sp.sem_inc(y_out[s], 16)
                with sp.Fori(0, MT) as i:
                    for s in range(2):
                        col = ds(i * (2 * P) + s * P, P)
                        stream.load(sp, i, s)
                        W(sp, "y_set", i, 3 * (s - 1) if s else 0)
                        sp.dma_start(x_tok[s][:, 0:TT, :], xp[:, col].rearrange("(t p) c -> p t c", p=P)).then_inc(x_in[s], 16)
                        sp.dma_start(x_tok[s][0:NSAMP, TT, :], xs[:, col]).then_inc(x_in[s], 16)
                    for s in range(2):
                        col = ds(i * (2 * P) + s * P, P)
                        W(sp, "y_set", i, 3 * s + 3)
                        sp.dma_start(yp[:, col].rearrange("(t p) c -> p t c", p=P), y_tok[s][:, 0:TT, :]).then_inc(y_out[s], 16)
                        sp.dma_start(ys[:, col], y_tok[s][0:NSAMP, TT, :]).then_inc(y_out[s], 16)
                for s in range(2):
                    sp.wait_ge(y_out[s], 16 + MT * 32)
                    sp.wait_ge(stream.loaded[s], (base + 3 * KT_ + 2) // 2 * 16)

            @block.gpsimd
            def _(pool):
                for k in range(KT_ - 1):
                    pool.wait_ge(m_hi, k + 1)
                    pool.tensor_tensor(stream.h_lo[:, k, :], m_fm[:, k, :], stream.h_hi[:, k, :].bitcast(F32),
                                       ALU.subtract).then_inc(m_lo, 1)

            @block.scalar
            def _(act):
                opened(act, *(S[n] for n in ("g_abs", "g_exp", "g_ln", "g_sig")))
                act.activation(fox_o[:, :, SEQ:NT], os_fm[:], ACT.Copy).then_inc(os_in, 1)
                gates_phase()
                with act.Fori(0, MT) as i:
                    for s in range(2):
                        for n, g in enumerate((g_a, g_b)):
                            stream.split_hi(act, i, 2 * s + n)
                            for c, (t0, w) in enumerate(CHUNKS):
                                act.wait_ge(stream.projected, stream.chunk(i, 2 * s + n, c))
                                W(act, "m_set", i, 3 * (s - 1) + c + 1 if s else 0)
                                sigmoid_act(act, lambda name: W(act, name, i, 6 * s + 3 * n + c + 1), inc,
                                            stream.bank_of(2 * s + n, c), g[:, t0:t0 + w])
                act.wait_ge(stream.projected, stream.chunk(MT - 1, 3, 2))
                W(act, "m_set", MT - 1, 3)
                for k in range(KT_ - 1):
                    act.activation(stream.h_hi[:, k, :], m_fm[:, k, :], ACT.Copy).then_inc(m_hi, 1)
                for c, (t0, w) in enumerate(CHUNKS):
                    W(act, "m_set", MT - 1, 3 + c + 1)
                    act.activation(stream.h_hi[:, KT_ - 1, t0:t0 + w], m_fm[:, KT_ - 1, t0:t0 + w], ACT.Copy).then_inc(m_hi, 1)
                output_phase()
                with act.Fori(0, MT) as i:
                    for s in range(2):
                        stream.split_hi(act, i, s)
                        for c, (t0, w) in enumerate(CHUNKS):
                            act.wait_ge(stream.projected, stream.chunk(i, s, c))
                            W(act, "y_turned", i, 0)
                            act.activation(y_fm[s][:, t0:t0 + w], stream.bank_of(s, c), ACT.Copy).then_inc(stream.z_read, 1)

            @block.vector
            def _(dve):
                opened(dve, *(S[n] for n in ("g_y", "a_read", "b_read", "m_set", "y_set")))
                gates_phase()
                with dve.Fori(0, MT) as i:
                    for s in range(2):
                        for n, g in enumerate((g_a, g_b)):
                            stream.split_lo(dve, i, 2 * s + n)
                            for c, (t0, w) in enumerate(CHUNKS):
                                sigmoid_dve(dve, lambda name: W(dve, name, i, 6 * s + 3 * n + c + 1), inc,
                                            stream.bank_of(2 * s + n, c), g[:, t0:t0 + w])
                                W(dve, "g_y", i, 6 * s + 3 * n + c + 1)
                                dve.sem_inc(stream.z_read, 1)
                        for c, (t0, w) in enumerate(CHUNKS):
                            e = 3 * s + c
                            W(dve, "g_sig", i, 6 * s + 3 + c + 1)
                            W(dve, "a_mm", i, e + 1)
                            inc(dve.tensor_tensor(g_a[:, t0:t0 + w], bank[2 + c][:, 0:w], g_a[:, t0:t0 + w], ALU.mult), "a_read")
                            W(dve, "b_mm", i, e + 1)
                            inc(dve.tensor_tensor(g_b[:, t0:t0 + w], bank[5 + c][:, 0:w], g_b[:, t0:t0 + w], ALU.mult), "b_read")
                            W(dve, "a_read", i, e + 1)
                            W(dve, "b_read", i, e + 1)
                            inc(dve.tensor_tensor(m_fm[:, ds(i * 2 + s, 1), t0:t0 + w], g_a[:, t0:t0 + w].unsqueeze(1),
                                                  g_b[:, t0:t0 + w].unsqueeze(1), ALU.add), "m_set")
                for c, (t0, w) in enumerate(CHUNKS):
                    dve.wait_ge(m_hi, KT_ - 1 + c + 1)
                    dve.tensor_tensor(stream.h_lo[:, KT_ - 1, t0:t0 + w], m_fm[:, KT_ - 1, t0:t0 + w],
                                      stream.h_hi[:, KT_ - 1, t0:t0 + w].bitcast(F32), ALU.subtract).then_inc(m_lo_last, 1)
                output_phase()
                with dve.Fori(0, MT) as i:
                    for s in range(2):
                        stream.split_lo(dve, i, s)
                        dve.wait_ge(x_in[s], i * 32 + 32)
                        dve.wait_ge(y_out[s], i * 32 + 16)
                        for g in range(3):
                            W(dve, "y_turned", i, 3 * s + g + 1)
                            if g < 2:
                                t = slice(4 * g, 4 * g + 4)
                                inc(dve.tensor_tensor(y_tok[s][:, t, :], bank[2 + g].rearrange("p (t c) -> p t c", c=P),
                                                      x_tok[s][:, t, :], ALU.add), "y_set")
                            else:
                                inc(dve.tensor_tensor(y_tok[s][0:NSAMP, TT, :], bank[4][0:NSAMP, 0:P], x_tok[s][0:NSAMP, TT, :],
                                                      ALU.add), "y_set")

            @block.tensor
            def _(pe):
                opened(pe, *(S[n] for n in ("a_mm", "b_mm", "y_turned")))
                gates_phase()
                with pe.Fori(0, MT) as i:
                    for s in range(2):
                        for n in range(2):
                            for c in range(3):
                                stream.project(pe, i, 2 * s + n, c)
                        pe.wait_ge(os_in, 1)
                        pe.wait_ge(o_in, (NA + GH) * 16)
                        for c, (t0, w) in enumerate(CHUNKS):
                            for name, read, b0, wt, o, nk in (("a_mm", "a_read", 2, up_a, fox_o, NA),
                                                              ("b_mm", "b_read", 5, up_b, gla_o, NBR)):
                                if c == 0:
                                    pe.wait_ge(up_a_in if nk == NA else up_b_in, i * 32 + (s + 1) * 16)
                                W(pe, read, i, 3 * s + c - 2 if s else 0)
                                if s:
                                    W(pe, read, i, c + 1)
                                for k in range(nk):
                                    m = pe.matmul(bank[b0 + c][:, 0:w], wt[:, k, :], o[:, k, t0:t0 + w], start=(k == 0), stop=(k == nk - 1))
                                inc(m, name)
                pe.wait_ge(m_lo, KT_ - 1)
                pe.wait_ge(m_lo_last, 3)
                output_phase()

                def turn_y(i, s, tiles):
                    for t in tiles:
                        n = P if t < TT else NSAMP
                        if t % 4 == 0:
                            W(pe, "y_set", i, 3 * (s - 1) + t // 4 + 1 if s else 0)
                            stream.pass_waits(pe)
                        m = pe.transpose(bank[2 + t // 4][0:n, t % 4 * P:(t % 4 + 1) * P], y_fm[s][:, t * P:t * P + n], cc("ident"))
                        if t in (3, 7, TT):
                            inc(m, "y_turned")

                with pe.Fori(0, MT) as i:
                    for s in range(2):
                        for c in range(3):
                            stream.project(pe, i, s, c)
                            if c:
                                pe.wait_ge(stream.z_read, stream.chunk(i, s, c - 1))
                                turn_y(i, s, range(3 * c - 3, 3 * c))
                        pe.wait_ge(stream.z_read, stream.chunk(i, s, 2))
                        turn_y(i, s, range(6, TT + 1))


def diag(flat, step, n):
    return bass.AP(flat.tensor, flat.offset, [list(flat.ap[0]), [step, n], [1, TS]])


_OUTS = {"y_p": (1, SEQ, D), "y_s": (NB, TS, D), "k_p": (1, 1, SEQ, H, HD), "v_p": (1, 1, SEQ, H, HD),
         "logf_p": (SEQ, H), "gla_p": (1, 1, GH, DK, DV), "k_s": (1, NB, TS, H, HD), "v_s": (1, NB, TS, H, HD),
         "logf_s": (NSAMP, H), "gla_s": (1, NB, GH, DK, DV)}


def kernel(x_prompt, x_sample, cache_k, cache_v, cache_logf, state_gla, page_table, ln_g, w_in, fox_b_f,
           q_norm_g, k_norm_g, gla_w_a2, gla_b_a, gla_norm_g, w_up_a, w_up_b, w_out):
    import concourse.bacc as bacc
    from concourse.bass_utils import run_bass_kernel_spmd as run

    def f(a):
        return np.ascontiguousarray(a)

    w = np.asarray(w_in)[0].reshape(KT_, P, -1).transpose(1, 0, 2)
    at = dict(zip(("fq", "fk", "fv", "ff", "fg", "gq", "gk", "gv", "glr", "gg", "ma", "mb"),
                  np.concatenate([[0], np.cumsum((FW, FW, FW, H, FW, GH * DK, GH * DK, GH * DV, RANK, GH * DV, D))])))

    wo = np.asarray(w_out)[0].reshape(KT_, P, D).transpose(1, 0, 2)

    def tile(name, j):
        if name == "w_out":
            return wo[:, :, j * P:(j + 1) * P]
        c = at[name] + j * P
        return w[:, :, c:c + P]

    order = [(n, j) for j in range(NHP) for n in ("fv", "fk", "fq", "fg")]
    order += [t for g in range(GH) for t in (("gv", 2 * g), ("gv", 2 * g + 1), ("gq", g), ("gk", g),
                                             ("gg", 2 * g), ("gg", 2 * g + 1))]
    order += [(n, j) for j in range(KT_) for n in ("ma", "mb")]
    order += [("w_out", j) for j in (*range(KT_), 0, 1)]
    vecs = np.zeros((P, NVEC), np.float32)

    def put(name, a):
        o, c = VEC_W[name]
        vecs[:a.shape[0], o:o + c] = a
    put("ln_g", np.asarray(ln_g)[0].reshape(KT_, P).T)
    put("gq", np.tile(np.asarray(q_norm_g)[0], 2)[:, None])
    put("gk", np.tile(np.asarray(k_norm_g)[0], 2)[:, None])
    put("gla_g", np.asarray(gla_norm_g)[0].reshape(2, P).T)
    put("b_f", np.asarray(fox_b_f)[0][:, None])
    put("b_a", np.asarray(gla_b_a)[0].reshape(GH, DK).T)
    arrays = {
        "x_prompt": x_prompt, "x_sample": x_sample, "const": constants(), "vecs": vecs,
        "w_ff": w[:, :, at["ff"]:at["ff"] + H], "w_lr": w[:, :, at["glr"]:at["glr"] + RANK],
        "w_tiles": np.stack([tile(n, j) for n, j in order]),
        "w_up_a": np.asarray(w_up_a)[0].reshape(NHP, P, KT_, P).transpose(2, 1, 0, 3),
        "w_up_b": np.asarray(w_up_b)[0].reshape(KT_, P, KT_, P).transpose(2, 1, 0, 3),
        "cache_k": np.asarray(cache_k).reshape(NPHYS, PAGE, FW), "cache_v": np.asarray(cache_v).reshape(NPHYS, PAGE, FW),
        "cache_logf": np.asarray(cache_logf).reshape(NPHYS, PAGE, H),
        "state": np.asarray(state_gla)[0], "page_table": np.asarray(page_table).reshape(1, NB * NPG),
        "w_a2": np.asarray(gla_w_a2)[0].reshape(RANK, GH, DK).transpose(1, 0, 2),
    }
    nc = bacc.Bacc("TRN2", target_bir_lowering=False, num_devices=1)
    feeds, ins, outs = {}, {}, {}
    for name, a in arrays.items():
        a = f(a)
        feeds[f"in_{name}"] = a
        ins[name] = nc.dram_tensor(f"in_{name}", a.shape, mybir.dt.from_np(a.dtype), kind="ExternalInput").ap()
    for name, shape in _OUTS.items():
        outs[name] = nc.dram_tensor(f"out_{name}", shape, F32, kind="ExternalOutput").ap()
    scratch = {name: nc.dram_tensor(f"tmp_{name}", shape, F32, kind="Internal").ap() for name, shape in
               {"cum": (H, SEQ), "ncum": (H, SEQ), "cum_s": (H, NSAMP), "ones": (1, SEQ), "ofox": (NHP, P, SEQ),
                "bias": (NB * H, PAST), "ogla": (GH, P, 2, NT)}.items()}
    fox_gla_step(nc, ins, outs, scratch)
    r = run(nc, [feeds], core_ids=[0]).results[0]
    o = {n: r[f"out_{n}"] for n in _OUTS}
    return (o["y_p"], o["y_s"], o["k_p"], o["v_p"], o["logf_p"].reshape(1, 1, SEQ, H), o["gla_p"],
            o["k_s"], o["v_s"], o["logf_s"].reshape(1, NB, TS, H), o["gla_s"])
```
